# Optimizing a Trainium2 kernel written in Bass

```python
import jax, jax.numpy as jnp
from jax import lax
import numpy as np

D_MODEL = 1024
BATCH = 1
SEQ = 512
DEPTH = 2

GRID_W = 64
CTX_LEN = 256
HEAD_DIM = 128
N_Q_HEADS = D_MODEL // HEAD_DIM
N_KV_HEADS = 2
GROUP = N_Q_HEADS // N_KV_HEADS
ATTN_WIDTH = N_Q_HEADS * HEAD_DIM
KV_WIDTH = N_KV_HEADS * HEAD_DIM
POOL_WIDTH = D_MODEL // 2
POOL_WINDOWS = (2, 4, 8, 16)
N_POOL_GROUPS = 4
POOL_GROUP = POOL_WIDTH // N_POOL_GROUPS
N_IN = 2 * ATTN_WIDTH + 2 * KV_WIDTH + 2 * POOL_WIDTH + 2 * D_MODEL
Q_BLOCK = 128
ROPE_THETA = 10000.0
ROT_AXIS = HEAD_DIM // 2
N_FREQ = ROT_AXIS // 2
EPS = 1e-6
ALPHA = (2 * DEPTH) ** 0.25
BETA = (8 * DEPTH) ** -0.25

kernel_name = "hybrid_gqa_pool_parallel_deepnorm"

def rms_norm(x, g):
    xf = x.astype(jnp.float32)
    y = xf * lax.rsqrt(jnp.mean(xf * xf, axis=-1, keepdims=True) + EPS)
    return (y * g.astype(jnp.float32)).astype(x.dtype)

def layer_norm(x, g, b):
    xf = x.astype(jnp.float32)
    mu = jnp.mean(xf, axis=-1, keepdims=True)
    var = jnp.mean(jnp.square(xf - mu), axis=-1, keepdims=True)
    y = (xf - mu) * lax.rsqrt(var + EPS)
    return (y * g.astype(jnp.float32) + b.astype(jnp.float32)).astype(x.dtype)

def rope_tables(L):
    t = jnp.arange(L, dtype=jnp.int32)
    row = (t // GRID_W).astype(jnp.float32)
    col = (t % GRID_W).astype(jnp.float32)
    inv_freq = 1.0 / (ROPE_THETA ** (jnp.arange(N_FREQ, dtype=jnp.float32) / N_FREQ))
    ang = jnp.stack([row[:, None] * inv_freq[None, :], col[:, None] * inv_freq[None, :]], axis=1)
    return jnp.cos(ang), jnp.sin(ang)

def apply_rope(x, cos, sin):
    xf = x.astype(jnp.float32).reshape(x.shape[:-1] + (2, 2, N_FREQ))
    x1 = xf[..., 0, :]
    x2 = xf[..., 1, :]
    out = jnp.stack([x1 * cos - x2 * sin, x1 * sin + x2 * cos], axis=-2)
    return out.reshape(x.shape).astype(x.dtype)

def split_in(h):
    sizes = (ATTN_WIDTH, KV_WIDTH, KV_WIDTH, ATTN_WIDTH, POOL_WIDTH, POOL_WIDTH, D_MODEL, D_MODEL)
    outs = []
    o = 0
    for s in sizes:
        outs.append(h[..., o:o + s])
        o += s
    return outs

def heads(q, k, v, q_g, k_g):
    B, L = q.shape[0], q.shape[1]
    q = rms_norm(q.reshape(B, L, N_KV_HEADS, GROUP, HEAD_DIM), q_g).transpose(0, 2, 3, 1, 4)
    k = rms_norm(k.reshape(B, L, N_KV_HEADS, HEAD_DIM), k_g).transpose(0, 2, 1, 3)
    v = v.reshape(B, L, N_KV_HEADS, HEAD_DIM).transpose(0, 2, 1, 3)
    return q, k, v

def attend(q, k, v):
    s = jnp.einsum('bgrqd,bgkd->bgrqk', q * (HEAD_DIM ** -0.5), k).astype(jnp.float32)
    p = jax.nn.softmax(s, axis=-1).astype(v.dtype)
    return jnp.einsum('bgrqk,bgkd->bgrqd', p, v)

def latent_attention(q, k_all, v_all):
    B, G, R, L, hd = q.shape
    nb = L // Q_BLOCK
    qb = q.reshape(B, G, R, nb, Q_BLOCK, hd).transpose(3, 0, 1, 2, 4, 5)
    ob = lax.map(lambda qblk: attend(qblk, k_all, v_all), qb)
    return ob.transpose(1, 0, 4, 2, 3, 5).reshape(B, L, G * R * hd)

def context_attention(q, k, v):
    B, G, R, T, hd = q.shape
    return attend(q, k, v).transpose(0, 3, 1, 2, 4).reshape(B, T, G * R * hd)

def window_mean(x, w):
    B, L, C = x.shape
    a = w // 2
    b = w - a
    xf = x.astype(jnp.float32)
    xp = jnp.pad(xf, ((0, 0), (a, b), (0, 0)))
    cs = jnp.concatenate([jnp.zeros((B, 1, C), jnp.float32), jnp.cumsum(xp, axis=1)], axis=1)
    s = cs[:, w:w + L] - cs[:, :L]
    t = jnp.arange(L, dtype=jnp.int32)
    cnt = (jnp.minimum(t + b, L) - jnp.maximum(t - a, 0)).astype(jnp.float32)
    return (s / cnt[None, :, None]).astype(x.dtype)

def pool_mixer(xb, w_pool, pool_scale):
    B, L, _ = xb.shape
    parts = []
    for gi, w in enumerate(POOL_WINDOWS):
        xg = xb[..., gi * POOL_GROUP:(gi + 1) * POOL_GROUP]
        parts.append(window_mean(xg, w) - xg)
    m = jnp.stack(parts, axis=2)
    y = jnp.einsum('blgc,gcd->blgd', m, w_pool).reshape(B, L, POOL_WIDTH)
    return y * pool_scale

def merge(o_attn, z_attn, p_pool, z_pool, g_attn, g_pool, w_br_a, w_br_b, w_out):
    ya = (o_attn * jax.nn.silu(z_attn)) @ w_br_a
    yb = (p_pool * jax.nn.silu(z_pool)) @ w_br_b
    y = jax.nn.sigmoid(g_attn) * ya + jax.nn.sigmoid(g_pool) * yb
    return y @ w_out

def layer(x, cx, c, c_ctx, cos, sin, w_mod, b_mod, w_in, q_g, k_g, w_pool, pool_scale,
          w_br_a, w_br_b, w_out, ln_g, ln_b, update_ctx):
    mod = jax.nn.silu(c) @ w_mod + b_mod
    mod_c = jax.nn.silu(c_ctx) @ w_mod + b_mod
    shift, scale, gate = mod[:, None, :D_MODEL], mod[:, None, D_MODEL:2 * D_MODEL], mod[:, None, 2 * D_MODEL:]
    shift_c, scale_c, gate_c = mod_c[:D_MODEL], mod_c[D_MODEL:2 * D_MODEL], mod_c[2 * D_MODEL:]
    u = x * (1.0 + scale) + shift
    uc = cx * (1.0 + scale_c) + shift_c

    q, k, v, za, xb, zb, ga, gb = split_in(u @ w_in)
    qc_, kc_, vc_, zac, xbc, zbc, gac, gbc = split_in(uc @ w_in)

    q, k, v = heads(q, k, v, q_g, k_g)
    q = apply_rope(q, cos, sin)
    k = apply_rope(k, cos, sin)
    qc, kc, vc = heads(qc_, kc_, vc_, q_g, k_g)

    k_all = jnp.concatenate([kc, k], axis=2)
    v_all = jnp.concatenate([vc, v], axis=2)
    o_lat = latent_attention(q, k_all, v_all)
    p_lat = pool_mixer(xb, w_pool, pool_scale)
    y_lat = merge(o_lat, za, p_lat, zb, ga, gb, w_br_a, w_br_b, w_out)
    x_new = layer_norm(ALPHA * x + gate * y_lat, ln_g, ln_b)

    if update_ctx:
        o_ctx = context_attention(qc, kc, vc)
        p_ctx = pool_mixer(xbc, w_pool, pool_scale)
        y_ctx = merge(o_ctx, zac, p_ctx, zbc, gac, gbc, w_br_a, w_br_b, w_out)
        cx = layer_norm(ALPHA * cx + gate_c * y_ctx, ln_g, ln_b)
    return x_new, cx

def setup_inputs(seed: int = 0) -> dict:
    key = jax.random.key(seed)
    ks = jax.random.split(key, 18)
    f32 = jnp.float32
    n = lambda k, s: jax.random.normal(k, s, f32)
    w_in = n(ks[6], (DEPTH, D_MODEL, N_IN)) * D_MODEL ** -0.5
    v_lo = ATTN_WIDTH + KV_WIDTH
    w_in = w_in.at[:, :, v_lo:v_lo + KV_WIDTH].multiply(BETA)
    return {
        "x": n(ks[0], (BATCH, SEQ, D_MODEL)),
        "c": n(ks[1], (BATCH, D_MODEL)),
        "ctx": n(ks[2], (BATCH, CTX_LEN, D_MODEL)),
        "c_ctx": n(ks[3], (D_MODEL,)),
        "w_mod": n(ks[4], (DEPTH, D_MODEL, 3 * D_MODEL)) * 0.5 * D_MODEL ** -0.5,
        "b_mod": n(ks[5], (DEPTH, 3 * D_MODEL)) * 0.01,
        "w_in": w_in,
        "q_norm": 1.0 + 0.02 * n(ks[7], (DEPTH, HEAD_DIM)),
        "k_norm": 1.0 + 0.02 * n(ks[8], (DEPTH, HEAD_DIM)),
        "w_pool": n(ks[9], (DEPTH, N_POOL_GROUPS, POOL_GROUP, POOL_GROUP)) * POOL_GROUP ** -0.5,
        "pool_scale": 1.0 + 0.1 * n(ks[10], (DEPTH, POOL_WIDTH)),
        "w_br_a": n(ks[11], (DEPTH, ATTN_WIDTH, D_MODEL)) * BETA * ATTN_WIDTH ** -0.5,
        "w_br_b": n(ks[12], (DEPTH, POOL_WIDTH, D_MODEL)) * BETA * POOL_WIDTH ** -0.5,
        "w_out": n(ks[13], (DEPTH, D_MODEL, D_MODEL)) * BETA * D_MODEL ** -0.5,
        "ln_g": 1.0 + 0.02 * n(ks[14], (DEPTH, D_MODEL)),
        "ln_b": 0.02 * n(ks[15], (DEPTH, D_MODEL)),
    }

def reference(x, c, ctx, c_ctx, w_mod, b_mod, w_in, q_norm, k_norm, w_pool, pool_scale,
              w_br_a, w_br_b, w_out, ln_g, ln_b):
    L = x.shape[1]
    cos, sin = rope_tables(L)
    cos = cos.astype(x.dtype)
    sin = sin.astype(x.dtype)
    cx = ctx
    for l in range(DEPTH):
        x, cx = layer(x, cx, c, c_ctx, cos, sin, w_mod[l], b_mod[l], w_in[l], q_norm[l], k_norm[l],
                      w_pool[l], pool_scale[l], w_br_a[l], w_br_b[l], w_out[l], ln_g[l], ln_b[l],
                      update_ctx=(l < DEPTH - 1))
    return x


_drawn_inputs = setup_inputs


def setup_inputs(seed=0):
    import zlib

    import numpy as np

    out = dict(_drawn_inputs(seed))
    spreads = {}
    factors = {'ctx': 8.0,
     'c_ctx': 8.0,
     'b_mod': 8.0,
     'q_norm': 8.0,
     'k_norm': 8.0,
     'pool_scale': 8.0,
     'w_br_a': 8.0}
    for name, (base, spread) in spreads.items():
        noise = np.random.default_rng([zlib.crc32(name.encode()), seed]).standard_normal(out[name].shape)
        drawn = base * np.exp(spread * noise) if base else spread * noise
        out[name] = __import__('jax').numpy.asarray(drawn.astype(out[name].dtype))
    for name, factor in factors.items():
        out[name] = (out[name] * factor).astype(out[name].dtype)
    return out
```

```python
import numpy as np
from contextlib import ExitStack

import concourse.bass as bass
from concourse import mybir

F32 = mybir.dt.float32
F32R = mybir.dt.float32r
ALU = mybir.AluOpType
ACT = mybir.ActivationFunctionType
AX_X = mybir.AxisListType.X

P = 128
D = 1024
KD = D // P
DEPTH = 2
LAT, CTX = 512, 256
TOK = LAT + CTX
HEADS, KV_HEADS, GROUP = 8, 2, 4
POOL_GROUPS = 4
WINDOWS = (2, 4, 8, 16)
GRID_W = 64
EPS = 1e-6
ALPHA = float((2 * DEPTH) ** 0.25)
COL_ZA = 1536
PAD = 8

STREAMS = ((0, 0, 2, 2), (0, 2, 4, 6), (1, 2, 4, 6))
LAYER_STREAMS = ((0, 1), (2,))


def weight_chunks(w):
    out = []
    for l in range(DEPTH):
        for cg in range(6):
            for q in range(4):
                out.append(("mod", w["w_mod"][l, cg, q], 2, 512))
    for l in range(DEPTH):
        for cg in (2, 0, 1):
            for q in range(4):
                out.append(("qkv", w["w_qkv"][l, cg, q], 2, 512))
        for s in LAYER_STREAMS[l]:
            out.append(("pool", w["w_pool"][l], 4, P))
            for h in range(HEADS):
                out.append(("za", w["w_gates"][l, h], KD, P))
                out.append(("xz", w["w_gates"][l, (8, 12)[h % 2] + h // 2], KD, P))
            for j in range(KD):
                out.append(("ga", w["w_gates"][l, 16 + j], KD, P))
                out.append(("gb", w["w_gates"][l, 24 + j], KD, P))
                out.append(("ya", w["w_br_a"][l, j], KD, P))
                out.append(("yb", w["w_br_b"][l, j], 4, P))
            for k in range(KD):
                out.append(("out", w["w_out"][l, k * P:(k + 1) * P, :], 1, D))
    return out


def build(nc, t):
    chunks = weight_chunks(t)
    RAW_SLOTS = 3
    raw_slot, raw_before, split_no, ring_before = [], [], [], []
    last_in_raw, last_in_ring, splits, ring_no = {}, {}, [], 0
    for n, (kind, _, a, b) in enumerate(chunks):
        raw_slot.append(n % RAW_SLOTS)
        raw_before.append(last_in_raw.get(n % RAW_SLOTS))
        last_in_raw[n % RAW_SLOTS] = n
        if kind == "mod":
            split_no.append(None)
            ring_before.append(None)
            continue
        split_no.append(len(splits))
        place = "pool" if kind == "pool" else ring_no % 2
        ring_no += kind != "pool"
        ring_before.append(last_in_ring.get(place))
        last_in_ring[place] = n
        splits.append((n, place))
    first = {}
    for n, (kind, *_r) in enumerate(chunks):
        first.setdefault(kind, []).append(n)
    POOL_N = first["pool"]
    XZ_N, GA_N, OUT_N, QKV_N = first["xz"], first["ga"], first["out"], first["qkv"]
    for s in (1, 2):
        ring_before[POOL_N[s]] = GA_N[8 * s - 8]

    done_count, ring_chunks = [], 0
    for kind, *_r in chunks:
        ring_chunks += kind != "pool"
        done_count.append(ring_chunks)

    def done(n):
        return done_count[n]

    def p2_no(l, g, tile):
        if l == 0:
            return 6 * g + tile
        return 18 + (tile if g == 0 else 6 + 4 * (g - 1) + tile - 2)

    def p2_tiles(l, g):
        return list(range(6)) if l == 0 or g == 0 else list(range(2, 6))

    STEP0 = (0, 16, 48)

    def step_no(s, h, i):
        return STEP0[s] + h * STREAMS[s][2] + i

    def head_no(s, h):
        return 8 * s + h

    TILE0 = (0, 2, 6)

    def out_no(s, tile):
        return TILE0[s] + tile

    def acc_count(l, g, tile):
        n = 0
        for ll in range(DEPTH):
            for gg in range(3):
                for tt in p2_tiles(ll, gg)[:-1]:
                    n += 1
                    if (ll, gg, tt) == (l, g, tile):
                        return n
        raise ValueError

    def bc_count(s):
        return 64 + 16 * (5 * (s + 1) if s < 2 else 13)

    def ssq_count(l, g, tile):
        n = 0
        for ll in range(DEPTH):
            for gg in range(3):
                for tt in p2_tiles(ll, gg):
                    n += 2 if gg == 0 else 4
                    if (ll, gg, tt) == (l, g, tile):
                        return n
        raise ValueError

    with ExitStack() as ctx:
        def sb(name, n, dt=F32):
            return ctx.enter_context(nc.sbuf_tensor(name, [P, n], dt))

        def sem(name):
            return ctx.enter_context(nc.semaphore(name))

        arena = sb("arena", 41984, F32R)
        work = sb("work", 7168)
        raw = sb("raw", 3072)
        ident = sb("ident", P)
        stat = sb("stat", 320)

        def view(off, a, b):
            return arena[:, off:off + a * b].rearrange("p (a b) -> p a b", a=a)

        def pair(off, a, b):
            return view(off, a, b), view(off + a * b, a, b)

        U = (pair(0, KD, CTX), pair(4096, KD, LAT))
        Q = (pair(12288, HEADS, CTX), pair(16384, HEADS, LAT))
        K = pair(24576, KV_HEADS, TOK)
        V = pair(27648, 6, KV_HEADS * P)
        SCR = 30720
        PT = (pair(SCR, 2, CTX), pair(SCR, 6, LAT), pair(SCR, 6, LAT))
        Y = (pair(SCR, KD, CTX), pair(24576, KD, LAT), pair(24576, KD, LAT))
        M = (pair(SCR + 4096, POOL_GROUPS, CTX), pair(12288, POOL_GROUPS, LAT), pair(12288, POOL_GROUPS, LAT))
        W = (36864, 38912)
        WP = pair(40960, POOL_GROUPS, P)

        def u_tile(tile):
            if tile < 2:
                return tuple(x[:, :, tile * P:(tile + 1) * P] for x in U[0])
            return tuple(x[:, :, (tile - 2) * P:(tile - 1) * P] for x in U[1])

        def q_tile(tile, h0, n):
            if tile < 2:
                return tuple(x[:, h0:h0 + n, tile * P:(tile + 1) * P] for x in Q[0])
            return tuple(x[:, h0:h0 + n, (tile - 2) * P:(tile - 1) * P] for x in Q[1])

        def split_place(m):
            n, place = splits[m]
            size = chunks[n][2] * chunks[n][3]
            off = 40960 if place == "pool" else W[place]
            step = 512 if place == "pool" else 1024
            return arena[:, off:off + size], arena[:, off + step:off + step + size]

        def ring(n):
            hi, lo = split_place(split_no[n])
            a = chunks[n][2]
            return hi.rearrange("p (a b) -> p a b", a=a), lo.rearrange("p (a b) -> p a b", a=a)

        def raw_of(n):
            size = chunks[n][2] * chunks[n][3]
            return raw[:, raw_slot[n] * 1024:raw_slot[n] * 1024 + size]

        def wk(off, n):
            return work[:, off:off + n]

        RQ = stat[:, 0:48].rearrange("p (t h) -> p t h", t=6)
        RK = stat[:, 48:60].rearrange("p (t h) -> p t h", t=6)
        SSQ = stat[:, 64:88].rearrange("p (t h) -> p t h", t=6)
        RTMP = stat[:, 88:112].rearrange("p (t h) -> p t h", t=6)
        MHALF = stat[:, 112:116]
        NB = stat[:, 116:118]
        MX = stat[:, 118:120]
        RSUM = stat[:, 120:122]
        RINV = stat[:, 122:124]
        BN = stat[:, 124:136].rearrange("p (a b) -> p a b", a=2)
        MV = stat[:, 136:138]
        RSTD = stat[:, 138:139]
        SC = stat[:, 140:156].rearrange("p (v k) -> p v k", v=2)
        CRAW = stat[:, 156:172].rearrange("p (v k) -> p v k", v=2)
        CTH = stat[:, 172:188].rearrange("p (v k) -> p v k", v=2)
        PS = stat[:, 188:196].rearrange("p (l g) -> p l g", l=2)
        EDGE = stat[:, 196:260].rearrange("p (g e) -> p g e", g=4)
        VEPS = stat[:, 260:261]

        ps = ctx.enter_context(nc.psum_tensor("ps", [P, 8, 512], F32))

        MODROW, BROW = wk(0, 3072), wk(3072, 3072)
        BC = [wk(1024 * i, 1024) for i in range(5)]
        G_GATE, G_G, G_B, G_SC, G_SH = range(5)
        X0, X1 = wk(5120, 1024), wk(6144, 1024)
        TAB = wk(0, 2048).rearrange("p (t k f) -> p t k f", t=4, k=4)
        GN = wk(2048, 512).rearrange("p (k f) -> p k f", k=4)
        QRAW = wk(2560, 3072).rearrange("p (t f) -> p t f", t=6)
        CS = wk(2560, 1024).rearrange("p (t k f) -> p t k f", t=4, k=2)
        SQ = wk(6656, 512)
        T1, T2 = wk(5632, 512), wk(6144, 512)
        PR = [wk(768 * i, 768) for i in range(2)]
        THZ = wk(1536, 512)
        SZA = [wk(2048, 512), wk(2560, 512)]
        XP, XA, XB_ = wk(3072, 528), wk(3600, 528), wk(4128, 528)
        PM = wk(4656, 512)
        THB = wk(5168, 512)
        SZB = wk(5680, 512)
        OG = wk(6192, 512)
        THA_, THB_, YA_, YB_ = wk(5120, 512), wk(5632, 512), wk(6144, 512), wk(6656, 512)

        mod_rows = nc.dram_tensor("mod_rows", (DEPTH, 2, 3 * D), F32, kind="Internal").ap()
        x_mid = nc.dram_tensor("x_mid", (LAT, D), F32, kind="Internal").ap()

        landed = [sem(f"raw_landed{i}") for i in range(RAW_SLOTS)]
        w_hi, w_lo = sem("w_hi"), sem("w_lo")
        chunk_done = sem("chunk_done")
        consts = sem("consts")
        ident_ready = sem("ident_ready")
        silu_c = sem("silu_c")
        act_own, dve_own, pool_own = sem("act_own"), sem("dve_own"), sem("pool_own")
        brow_in = sem("brow_in")
        mod_evac = sem("mod_evac")
        mod_stored = sem("mod_stored")
        bc_in = sem("bc_in")
        x_in = [sem(f"x_in{i}") for i in range(3)]
        x_res = sem("x_res")
        u_made, u_turned, u_hi, u_lo = sem("u_made"), sem("u_turned"), sem("u_hi"), sem("u_lo")
        tab_in, tab_ready = sem("tab_in"), sem("tab_ready")
        acc_done = sem("acc_done")
        q_copied, ssq_done, rms_ready = sem("q_copied"), sem("ssq_done"), sem("rms_ready")
        v_split = sem("v_split")
        roped, q_turned, qk_hi, qk_lo = sem("roped"), sem("q_turned"), sem("qk_hi"), sem("qk_lo")
        s_done, nb_ready, exp_done, p_ready = sem("s_done"), sem("nb_ready"), sem("exp_done"), sem("p_ready")
        p_turned, pt_hi, pt_lo = sem("p_turned"), sem("pt_hi"), sem("pt_lo")
        pv_done, og_ready, o_hi, o_lo = sem("pv_done"), sem("og_ready"), sem("o_hi"), sem("o_lo")
        za_tanh, sza_ready = sem("za_tanh"), sem("sza_ready")
        xb_copied, pooled = sem("xb_copied"), sem("pooled")
        m_hi, m_lo, pool_mm = sem("m_hi"), sem("m_lo"), sem("pool_mm")
        zb_tanh, szb_ready = sem("zb_tanh"), sem("szb_ready")
        pg_ready, pg_hi, pg_lo = sem("pg_ready"), sem("pg_hi"), sem("pg_lo")
        ga_tanh, merged, y_hi, y_lo = sem("ga_tanh"), sem("merged"), sem("y_hi"), sem("y_lo")
        r_ready, xn_stored, xn_ready = sem("r_ready"), sem("xn_stored"), sem("xn_ready")
        xhat_ready = sem("xhat_ready")
        var_ready, rstd_ready = sem("var_ready"), sem("rstd_ready")
        block = ctx.enter_context(nc.Block())

        @block.sync
        def _(sp):
            for n, (kind, src, a, b) in enumerate(chunks):
                before = raw_before[n]
                if before is not None:
                    if chunks[before][0] == "mod":
                        sp.wait_ge(chunk_done, done(before))
                    else:
                        sp.wait_ge(w_lo, split_no[before] + 1)
                sp.dma_start(raw_of(n), src).then_inc(landed[raw_slot[n]], 16)

        def wait_landed(eng, n):
            eng.wait_ge(landed[raw_slot[n]], 16 * (n // RAW_SLOTS + 1))

        @block.scalar
        def _(act):
            own = [0]

            def split(m):
                if m >= len(splits):
                    return
                n = splits[m][0]
                wait_landed(act, n)
                if ring_before[n] is not None:
                    act.wait_ge(chunk_done, done(ring_before[n]))
                nc.scalar.activation(split_place(m)[0], raw_of(n), ACT.Copy).then_inc(w_hi, 1)

            act.wait_ge(consts, 16 * 3)
            nc.scalar.activation(CTH, CRAW, ACT.Tanh, scale=0.5).then_inc(silu_c, 1)

            def turn_u(no, tile, bank):
                act.wait_ge(u_turned, no + 1)
                nc.scalar.activation(u_tile(tile)[0], ps[:, bank:bank + 2, :].rearrange("p a (b c) -> p (a b) c", c=P),
                                     ACT.Copy).then_inc(u_hi, 1)

            m = 0
            for tile in range(6):
                turn_u(tile, tile, 2 * (tile % 3))
            split(0)
            for l in range(DEPTH):
                def copies(g, c):
                    for tile in p2_tiles(l, g):
                        no = p2_no(l, g, tile)
                        if tile == p2_tiles(l, g)[-1]:
                            act.wait_ge(chunk_done, done(QKV_N[12 * l + 4 * g + 3]))
                        else:
                            act.wait_ge(acc_done, acc_count(l, g, tile))
                        if g > 0:
                            act.wait_ge(q_turned, p2_no(l, g - 1, tile) + 1)
                        elif tile == 0:
                            act.wait_ge(tab_ready, 4 * (l + 1))
                        if g == 0:
                            nc.scalar.activation(QRAW[:, tile, 0:256], ps[:, tile, 0:256], ACT.Copy)
                            nc.scalar.activation(V[0][:, tile, :], ps[:, tile, 256:512], ACT.Copy).then_inc(q_copied, 1)
                        else:
                            nc.scalar.activation(QRAW[:, tile, :], ps[:, tile, :], ACT.Copy).then_inc(q_copied, 1)

                def squares(g, tiles):
                    n = 2 if g == 0 else 4
                    for tile in tiles:
                        no = p2_no(l, g, tile)
                        act.wait_ge(q_copied, no + 1)
                        if g or l:
                            act.wait_ge(rms_ready, (p2_no(l, g - 1, tile) if g else p2_no(l - 1, 2, tile)) + 1)
                        if own[0]:
                            act.wait_ge(ssq_done, own[0])
                        for h in range(n):
                            ins = nc.scalar.activation(SQ[:, h * P:(h + 1) * P], QRAW[:, tile, h * P:(h + 1) * P], ACT.Square,
                                                       accum_out=SSQ[:, tile, h:h + 1])
                            own[0] += 1
                            ins.then_inc(ssq_done, 1)

                def turned(g, tiles):
                    n = 2 if g == 0 else 4
                    for tile in tiles:
                        no = p2_no(l, g, tile)
                        act.wait_ge(q_turned, no + 1)
                        src = ps[:, 6 + no % 2, 0:n * P].rearrange("p (h c) -> p h c", h=n)
                        dst = K[0][:, :, tile * P:(tile + 1) * P] if g == 0 else q_tile(tile, 4 * (g - 1), 4)[0]
                        nc.scalar.activation(dst, src, ACT.Copy).then_inc(qk_hi, 1)

                for g in range(3):
                    for c in range(4):
                        split(m + 1)
                        m += 1
                        if g > 0:
                            tl = p2_tiles(l, g - 1)
                            if c < 3:
                                squares(g - 1, tl[2 * c:2 * c + 2])
                            if c > 0:
                                turned(g - 1, tl[2 * c - 2:2 * c])
                        if c == 3:
                            copies(g, c)
                tl = p2_tiles(l, 2)
                for c in range(3):
                    squares(2, tl[2 * c:2 * c + 2])
                for c in range(3):
                    turned(2, tl[2 * c:2 * c + 2])

                for s in LAYER_STREAMS[l]:
                    _, t0, nt, nk = STREAMS[s]
                    T, lat = nt * P, s > 0
                    split(m + 1)
                    m += 1

                    def probs_hi(h, i):
                        a = step_no(s, h, i)
                        act.wait_ge(p_turned, a + 1)
                        if h > 0 and i == 0:
                            act.wait_ge(pv_done, head_no(s, h))
                        src = ps[:, 2:4, :].rearrange("p a b -> p (a b)")[:, 0:nk * P].rearrange("p (k c) -> p k c", k=nk)
                        nc.scalar.activation(PT[s][0][:, :, i * P:(i + 1) * P], src, ACT.Copy).then_inc(pt_hi, 1)

                    def gate_tanh(h):
                        act.wait_ge(chunk_done, done(XZ_N[8 * s + h] - 1))
                        if h > 0 or s > 0:
                            act.wait_ge(sza_ready, head_no(s, h))
                        nc.scalar.activation(THZ[:, 0:T], ps[:, 4, 0:T], ACT.Tanh, scale=0.5).then_inc(za_tanh, 1)

                    def pool_out(h):
                        g = h // 2
                        act.wait_ge(chunk_done, done(XZ_N[8 * s + h]))
                        no = 4 * s + g
                        if h % 2 == 0:
                            if no:
                                act.wait_ge(m_lo, no)
                            nc.scalar.activation(XP[:, PAD:PAD + T], ps[:, 5, 0:T], ACT.Copy).then_inc(xb_copied, 1)
                        else:
                            if no:
                                act.wait_ge(szb_ready, no)
                            nc.scalar.activation(THB[:, 0:T], ps[:, 5, 0:T], ACT.Tanh, scale=0.5).then_inc(zb_tanh, 1)

                    def pooled_hi(g):
                        no = 4 * s + g
                        act.wait_ge(pooled, no + 1)
                        nc.scalar.activation(M[s][0][:, g, :], PM[:, 0:T], ACT.Copy).then_inc(m_hi, 1)

                    def pool_gated_hi(g):
                        no = 4 * s + g
                        act.wait_ge(pg_ready, no + 1)
                        nc.scalar.activation(M[s][0][:, g, :], PM[:, 0:T], ACT.Copy).then_inc(pg_hi, 1)

                    def attn_out(h):
                        act.wait_ge(og_ready, head_no(s, h) + 1)
                        nc.scalar.activation(Q[min(s, 1)][0][:, h, :], OG[:, 0:T], ACT.Copy).then_inc(o_hi, 1)

                    act.wait_ge(rms_ready, p2_no(l, 2, 5) + 1)
                    prev = None
                    for h in range(HEADS):
                        for i in range(nt):
                            a = step_no(s, h, i)
                            if i == 0 or i == nt // 2:
                                split(m + 1)
                                m += 1
                            act.wait_ge(nb_ready, a + 1)
                            if a >= 2:
                                act.wait_ge(p_turned, a - 1)
                            nc.scalar.activation(PR[a % 2][:, 0:nk * P],
                                                 ps[:, 0:2, :].rearrange("p a b -> p (a b)")[:, 0:nk * P], ACT.Exp,
                                                 bias=NB[:, a % 2:a % 2 + 1], scale=RQ[:, t0 + i, h:h + 1],
                                                 accum_out=RSUM[:, a % 2:a % 2 + 1]).then_inc(exp_done, 1)
                            if prev is not None:
                                probs_hi(*prev)
                            prev = (h, i)
                            if i == nt // 2:
                                gate_tanh(h)
                            if i == 0 and h > 0:
                                pool_out(h - 1)
                            if i == nt // 2 and h % 2 == 1:
                                pooled_hi(h // 2)
                            if i == nt // 2 and h % 2 == 0 and h > 0:
                                pool_gated_hi(h // 2 - 1)
                            if lat and i == 2 and h > 0:
                                attn_out(h - 1)
                            if not lat and i == 0 and h > 1:
                                attn_out(h - 2)
                    probs_hi(*prev)
                    pool_out(7)
                    pool_gated_hi(3)
                    if not lat:
                        attn_out(6)
                    attn_out(7)

                    for j in range(KD):
                        for g in range(4):
                            split(m + 1)
                            m += 1
                            n = GA_N[8 * s + j] + g
                            if g < 2:
                                act.wait_ge(chunk_done, done(n))
                                if j or s:
                                    act.wait_ge(merged, 8 * s + j)
                                if j == 0 and g == 0:
                                    act.wait_ge(pg_lo, 4 * s + 4)
                                    act.wait_ge(o_lo, 8 * s + 8)
                                nc.scalar.activation((THA_, THB_)[g][:, 0:T], ps[:, 4 * (j % 2) + g, 0:T],
                                                     ACT.Tanh, scale=0.5).then_inc(ga_tanh, 1)
                            if g == 2 and j > 0:
                                act.wait_ge(merged, 8 * s + j)
                                nc.scalar.activation(Y[s][0][:, j - 1, :], YA_[:, 0:T], ACT.Copy).then_inc(y_hi, 1)
                    act.wait_ge(merged, 8 * s + 8)
                    nc.scalar.activation(Y[s][0][:, 7, :], YA_[:, 0:T], ACT.Copy).then_inc(y_hi, 1)

                    for k in range(KD):
                        split(m + 1)
                        m += 1
                    if s < 2:
                        for tile in range(nt):
                            turn_u(6 + out_no(s, tile), t0 + tile, 2 * tile)


        @block.vector
        def _(dve):
            own = [0]

            def link(ins):
                own[0] += 1
                ins.then_inc(dve_own, 1)
                dve.wait_ge(dve_own, own[0])

            def split(m):
                if m >= len(splits):
                    return
                n = splits[m][0]
                hi, lo = split_place(m)
                dve.wait_ge(w_hi, m + 1)
                nc.vector.tensor_tensor(lo, raw_of(n), hi.bitcast(F32), ALU.subtract).then_inc(w_lo, 1)

            dve.wait_ge(silu_c, 1)
            link(nc.vector.scalar_tensor_tensor(out=CTH, in0=CTH, scalar=1.0, in1=CRAW, op0=ALU.add, op1=ALU.mult))
            nc.vector.tensor_scalar(SC, CTH, 0.5, None, ALU.mult).then_inc(silu_c, 1)
            dve.wait_ge(consts, 16 * 3)
            link(nc.vector.tensor_scalar(PS, PS, 0.5, None, ALU.mult))

            for l in range(DEPTH):
                dve.wait_ge(brow_in, 16 * (l + 1))
                if l:
                    dve.wait_ge(mod_stored, 16 * l)
                for cg in range(6):
                    n = 4 * (6 * l + cg) + 3
                    dve.wait_ge(chunk_done, done(n))
                    row, bias, acc = (x[0:2, cg * 512:(cg + 1) * 512] for x in (MODROW, BROW, MODROW))
                    acc = ps[0:2, cg % 2, :]
                    if cg < 2:
                        nc.vector.tensor_tensor(row, acc, bias, ALU.add).then_inc(mod_evac, 1)
                    elif cg < 4:
                        nc.vector.scalar_tensor_tensor(out=row, in0=acc, scalar=1.0, in1=bias, op0=ALU.add,
                                                       op1=ALU.add).then_inc(mod_evac, 1)
                    else:
                        link(nc.vector.tensor_tensor(row, acc, bias, ALU.add))
                        nc.vector.tensor_scalar(row, row, 0.5, None, ALU.mult).then_inc(mod_evac, 1)

            def turn_u(no, tile, bank):
                dve.wait_ge(u_hi, no + 1)
                hi, lo = u_tile(tile)
                nc.vector.tensor_tensor(lo, ps[:, bank:bank + 2, :].rearrange("p a (b c) -> p (a b) c", c=P),
                                        hi.bitcast(F32), ALU.subtract).then_inc(u_lo, 1)

            for tile in range(6):
                s = 0 if tile < 2 else 1
                x_t = wk(4096 + 1024 * (tile % 3), 1024)
                dve.wait_ge(bc_in, 64)
                dve.wait_ge(x_in[tile % 3], 16 * (tile // 3 + 1))
                link(nc.vector.tensor_tensor(x_t, x_t, BC[2 * s], ALU.mult))
                nc.vector.tensor_tensor(x_t, x_t, BC[2 * s + 1], ALU.add).then_inc(u_made, 1)
                if tile:
                    turn_u(tile - 1, tile - 1, 2 * ((tile - 1) % 3))
            turn_u(5, 5, 4)
            m = 0
            split(0)
            for l in range(DEPTH):
                dve.wait_ge(tab_in, 16 * 7 * (l + 1))
                for k in range(4):
                    nc.vector.tensor_tensor(TAB[:, :, k, :], CS[:, :, k % 2, :],
                                            GN[:, k:k + 1, :].to_broadcast([P, 4, P]), ALU.mult).then_inc(tab_ready, 1)

                def v_lo(tile):
                    dve.wait_ge(q_copied, p2_no(l, 0, tile) + 1)
                    nc.vector.tensor_tensor(V[1][:, tile, :], ps[:, tile, 256:512], V[0][:, tile, :].bitcast(F32),
                                            ALU.subtract).then_inc(v_split, 1)

                def rope(g, tiles):
                    n = 2 if g == 0 else 4
                    for tile in tiles:
                        no = p2_no(l, g, tile)
                        dve.wait_ge(q_copied, no + 1)
                        dve.wait_ge(tab_ready, 4 * (l + 1))
                        x = QRAW[:, tile, 0:n * P]
                        ki = 2 if g == 0 else 0
                        heads_ = x.rearrange("p (h f) -> p h f", h=n)
                        dve.wait_ge(ssq_done, ssq_count(l, g, tile))
                        if tile < 2:
                            out = heads_
                            last = nc.vector.tensor_tensor(out, heads_, GN[:, ki:ki + 1, :].to_broadcast([P, n, P]),
                                                           ALU.mult)
                        else:
                            a, b = T1[:, 0:n * P], T2[:, 0:n * P]
                            dve.wait_ge(roped, no)
                            ca = TAB[:, tile - 2, ki:ki + 1, :].to_broadcast([P, n, P])
                            sn = TAB[:, tile - 2, ki + 1, :].rearrange("p (a z f) -> p a z f", z=2, f=32)
                            nc.vector.tensor_tensor(a.rearrange("p (h f) -> p h f", h=n), heads_, ca,
                                                    ALU.mult).then_inc(dve_own, 1)
                            for z in range(2):
                                nc.vector.tensor_tensor(
                                    b.rearrange("p (h a z f) -> p h a z f", a=2, z=2, f=32)[:, :, :, z, :],
                                    x.rearrange("p (h a z f) -> p h a z f", a=2, z=2, f=32)[:, :, :, 1 - z, :],
                                    sn[:, :, z, :].unsqueeze(1).to_broadcast([P, n, 2, 32]), ALU.mult).then_inc(dve_own, 1)
                            own[0] += 3
                            dve.wait_ge(dve_own, own[0])
                            last = nc.vector.tensor_tensor(x, a, b, ALU.add)
                        if g == 0:
                            link(last)
                            dve.wait_ge(rms_ready, no + 1)
                            last = nc.vector.tensor_tensor(
                                heads_, heads_, RK[:, tile, :].unsqueeze(2).to_broadcast([P, 2, P]), ALU.mult)
                        last.then_inc(roped, 1)

                def turned(g, tiles):
                    n = 2 if g == 0 else 4
                    for tile in tiles:
                        no = p2_no(l, g, tile)
                        dve.wait_ge(qk_hi, no + 1)
                        src = ps[:, 6 + no % 2, 0:n * P].rearrange("p (h c) -> p h c", h=n)
                        hi, lo = ((x[:, :, tile * P:(tile + 1) * P] for x in K) if g == 0
                                  else q_tile(tile, 4 * (g - 1), 4))
                        nc.vector.tensor_tensor(lo, src, hi.bitcast(F32), ALU.subtract).then_inc(qk_lo, 1)

                for g in range(3):
                    for c in range(4):
                        split(m + 1)
                        m += 1
                        if g > 0:
                            tl = p2_tiles(l, g - 1)
                            if c < 3:
                                rope(g - 1, tl[2 * c:2 * c + 2])
                            if c > 0:
                                turned(g - 1, tl[2 * c - 2:2 * c])
                        if c == 3 and g == 0:
                            for tile in range(6):
                                v_lo(tile)
                tl = p2_tiles(l, 2)
                for c in range(3):
                    rope(2, tl[2 * c:2 * c + 2])
                for c in range(3):
                    turned(2, tl[2 * c:2 * c + 2])

                for s in LAYER_STREAMS[l]:
                    _, t0, nt, nk = STREAMS[s]
                    T, lat = nt * P, s > 0
                    split(m + 1)
                    m += 1
                    dve.wait_ge(rms_ready, p2_no(l, 2, 5) + 1)
                    for buf in (XP, XA, XB_):
                        link(nc.vector.memset(buf[:, 0:528], 0.0))
                    zeroed = own[0]

                    def softmax_max(h, i):
                        a = step_no(s, h, i)
                        dve.wait_ge(s_done, a + 1)
                        link(nc.vector.reduce_max(MX[:, a % 2:a % 2 + 1],
                                                  ps[:, 0:2, :].rearrange("p a b -> p (a b)")[:, 0:nk * P], AX_X))
                        nc.vector.tensor_scalar(NB[:, a % 2:a % 2 + 1], MX[:, a % 2:a % 2 + 1],
                                                RQ[:, t0 + i, h:h + 1], -1.0, ALU.mult, ALU.mult).then_inc(nb_ready, 1)

                    def softmax_norm(h, i):
                        a = step_no(s, h, i)
                        dve.wait_ge(exp_done, a + 1)
                        link(nc.vector.reciprocal(RINV[:, a % 2:a % 2 + 1], RSUM[:, a % 2:a % 2 + 1]))
                        nc.vector.tensor_scalar(PR[a % 2][:, 0:nk * P], PR[a % 2][:, 0:nk * P],
                                                RINV[:, a % 2:a % 2 + 1], 0.5, ALU.mult, ALU.mult).then_inc(p_ready, 1)

                    def probs_lo(h, i):
                        a = step_no(s, h, i)
                        dve.wait_ge(pt_hi, a + 1)
                        src = ps[:, 2:4, :].rearrange("p a b -> p (a b)")[:, 0:nk * P].rearrange("p (k c) -> p k c", k=nk)
                        hi, lo = (x[:, :, i * P:(i + 1) * P] for x in PT[s])
                        nc.vector.tensor_tensor(lo, src, hi.bitcast(F32), ALU.subtract).then_inc(pt_lo, 1)

                    def gate_silu(h):
                        b = head_no(s, h)
                        dve.wait_ge(za_tanh, b + 1)
                        if b >= 2:
                            dve.wait_ge(og_ready, b - 1)
                        nc.vector.scalar_tensor_tensor(out=SZA[b % 2][:, 0:T], in0=THZ[:, 0:T], scalar=1.0,
                                                       in1=ps[:, 4, 0:T], op0=ALU.add, op1=ALU.mult).then_inc(sza_ready, 1)

                    def attn_out(h):
                        b = head_no(s, h)
                        dve.wait_ge(pv_done, b + 1)
                        dve.wait_ge(sza_ready, b + 1)
                        if b:
                            dve.wait_ge(o_lo, b)
                        nc.vector.tensor_tensor(OG[:, 0:T], ps[:, 6, 0:T], SZA[b % 2][:, 0:T],
                                                ALU.mult).then_inc(og_ready, 1)

                    def attn_out_lo(h):
                        b = head_no(s, h)
                        hi, lo = (x[:, h, :] for x in Q[min(s, 1)])
                        dve.wait_ge(o_hi, b + 1)
                        dve.wait_ge(og_ready, b + 1)
                        nc.vector.tensor_tensor(lo, OG[:, 0:T], hi.bitcast(F32), ALU.subtract).then_inc(o_lo, 1)

                    def window_means(g):
                        no = 4 * s + g
                        dve.wait_ge(xb_copied, no + 1)
                        src, w = XP, 1
                        bufs = [XA, XB_]
                        for d in range(g + 1):
                            dst = bufs[d % 2]
                            lo_ = PAD - PAD + (1 if w == 1 else w // 2)
                            n = 528 - 16
                            if w == 1:
                                link(nc.vector.tensor_tensor(dst[:, 1:T + 2 * PAD], src[:, 0:T + 2 * PAD - 1],
                                                             src[:, 1:T + 2 * PAD], ALU.add))
                            else:
                                k = w // 2
                                link(nc.vector.tensor_tensor(dst[:, k:T + 2 * PAD - k], src[:, 0:T + 2 * PAD - 2 * k],
                                                             src[:, 2 * k:T + 2 * PAD], ALU.add))
                            src, w = dst, 2 * w
                        if no:
                            dve.wait_ge(pg_lo, no)
                        link(nc.vector.tensor_tensor(src[:, PAD:PAD + 8], src[:, PAD:PAD + 8], EDGE[:, g, 0:8], ALU.mult))
                        link(nc.vector.tensor_tensor(src[:, PAD + T - 8:PAD + T], src[:, PAD + T - 8:PAD + T],
                                                     EDGE[:, g, 8:16], ALU.mult))
                        nc.vector.scalar_tensor_tensor(out=PM[:, 0:T], in0=src[:, PAD:PAD + T], scalar=1.0 / w,
                                                       in1=XP[:, PAD:PAD + T], op0=ALU.mult,
                                                       op1=ALU.subtract).then_inc(pooled, 1)

                    def pooled_lo(g):
                        no = 4 * s + g
                        dve.wait_ge(m_hi, no + 1)
                        dve.wait_ge(pooled, no + 1)
                        nc.vector.tensor_tensor(M[s][1][:, g, :], PM[:, 0:T], M[s][0][:, g, :].bitcast(F32),
                                                ALU.subtract).then_inc(m_lo, 1)

                    def pool_silu(g):
                        no = 4 * s + g
                        dve.wait_ge(zb_tanh, no + 1)
                        if no:
                            dve.wait_ge(pg_ready, no)
                        nc.vector.scalar_tensor_tensor(out=SZB[:, 0:T], in0=THB[:, 0:T], scalar=1.0,
                                                       in1=ps[:, 5, 0:T], op0=ALU.add, op1=ALU.mult).then_inc(szb_ready, 1)

                    def pool_gated(g):
                        no = 4 * s + g
                        dve.wait_ge(pool_mm, no + 1)
                        dve.wait_ge(szb_ready, no + 1)
                        nc.vector.scalar_tensor_tensor(out=PM[:, 0:T], in0=ps[:, 7, 0:T], scalar=PS[:, l, g:g + 1],
                                                       in1=SZB[:, 0:T], op0=ALU.mult, op1=ALU.mult).then_inc(pg_ready, 1)

                    def pool_gated_lo(g):
                        no = 4 * s + g
                        dve.wait_ge(pg_hi, no + 1)
                        dve.wait_ge(pg_ready, no + 1)
                        nc.vector.tensor_tensor(M[s][1][:, g, :], PM[:, 0:T], M[s][0][:, g, :].bitcast(F32),
                                                ALU.subtract).then_inc(pg_lo, 1)

                    prev = None
                    for h in range(HEADS):
                        for i in range(nt):
                            softmax_max(h, i)
                            if i == 0 or i == nt // 2:
                                split(m + 1)
                                m += 1
                            softmax_norm(h, i)
                            if prev is not None:
                                probs_lo(*prev)
                            prev = (h, i)
                            if i == nt // 2:
                                gate_silu(h)
                            if i == 0 and h > 0:
                                if h % 2 == 1:
                                    window_means(h // 2)
                                else:
                                    pool_silu(h // 2 - 1)
                                    pool_gated(h // 2 - 1)
                            if i == nt - 1 and h > 0:
                                if h % 2 == 1:
                                    pooled_lo(h // 2)
                                else:
                                    pool_gated_lo(h // 2 - 1)
                            if lat and i == 2 and h > 0:
                                attn_out(h - 1)
                            if not lat and i == 0 and h > 1:
                                attn_out(h - 2)
                            if lat and i == 3 and h > 0:
                                attn_out_lo(h - 1)
                            if not lat and i == 1 and h > 1:
                                attn_out_lo(h - 2)
                    probs_lo(*prev)
                    pool_silu(3)
                    pool_gated(3)
                    pool_gated_lo(3)
                    for h in (6, 7) if not lat else (7,):
                        attn_out(h)
                        attn_out_lo(h)

                    for j in range(KD):
                        for g in range(4):
                            split(m + 1)
                            m += 1
                            n = GA_N[8 * s + j] + g
                            no = 8 * s + j
                            if g == 2 and j > 0:
                                dve.wait_ge(y_hi, no)
                                nc.vector.tensor_tensor(Y[s][1][:, j - 1, :], YA_[:, 0:T],
                                                        Y[s][0][:, j - 1, :].bitcast(F32), ALU.subtract).then_inc(y_lo, 1)
                        dve.wait_ge(chunk_done, done(n))
                        dve.wait_ge(ga_tanh, 2 * no + 2)
                        if no:
                            dve.wait_ge(y_lo, no)
                        b0 = 4 * (j % 2)
                        link(nc.vector.scalar_tensor_tensor(out=YA_[:, 0:T], in0=THA_[:, 0:T], scalar=1.0,
                                                            in1=ps[:, b0 + 2, 0:T], op0=ALU.add, op1=ALU.mult))
                        link(nc.vector.scalar_tensor_tensor(out=YB_[:, 0:T], in0=THB_[:, 0:T], scalar=1.0,
                                                            in1=ps[:, b0 + 3, 0:T], op0=ALU.add, op1=ALU.mult))
                        nc.vector.tensor_tensor(YA_[:, 0:T], YA_[:, 0:T], YB_[:, 0:T], ALU.add).then_inc(merged, 1)
                    dve.wait_ge(y_hi, 8 * s + 8)
                    nc.vector.tensor_tensor(Y[s][1][:, 7, :], YA_[:, 0:T], Y[s][0][:, 7, :].bitcast(F32),
                                            ALU.subtract).then_inc(y_lo, 1)

                    for k in range(KD):
                        split(m + 1)
                        m += 1
                    last_layer = s == 2
                    for tile in range(nt):
                        no = out_no(s, tile)
                        dve.wait_ge(chunk_done, done(OUT_N[8 * s + 7]))
                        dve.wait_ge(bc_in, bc_count(s))
                        dve.wait_ge(x_res, 16 * (no + 1))
                        if no > 2:
                            dve.wait_ge(xn_stored, 16 * (no - 2))
                        acc = ps[:, 2 * tile:2 * tile + 2, :].rearrange("p a b -> p (a b)")
                        link(nc.vector.tensor_tensor(X1, acc, BC[G_GATE], ALU.mult))
                        link(nc.vector.scalar_tensor_tensor(out=X0, in0=X0, scalar=ALPHA, in1=X1, op0=ALU.mult,
                                                            op1=ALU.add))
                        for hf in range(2):
                            link(nc.vector.bn_stats(BN[:, hf, :], X0[:, hf * 512:(hf + 1) * 512]))
                        nc.vector.bn_aggr(MV, BN.rearrange("p a b -> p (a b)")).then_inc(var_ready, 1)
                        dve.wait_ge(rstd_ready, no + 1)
                        link(nc.vector.tensor_scalar(X0, X0, MV[:, 0:1], RSTD, ALU.subtract, ALU.mult))
                        link(nc.vector.tensor_tensor(X0, X0, BC[G_G], ALU.mult))
                        nc.vector.tensor_tensor(X1, X0, BC[G_B], ALU.add).then_inc(xn_ready, 1)
                        if not last_layer:
                            dve.wait_ge(xn_ready, no + 1)
                            link(nc.vector.tensor_tensor(X0, X1, BC[G_SC], ALU.mult))
                            nc.vector.tensor_tensor(X0, X0, BC[G_SH], ALU.add).then_inc(u_made, 1)
                            turn_u(6 + no, t0 + tile, 2 * tile)



        @block.gpsimd
        def _(pool):
            own = [0]

            def link(ins):
                own[0] += 1
                ins.then_inc(pool_own, 1)
                pool.wait_ge(pool_own, own[0])

            pool.dma_start(CRAW.rearrange("p v k -> p (v k)"), t["c_cols"]).then_inc(consts, 16)
            pool.dma_start(PS.rearrange("p l g -> p (l g)"), t["pool_scale"]).then_inc(consts, 16)
            pool.dma_start(EDGE.rearrange("p g e -> p (g e)"), t["edge"].partition_broadcast(P)).then_inc(consts, 16)
            link(nc.gpsimd.memset(ident[:], 0.0))
            nc.gpsimd.affine_select(out=ident[:], in_=ident[:], compare_op=ALU.not_equal, fill=1.0, base=0,
                                    pattern=[[-1, P]], channel_multiplier=1).then_inc(ident_ready, 1)
            link(nc.gpsimd.memset(MHALF, -0.5))
            for l in range(DEPTH):
                if l:
                    pool.wait_ge(mod_evac, 6)
                for v in range(2):
                    pass
                pool.dma_start(BROW[0:2, :], t["b_mod"][l].partition_broadcast(2)).then_inc(brow_in, 16)
                pool.wait_ge(mod_evac, 6 * (l + 1))
                pool.dma_start(mod_rows[l], MODROW[0:2, :]).then_inc(mod_stored, 16)
            pool.wait_ge(mod_stored, 32)

            def row(l, s, part):
                return mod_rows[l, min(s, 1), part * D:(part + 1) * D].partition_broadcast(P)

            for s in range(2):
                pool.dma_start(BC[2 * s], row(0, s, 1)).then_inc(bc_in, 16)
                pool.dma_start(BC[2 * s + 1], row(0, s, 0)).then_inc(bc_in, 16)

            def x_rows(tile):
                return t["ctx"][tile * P:(tile + 1) * P, :] if tile < 2 else t["x"][(tile - 2) * P:(tile - 1) * P, :]

            for tile in range(6):
                if tile >= 3:
                    pool.wait_ge(u_turned, tile - 2)
                pool.dma_start(wk(4096 + 1024 * (tile % 3), 1024), x_rows(tile)).then_inc(x_in[tile % 3], 16)

            for l in range(DEPTH):
                pool.wait_ge(u_lo, (6, 12)[l])
                if l:
                    pool.wait_ge(xn_stored, 16 * 4)
                pool.dma_start(CS.rearrange("p t k f -> p t (k f)"), t["rope"].rearrange("(t p) f -> p t f", p=P)).then_inc(tab_in, 16)
                for k, g in enumerate((t["q_norm"], t["k_norm"])):
                    pool.dma_start(GN[:, 2 * k, :], g[l].partition_broadcast(P)).then_inc(tab_in, 16)
                    gh = g[l].rearrange("(a z f) -> a z f", z=2, f=32)
                    dst = GN[:, 2 * k + 1, :].rearrange("p (a z f) -> p a z f", z=2, f=32)
                    for z in range(2):
                        pool.dma_start(dst[:, :, z, :], gh[:, 1 - z, :].partition_broadcast(P)).then_inc(tab_in, 16)

                for g in range(3):
                    n = 2 if g == 0 else 4
                    for tile in p2_tiles(l, g):
                        no = p2_no(l, g, tile)
                        pool.wait_ge(ssq_done, ssq_count(l, g, tile))
                        v = RTMP[:, tile, 0:n]
                        link(nc.gpsimd.tensor_scalar(v, SSQ[:, tile, 0:n], 1.0 / P, EPS, ALU.mult, ALU.add))
                        if g == 0:
                            nc.gpsimd.tensor_tensor(RK[:, tile, :], v, MHALF[:, 0:n], ALU.pow).then_inc(rms_ready, 1)
                        else:
                            link(nc.gpsimd.tensor_tensor(v, v, MHALF[:, 0:n], ALU.pow))
                            nc.gpsimd.tensor_scalar(RQ[:, tile, 4 * (g - 1):4 * g], v, float(P) ** -0.5, 0.0,
                                                    ALU.mult, ALU.add).then_inc(rms_ready, 1)

                for s in LAYER_STREAMS[l]:
                    _, t0, nt, _ = STREAMS[s]
                    last_layer = s == 2
                    pool.wait_ge(o_lo, 8 * s + 8)
                    pool.wait_ge(pg_lo, 4 * s + 4)
                    pool.dma_start(BC[G_GATE], row(l, s, 2)).then_inc(bc_in, 16)
                    pool.dma_start(BC[G_G], t["ln_g"][l].partition_broadcast(P)).then_inc(bc_in, 16)
                    pool.dma_start(BC[G_B], t["ln_b"][l].partition_broadcast(P)).then_inc(bc_in, 16)
                    if not last_layer:
                        pool.dma_start(BC[G_SC], row(l + 1, s, 1)).then_inc(bc_in, 16)
                        pool.dma_start(BC[G_SH], row(l + 1, s, 0)).then_inc(bc_in, 16)
                    pool.wait_ge(y_lo, 8 * s + 8)
                    for tile in range(nt):
                        no = out_no(s, tile)
                        if tile:
                            pool.wait_ge(*((xn_ready, no) if last_layer else (u_turned, 6 + no)))
                        src = x_rows(t0 + tile) if l == 0 else x_mid[tile * P:(tile + 1) * P, :]
                        pool.dma_start(X0, src).then_inc(x_res, 16)
                        pool.wait_ge(var_ready, no + 1)
                        link(nc.gpsimd.tensor_scalar(VEPS, MV[:, 1:2], 1.0, EPS, ALU.mult, ALU.add))
                        nc.gpsimd.tensor_tensor(RSTD, VEPS, MHALF[:, 0:1], ALU.pow).then_inc(rstd_ready, 1)
                        if s:
                            pool.wait_ge(xn_ready, no + 1)
                            dst = x_mid if s == 1 else t["out"]
                            pool.dma_start(dst[tile * P:(tile + 1) * P, :], X1).then_inc(xn_stored, 16)
            pool.wait_ge(xn_stored, 16 * 8)

        @block.tensor
        def _(pe):
            def product(out, st, mv, start, stop):
                nc.tensor.matmul(out, st[1], mv[0], start=start, stop=False)
                nc.tensor.matmul(out, st[0], mv[1], start=False, stop=False)
                return nc.tensor.matmul(out, st[0], mv[0], start=False, stop=stop)

            n = 0
            pe.wait_ge(silu_c, 2)
            for l in range(DEPTH):
                for cg in range(6):
                    no = 6 * l + cg
                    if no >= 2:
                        pe.wait_ge(mod_evac, no - 1)
                    for q in range(4):
                        wait_landed(pe, n)
                        w = raw_of(n).rearrange("p (a b) -> p a b", a=2)
                        for kk in range(2):
                            k = 2 * q + kk
                            ins = nc.tensor.matmul(ps[0:2, cg % 2, :], SC[:, :, k], w[:, kk, :],
                                                   start=(k == 0), stop=(k == KD - 1))
                        ins.then_inc(chunk_done, 1)
                        n += 1

            def turn_u(no, src, bank):
                pe.wait_ge(u_made, no + 1)
                for k in range(KD):
                    ins = nc.tensor.transpose(ps[:, bank + k // 4, (k % 4) * P:(k % 4 + 1) * P],
                                              src[:, k * P:(k + 1) * P], ident[:])
                ins.then_inc(u_turned, 1)

            pe.wait_ge(ident_ready, 1)
            pe.wait_ge(mod_evac, 12)
            for tile in range(6):
                if tile >= 3:
                    pe.wait_ge(u_lo, tile - 2)
                turn_u(tile, wk(4096 + 1024 * (tile % 3), 1024), 2 * (tile % 3))

            for l in range(DEPTH):
                pe.wait_ge(u_lo, (6, 12)[l])

                def turn_q(g, tiles):
                    nh = 2 if g == 0 else 4
                    for tile in tiles:
                        no = p2_no(l, g, tile)
                        pe.wait_ge(roped, no + 1)
                        if no >= 2:
                            pe.wait_ge(qk_lo, no - 1)
                        for h in range(nh):
                            ins = nc.tensor.transpose(ps[:, 6 + no % 2, h * P:(h + 1) * P],
                                                      QRAW[:, tile, h * P:(h + 1) * P], ident[:])
                        ins.then_inc(q_turned, 1)

                for g in range(3):
                    tl = p2_tiles(l, g)
                    for c in range(4):
                        if g > 0 and c > 0:
                            turn_q(g - 1, p2_tiles(l, g - 1)[2 * c - 2:2 * c])
                        pe.wait_ge(w_lo, split_no[n] + 1)
                        wh, wl = ring(n)
                        for tile in tl:
                            if c == 0 and g > 0:
                                pe.wait_ge(q_copied, p2_no(l, g - 1, tile) + 1)
                                if g == 1:
                                    pe.wait_ge(v_split, 6 * l + tile + 1)
                            for kk in range(2):
                                k = 2 * c + kk
                                uh, ul = u_tile(tile)
                                ins = product(ps[:, tile, :], (uh[:, k, :], ul[:, k, :]), (wh[:, kk, :], wl[:, kk, :]),
                                              k == 0, k == KD - 1)
                            if tile == tl[-1]:
                                ins.then_inc(chunk_done, 1)
                            elif c == 3:
                                ins.then_inc(acc_done, 1)
                        n += 1
                turn_q(2, p2_tiles(l, 2))

                for s in LAYER_STREAMS[l]:
                    _, t0, nt, nk = STREAMS[s]
                    T, lat = nt * P, s > 0
                    si = min(s, 1)
                    pe.wait_ge(qk_lo, p2_no(l, 2, 5) + 1)
                    pe.wait_ge(w_lo, split_no[n] + 1)
                    if s == 1:
                        pe.wait_ge(u_lo, 8)
                    n += 1
                    s_view = ps[:, 0:2, :].rearrange("p a b -> p (a b)")

                    def scores(h, i):
                        a = step_no(s, h, i)
                        if a:
                            pe.wait_ge(exp_done, a)
                        qh, ql = (x[:, 0, :] for x in q_tile(t0 + i, h, 1))
                        kh, kl = (x[:, h // GROUP, :] for x in K)
                        for c0 in range(0, nk * P, 512):
                            c1 = min(c0 + 512, nk * P)
                            ins = product(s_view[:, c0:c1], (qh, ql), (kh[:, c0:c1], kl[:, c0:c1]), True, True)
                        ins.then_inc(s_done, 1)

                    def turn_p(h, i):
                        a = step_no(s, h, i)
                        pe.wait_ge(p_ready, a + 1)
                        if a:
                            pe.wait_ge(pt_lo, a)
                        for k in range(nk):
                            ins = nc.tensor.transpose(ps[:, 2 + k // 4, (k % 4) * P:(k % 4 + 1) * P],
                                                      PR[a % 2][:, k * P:(k + 1) * P], ident[:])
                        ins.then_inc(p_turned, 1)

                    def values(h):
                        b = head_no(s, h)
                        if b:
                            pe.wait_ge(og_ready, b)
                        pe.wait_ge(pt_lo, step_no(s, h, nt - 1) + 1)
                        c0 = (h // GROUP) * P
                        for k in range(nk):
                            ins = product(ps[:, 6, 0:T], (V[0][:, k, c0:c0 + P], V[1][:, k, c0:c0 + P]),
                                          (PT[s][0][:, k, :], PT[s][1][:, k, :]), k == 0, k == nk - 1)
                        ins.then_inc(pv_done, 1)

                    def project(bank, n, ks, start, stop):
                        wh, wl = ring(n)
                        for k in ks:
                            ins = product(ps[:, bank, 0:T], (wh[:, k, :], wl[:, k, :]),
                                          (U[si][0][:, k, :], U[si][1][:, k, :]), start and k == ks[0], stop and k == ks[-1])
                        return ins

                    def pool_product(g):
                        no = 4 * s + g
                        pe.wait_ge(m_lo, no + 1)
                        if no:
                            pe.wait_ge(pg_ready, no)
                        product(ps[:, 7, 0:T], (WP[0][:, g, :], WP[1][:, g, :]), (M[s][0][:, g, :], M[s][1][:, g, :]),
                                True, True).then_inc(pool_mm, 1)

                    prev = None
                    half = nt // 2
                    ks_of = [list(range(KD))] if half == 1 else [[0, 1, 2, 3], [4, 5, 6, 7]]
                    for h in range(HEADS):
                        for i in range(nt):
                            scores(h, i)
                            if prev is not None:
                                turn_p(*prev)
                            prev = (h, i)
                            part = i % half
                            bank = 4 + i // half
                            if part == 0:
                                pe.wait_ge(w_lo, split_no[n] + 1)
                                b = head_no(s, h)
                                if bank == 4 and b:
                                    pe.wait_ge(sza_ready, b)
                                if bank == 5 and b:
                                    if h % 2:
                                        pe.wait_ge(xb_copied, 4 * s + h // 2 + 1)
                                    else:
                                        pe.wait_ge(szb_ready, 4 * s + h // 2)
                            ins = project(bank, n, ks_of[part], part == 0, part == half - 1)
                            if part == half - 1:
                                ins.then_inc(chunk_done, 1)
                                n += 1
                            if i == 1 and h > 0:
                                values(h - 1)
                            if lat and i == 3 and h % 2 == 1 or not lat and i == 0 and h % 2 == 0 and h > 0:
                                pool_product((h - 1) // 2)
                    turn_p(*prev)
                    if not lat:
                        pool_product(3)
                    values(7)

                    for j in range(KD):
                        no = 8 * s + j
                        for g in range(4):
                            bank = 4 * (j % 2) + g
                            pe.wait_ge(w_lo, split_no[n] + 1)
                            if g == 0:
                                if j >= 2:
                                    pe.wait_ge(merged, no - 1)
                                elif j == 0:
                                    pe.wait_ge(pt_lo, step_no(s, 7, nt - 1) + 1)
                                    pe.wait_ge(exp_done, step_no(s, 7, nt - 1) + 1)
                                elif j == 1:
                                    pe.wait_ge(pg_ready, 4 * s + 4)
                                    pe.wait_ge(og_ready, 8 * s + 8)
                            if g == 2 and j == 0:
                                pe.wait_ge(o_lo, 8 * s + 8)
                            if g == 3 and j == 0:
                                pe.wait_ge(pg_lo, 4 * s + 4)
                            if g < 2:
                                ins = project(bank, n, list(range(KD)), True, True)
                            else:
                                op = Q[si] if g == 2 else M[s]
                                nkk = KD if g == 2 else POOL_GROUPS
                                wh, wl = ring(n)
                                for k in range(nkk):
                                    ins = product(ps[:, bank, 0:T], (wh[:, k, :], wl[:, k, :]),
                                                  (op[0][:, k, :], op[1][:, k, :]), k == 0, k == nkk - 1)
                            ins.then_inc(chunk_done, 1)
                            n += 1

                    for k in range(KD):
                        pe.wait_ge(w_lo, split_no[n] + 1)
                        pe.wait_ge(y_lo, 8 * s + k + 1)
                        if k == 0:
                            pe.wait_ge(merged, 8 * s + 8)
                        wh, wl = ring(n)
                        for tile in range(nt):
                            for hf in range(2):
                                st = tuple(x[:, k, tile * P:(tile + 1) * P] for x in Y[s])
                                mv = tuple(x[:, 0, hf * 512:(hf + 1) * 512] for x in (wh, wl))
                                ins = product(ps[:, 2 * tile + hf, :], st, mv, k == 0, k == KD - 1)
                        ins.then_inc(chunk_done, 1)
                        n += 1
                    if s < 2:
                        for tile in range(nt):
                            turn_u(6 + out_no(s, tile), X0, 2 * tile)


def chunked(w, rows, cols):
    n, r, c = w.shape
    w = w.reshape(n, r // rows, rows // P, P, c // cols, cols).transpose(0, 4, 1, 3, 2, 5)
    return np.ascontiguousarray(w.reshape(n, c // cols, r // rows, P, rows // P * cols))


def rope_rows():
    tok = np.arange(LAT)
    pos = np.stack([tok // GRID_W, tok % GRID_W], 1).astype(np.float32)
    freq = (np.float32(1.0) / (np.float32(10000.0) ** (np.arange(32, dtype=np.float32) / np.float32(32)))).astype(np.float32)
    ang = pos[:, :, None] * freq
    cos, sin = np.cos(ang, dtype=np.float32), np.sin(ang, dtype=np.float32)
    c = np.stack([cos, cos], 2).reshape(LAT, P)
    s = np.stack([-sin, sin], 2).reshape(LAT, P)
    return np.ascontiguousarray(np.stack([c, s], 1).reshape(LAT, 2 * P).astype(np.float32))


def edge_rows():
    rows = []
    for w in WINDOWS:
        a = w // 2
        left = [w / (t + a - max(t - a, 0)) for t in range(8)]
        right = [w / (min(t + a, 8) - (t - a)) for t in range(8)]
        rows.append(left + right)
    return np.asarray(rows, np.float32).reshape(-1)


def kernel(**inputs):
    import concourse.bacc as bacc
    from concourse.bass_utils import run_bass_kernel_spmd as run

    nc = bacc.Bacc("TRN2", target_bir_lowering=False, num_devices=1)
    x = {k: np.asarray(v) for k, v in inputs.items()}
    w_in = x["w_in"]
    arrays = {
        "x": x["x"].reshape(LAT, D),
        "ctx": x["ctx"].reshape(CTX, D),
        "c_cols": np.stack([x["c_ctx"], x["c"][0]]).reshape(2, KD, P).transpose(2, 0, 1).reshape(P, 2 * KD),
        "pool_scale": x["pool_scale"].reshape(DEPTH, POOL_GROUPS, P).transpose(2, 0, 1).reshape(P, DEPTH * POOL_GROUPS),
        "w_mod": chunked(x["w_mod"], 2 * P, 512),
        "w_qkv": chunked(w_in[:, :, :COL_ZA], 2 * P, 512),
        "w_gates": chunked(w_in[:, :, COL_ZA:], D, P)[:, :, 0],
        "w_pool": x["w_pool"].transpose(0, 2, 1, 3).reshape(DEPTH, P, POOL_GROUPS * P),
        "w_br_a": chunked(x["w_br_a"], D, P)[:, :, 0],
        "w_br_b": chunked(x["w_br_b"], D // 2, P)[:, :, 0],
        "w_out": x["w_out"],
        "rope": rope_rows(),
        "edge": edge_rows(),
    }
    for name in ("b_mod", "q_norm", "k_norm", "ln_g", "ln_b"):
        arrays[name] = x[name]
    arrays = {k: np.ascontiguousarray(v) for k, v in arrays.items()}
    t = {k: nc.dram_tensor(k + "_dram", v.shape, F32, kind="ExternalInput").ap() for k, v in arrays.items()}
    t["out"] = nc.dram_tensor("out_dram", (LAT, D), F32, kind="ExternalOutput").ap()
    build(nc, t)
    r = run(nc, [{k + "_dram": v for k, v in arrays.items()}], core_ids=[0])
    return r.results[0]["out_dram"].reshape(1, LAT, D)
```

```python
import numpy as np
from contextlib import ExitStack

import concourse.bass as bass
from concourse import mybir

F32 = mybir.dt.float32
F32R = mybir.dt.float32r
ALU = mybir.AluOpType
ACT = mybir.ActivationFunctionType
AX_X = mybir.AxisListType.X

P = 128
D = 1024
KD = D // P
DEPTH = 2
LAT, CTX = 512, 256
TOK = LAT + CTX
HEADS, KV_HEADS, GROUP = 8, 2, 4
POOL_GROUPS = 4
WINDOWS = (2, 4, 8, 16)
GRID_W = 64
EPS = 1e-6
ALPHA = float((2 * DEPTH) ** 0.25)
COL_ZA = 1536
PAD = 8

STREAMS = ((0, 0, 2, 2), (0, 2, 4, 6), (1, 2, 4, 6))
LAYER_STREAMS = ((0, 1), (2,))


def weight_chunks(w):
    out = []

    def modulation(l, cgs):
        for cg in cgs:
            for q in range(4):
                out.append(("mod", w["w_mod"][l, cg, q], 2, 512))

    modulation(0, (2, 3, 0, 1))
    modulation(1, range(4))
    for l in range(DEPTH):
        for cg in (2, 0, 1):
            for q in range(4):
                out.append(("qkv", w["w_qkv"][l, cg, q], 2, 512))
        if l == 0:
            modulation(0, (4, 5))
        for s in LAYER_STREAMS[l]:
            out.append(("pool", w["w_pool"][l], 4, P))
            for h in range(HEADS):
                out.append(("za", w["w_gates"][l, h], KD, P))
                out.append(("xz", w["w_gates"][l, (8, 12)[h % 2] + h // 2], KD, P))
            for j in range(KD):
                out.append(("ga", w["w_gates"][l, 16 + j], KD, P))
                out.append(("gb", w["w_gates"][l, 24 + j], KD, P))
                out.append(("ya", w["w_br_a"][l, j], KD, P))
                out.append(("yb", w["w_br_b"][l, j], 4, P))
            for k in range(KD):
                out.append(("out", w["w_out"][l, k * P:(k + 1) * P, :], 1, D))
            if s == 0:
                modulation(1, (4, 5))
    return out


def build(nc, t):
    chunks = weight_chunks(t)
    RAW, BORROWED = (0, 1, 2), (3, 4, 5, 6)
    EARLY_PLACES = 6
    raw_slot, raw_before, raw_turn, split_no, ring_before = [], [], [], [], []
    last_in_raw, last_in_ring, splits, ring_no = {}, {}, [], 0
    uses, outs, streams_begun, last_yb, last_borrowed = {}, 0, 0, None, None
    phase, phase_begin = None, 0
    for n, (kind, _, a, b) in enumerate(chunks):
        if kind == "pool":
            streams_begun += 1
        s_now = streams_begun - 1
        if n < 16:
            now, slots = "first modulation", RAW + BORROWED
        elif s_now == 0 and kind in ("ga", "gb", "ya", "yb"):
            now, slots = "context merge", RAW + BORROWED
        else:
            now, slots = "else", RAW
        if now != phase:
            phase, phase_begin = now, n
        slot = min(slots, key=lambda i: (last_in_raw.get(i, -1) if i in RAW else
                                         max(last_in_raw.get(i, -1), phase_begin - 0.5)))
        raw_slot.append(slot)
        raw_before.append(last_in_raw.get(slot))
        last_in_raw[slot] = n
        uses[slot] = uses.get(slot, 0) + 1
        raw_turn.append(uses[slot])
        if slot in BORROWED:
            last_borrowed = n
        split_no.append(len(splits))
        outs = outs + 1 if kind == "out" else outs
        if kind != "out" and kind != "mod":
            outs = 0
        if kind == "mod" and n < 32:
            place = ("q", n % EARLY_PLACES)
        elif kind == "out" and s_now >= 1 and outs > 2:
            place = ("q", outs - 3)
        elif kind in ("pool", "yb"):
            place = "pool"
        else:
            place = ring_no % 2
            ring_no += 1
        ring_before.append(last_yb if kind == "out" and isinstance(place, tuple) else last_in_ring.get(place))
        last_in_ring[place] = n
        if kind == "yb":
            last_yb = n
        splits.append((n, place))
    first = {}
    for n, (kind, *_r) in enumerate(chunks):
        first.setdefault(kind, []).append(n)
    POOL_N = first["pool"]
    XZ_N, GA_N, OUT_N, QKV_N = first["xz"], first["ga"], first["out"], first["qkv"]
    for s in range(3):
        ring_before[first["yb"][8 * s]] = GA_N[8 * s]

    done_count, ring_chunks = [], 0
    for kind, *_r in chunks:
        ring_chunks += kind != "pool"
        done_count.append(ring_chunks)

    MOD_N = [first["mod"][4 * i + 3] for i in range(12)]
    MOD_GROUPS = [(0, g) for g in (2, 3, 0, 1)] + [(1, g) for g in range(4)] + [(0, 4), (0, 5), (1, 4), (1, 5)]
    MOD_BANKS = (6, 7, 6, 7, 6, 7, 6, 7, 4, 5, 6, 7)

    POOL_LO = [n for n in first["mod"][33::2]]
    lo_no = {}
    for n in range(len(chunks)):
        lo_no[n] = POOL_LO.index(n) if n in POOL_LO else n - sum(p < n for p in POOL_LO)

    def done(n):
        return done_count[n]

    def p2_no(l, g, tile):
        if l == 0:
            return 6 * g + tile
        return 18 + (tile if g == 0 else 6 + 4 * (g - 1) + tile - 2)

    def p2_tiles(l, g):
        return list(range(6)) if l == 0 or g == 0 else list(range(2, 6))

    STEP0 = (0, 16, 48)

    def step_no(s, h, i):
        return STEP0[s] + h * STREAMS[s][2] + i

    def head_no(s, h):
        return 8 * s + h

    TILE0 = (0, 2, 6)

    def out_no(s, tile):
        return TILE0[s] + tile

    def acc_count(l, g, tile):
        n = 0
        for ll in range(DEPTH):
            for gg in range(3):
                for tt in p2_tiles(ll, gg)[:-1]:
                    n += 1
                    if (ll, gg, tt) == (l, g, tile):
                        return n
        raise ValueError

    def bc_count(s):
        return 16 * 5 * (s + 1)

    def ssq_count(l, g, tile):
        n = 0
        for ll in range(DEPTH):
            for gg in range(3):
                for tt in p2_tiles(ll, gg):
                    n += 2 if gg == 0 else 4
                    if (ll, gg, tt) == (l, g, tile):
                        return n
        raise ValueError

    with ExitStack() as ctx:
        def sb(name, n, dt=F32):
            return ctx.enter_context(nc.sbuf_tensor(name, [P, n], dt))

        def sem(name):
            return ctx.enter_context(nc.semaphore(name))

        arena = sb("arena", 41984, F32R)
        work = sb("work", 7168)
        raw = sb("raw", 3072)
        ident = sb("ident", P)
        stat = sb("stat", 272)
        sc_pair = sb("sc_pair", 32, F32R)
        half = sb("half", 512)

        def view(off, a, b):
            return arena[:, off:off + a * b].rearrange("p (a b) -> p a b", a=a)

        def pair(off, a, b):
            return view(off, a, b), view(off + a * b, a, b)

        U = (pair(0, KD, CTX), pair(4096, KD, LAT))
        Q = (pair(12288, HEADS, CTX), pair(16384, HEADS, LAT))
        K = pair(24576, KV_HEADS, TOK)
        V = pair(27648, 6, KV_HEADS * P)
        SCR = 30720
        PT = (pair(SCR, 2, CTX), pair(SCR, 6, LAT), pair(SCR, 6, LAT))
        Y = (pair(SCR, KD, CTX), pair(24576, KD, LAT), pair(24576, KD, LAT))
        M = (pair(SCR + 4096, POOL_GROUPS, CTX), pair(12288, POOL_GROUPS, LAT), pair(12288, POOL_GROUPS, LAT))
        W = (36864, 38912)
        Q_PLACE = 12288
        WP = pair(40960, POOL_GROUPS, P)

        def u_tile(tile):
            if tile < 2:
                return tuple(x[:, :, tile * P:(tile + 1) * P] for x in U[0])
            return tuple(x[:, :, (tile - 2) * P:(tile - 1) * P] for x in U[1])

        def q_tile(tile, h0, n):
            if tile < 2:
                return tuple(x[:, h0:h0 + n, tile * P:(tile + 1) * P] for x in Q[0])
            return tuple(x[:, h0:h0 + n, (tile - 2) * P:(tile - 1) * P] for x in Q[1])

        def split_place(m):
            n, place = splits[m]
            size = chunks[n][2] * chunks[n][3]
            if place == "pool":
                off = 40960
            elif isinstance(place, tuple):
                off = Q_PLACE + 2048 * place[1]
            else:
                off = W[place]
            step = 512 if place == "pool" else 1024
            return arena[:, off:off + size], arena[:, off + step:off + step + size]

        def ring(n):
            hi, lo = split_place(split_no[n])
            a = chunks[n][2]
            return hi.rearrange("p (a b) -> p a b", a=a), lo.rearrange("p (a b) -> p a b", a=a)

        def raw_of(n):
            size, slot = chunks[n][2] * chunks[n][3], raw_slot[n]
            if slot in BORROWED:
                off = 1024 * (slot - BORROWED[0])
                return work[:, off:off + size]
            return raw[:, slot * 1024:slot * 1024 + size]

        def wk(off, n):
            return work[:, off:off + n]

        RQ = stat[:, 0:48].rearrange("p (t h) -> p t h", t=6)
        RK = stat[:, 48:60].rearrange("p (t h) -> p t h", t=6)
        SSQ = stat[:, 64:88].rearrange("p (t h) -> p t h", t=6)
        RTMP = stat[:, 88:112].rearrange("p (t h) -> p t h", t=6)
        MHALF = stat[:, 112:116]
        NB = stat[:, 116:118]
        MX = stat[:, 118:120]
        RSUM = stat[:, 120:122]
        RINV = stat[:, 122:124]
        BN = stat[:, 124:136].rearrange("p (a b) -> p a b", a=2)
        MV = stat[:, 264:268].rearrange("p (a b) -> p a b", a=2)
        RSTD = stat[:, 268:270]
        NMR = stat[:, 270:272]
        SC = stat[:, 140:156].rearrange("p (v k) -> p v k", v=2)
        SC_HI, SC_LO = (sc_pair[:, 16 * i:16 * i + 16].rearrange("p (v k) -> p v k", v=2) for i in range(2))
        CRAW = stat[:, 156:172].rearrange("p (v k) -> p v k", v=2)
        CTH = stat[:, 172:188].rearrange("p (v k) -> p v k", v=2)
        PS = stat[:, 188:196].rearrange("p (l g) -> p l g", l=2)
        EDGE = stat[:, 196:260].rearrange("p (g e) -> p g e", g=4)
        VEPS = stat[:, 260:262]

        ps = ctx.enter_context(nc.psum_tensor("ps", [P, 8, 512], F32))

        MODROW = half[0:2, :]
        FIRST_ROWS = work[0:2, 5120:7168]
        BC = [wk(1024 * i, 1024) for i in range(5)]
        R = ((wk(5120, 1024), wk(6144, 1024)), (wk(5120, 1024), wk(6144, 1024)) * 2,
             (wk(1024, 1024), wk(2048, 1024), wk(5120, 1024), wk(6144, 1024)))
        N = [wk(3072, 1024), wk(4096, 1024)]
        TAB = wk(0, 2048).rearrange("p (t k f) -> p t k f", t=4, k=4)
        GN = wk(2048, 512).rearrange("p (k f) -> p k f", k=4)
        QRAW = wk(2560, 3072).rearrange("p (t f) -> p t f", t=6)
        CS = wk(2560, 1024).rearrange("p (t k f) -> p t k f", t=4, k=2)
        SQ = wk(6656, 512)
        T1, T2 = wk(5632, 512), wk(6144, 512)
        PR = [wk(768 * i, 768) for i in range(2)]
        THZ = wk(1536, 512)
        SZA = [wk(2048, 512), wk(2560, 512)]
        XP, XA, XB_ = wk(3072, 528), wk(3600, 528), wk(4128, 528)
        PM = wk(4656, 512)
        THB = wk(5168, 512)
        SZB = wk(5680, 512)
        OG = wk(6192, 512)
        THA_, THB_, YA_, YB_ = wk(5120, 512), wk(5632, 512), wk(6144, 512), wk(6656, 512)

        mod_rows = nc.dram_tensor("mod_rows", (DEPTH, 2, 3 * D), F32, kind="Internal").ap()
        xhat_mid = nc.dram_tensor("xhat_mid", (LAT, D), F32, kind="Internal").ap()

        landed = [sem(f"raw_landed{i}") for i in range(len(RAW + BORROWED))]
        w_hi, w_lo, w_lo_pool = sem("w_hi"), sem("w_lo"), sem("w_lo_pool")
        chunk_done = sem("chunk_done")
        c_in, consts = sem("c_in"), sem("consts")
        ident_ready = sem("ident_ready")
        silu_c = sem("silu_c")
        act_own, dve_own, pool_own = sem("act_own"), sem("dve_own"), sem("pool_own")
        rows_init, dram_init = sem("rows_init"), sem("dram_init")
        rows_spread, bc_copied = sem("rows_spread"), sem("bc_copied")
        mod_evac = sem("mod_evac")
        mod_stored = sem("mod_stored")
        bc_in = sem("bc_in")
        x_in = [sem(f"x_in{i}") for i in range(3)]
        x_res = [sem(f"x_res{i}") for i in range(2)]
        u_made, u_turned, u_hi, u_lo = sem("u_made"), sem("u_turned"), sem("u_hi"), sem("u_lo")
        tab_in, tab_ready = sem("tab_in"), sem("tab_ready")
        acc_done = sem("acc_done")
        q_copied, ssq_done, rms_ready = sem("q_copied"), sem("ssq_done"), sem("rms_ready")
        v_split = sem("v_split")
        roped, q_turned, qk_hi, qk_lo = sem("roped"), sem("q_turned"), sem("qk_hi"), sem("qk_lo")
        s_done, nb_ready, exp_done, p_ready = sem("s_done"), sem("nb_ready"), sem("exp_done"), sem("p_ready")
        p_turned, pt_hi, pt_lo = sem("p_turned"), sem("pt_hi"), sem("pt_lo")
        pv_done, og_ready, o_hi, o_lo = sem("pv_done"), sem("og_ready"), sem("o_hi"), sem("o_lo")
        za_tanh, sza_ready = sem("za_tanh"), sem("sza_ready")
        xb_copied, pooled = sem("xb_copied"), sem("pooled")
        m_hi, m_lo, pool_mm = sem("m_hi"), sem("m_lo"), sem("pool_mm")
        zb_tanh, szb_ready = sem("zb_tanh"), sem("szb_ready")
        pg_ready, pg_hi, pg_lo = sem("pg_ready"), sem("pg_hi"), sem("pg_lo")
        ga_tanh, merged, y_hi, y_lo = sem("ga_tanh"), sem("merged"), sem("y_hi"), sem("y_lo")
        out_acc, xhat_ready, stored = sem("out_acc"), sem("xhat_ready"), sem("stored")
        r_affine, out_ready, out_stored = sem("r_affine"), sem("out_ready"), sem("out_stored")
        centred = sem("centred")
        var_ready, rstd_ready = sem("var_ready"), sem("rstd_ready")
        block = ctx.enter_context(nc.Block())

        def s_bank(s, a):
            cols = STREAMS[s][3] * P
            return ps[:, a % 2, 0:cols] if s == 0 else ps[:, 0:2, :].rearrange("p a b -> p (a b)")[:, 0:cols]

        def p_bank(s, a):
            nk = STREAMS[s][3]
            bank = 2 + a % 2
            v = ps[:, bank:bank + 1, :] if s == 0 else ps[:, 2:4, :]
            return v.rearrange("p a (b c) -> p (a b) c", c=P)[:, 0:nk]

        def wait_lo(eng, n):
            eng.wait_ge(w_lo_pool if n in POOL_LO else w_lo, lo_no[n] + 1)

        @block.sync
        def _(sp):
            sp.dma_start(CRAW.rearrange("p v k -> p (v k)"), t["c_cols"]).then_inc(c_in, 16)
            for n, (kind, src, a, b) in enumerate(chunks):
                if n == 3:
                    sp.dma_start(FIRST_ROWS, t["b_mod"][0, 0:2 * D].partition_broadcast(2)).then_inc(rows_init, 16)
                if n > 16 and raw_slot[n] in BORROWED:
                    sp.wait_ge(o_lo, 8)
                    sp.wait_ge(pg_lo, 4)
                if raw_before[n] is not None:
                    wait_lo(sp, raw_before[n])
                sp.dma_start(raw_of(n), src).then_inc(landed[raw_slot[n]], 16)
            for tile in range(4):
                for hf in range(2):
                    cols = slice(hf * 512, (hf + 1) * 512)
                    sp.wait_ge(out_ready, 2 * tile + hf + 1)
                    sp.dma_start(t["out"][tile * P:(tile + 1) * P, cols], R[2][tile][:, cols]).then_inc(out_stored, 16)
            sp.wait_ge(out_stored, 16 * 8)

        def wait_landed(eng, n):
            eng.wait_ge(landed[raw_slot[n]], 16 * raw_turn[n])

        @block.scalar
        def _(act):
            own = [0]
            m = 0

            def split(m):
                if m >= len(splits):
                    return
                n = splits[m][0]
                wait_landed(act, n)
                if ring_before[n] is not None:
                    act.wait_ge(chunk_done, done(ring_before[n]))
                nc.scalar.activation(split_place(m)[0], raw_of(n), ACT.Copy).then_inc(w_hi, 1)

            act.wait_ge(c_in, 16)
            nc.scalar.activation(CTH, CRAW, ACT.Tanh, scale=0.5).then_inc(silu_c, 1)
            act.wait_ge(silu_c, 2)
            nc.scalar.activation(SC_HI, SC, ACT.Copy).then_inc(silu_c, 1)

            def turn_u(no, tile, bank):
                act.wait_ge(u_turned, no + 1)
                nc.scalar.activation(u_tile(tile)[0], ps[:, bank:bank + 2, :].rearrange("p a (b c) -> p (a b) c", c=P),
                                     ACT.Copy).then_inc(u_hi, 1)

            def spread_copy(no):
                act.wait_ge(rows_spread, no + 1)
                if no == 0:
                    act.wait_ge(w_lo, 16)
                bank = 2 * (no % 3)
                nc.scalar.activation(BC[2 * (no % 2) + no // 2], ps[:, bank:bank + 2, :].rearrange("p a b -> p (a b)"),
                                     ACT.Copy).then_inc(bc_copied, 1)

            for m in range(18):
                split(m)
            spread_copy(0)
            spread_copy(1)
            split(18)
            split(19)
            spread_copy(2)
            spread_copy(3)
            for m in range(20, 24):
                split(m)
            for tile in range(2):
                turn_u(tile, tile, 2 * (tile % 3))
                for m in range(24 + 4 * tile, 28 + 4 * tile):
                    split(m)
            for tile in range(2, 5):
                turn_u(tile, tile, 2 * (tile % 3))
            m = 32
            split(m)
            turn_u(5, 5, 4)
            for l in range(DEPTH):
                def copies(g, c):
                    for tile in p2_tiles(l, g):
                        no = p2_no(l, g, tile)
                        if tile == p2_tiles(l, g)[-1]:
                            act.wait_ge(chunk_done, done(QKV_N[12 * l + 4 * g + 3]))
                        else:
                            act.wait_ge(acc_done, acc_count(l, g, tile))
                        if g > 0:
                            act.wait_ge(q_turned, p2_no(l, g - 1, tile) + 1)
                        elif tile == 0:
                            act.wait_ge(tab_ready, 4 * (l + 1))
                        if g == 0:
                            nc.scalar.activation(QRAW[:, tile, 0:256], ps[:, tile, 0:256], ACT.Copy)
                            nc.scalar.activation(V[0][:, tile, :], ps[:, tile, 256:512], ACT.Copy).then_inc(q_copied, 1)
                        else:
                            nc.scalar.activation(QRAW[:, tile, :], ps[:, tile, :], ACT.Copy).then_inc(q_copied, 1)

                def squares(g, tiles):
                    n = 2 if g == 0 else 4
                    for tile in tiles:
                        no = p2_no(l, g, tile)
                        act.wait_ge(q_copied, no + 1)
                        if g or l:
                            act.wait_ge(rms_ready, (p2_no(l, g - 1, tile) if g else p2_no(l - 1, 2, tile)) + 1)
                        if own[0]:
                            act.wait_ge(ssq_done, own[0])
                        for h in range(n):
                            ins = nc.scalar.activation(SQ[:, h * P:(h + 1) * P], QRAW[:, tile, h * P:(h + 1) * P], ACT.Square,
                                                       accum_out=SSQ[:, tile, h:h + 1])
                            own[0] += 1
                            ins.then_inc(ssq_done, 1)

                def turned(g, tiles):
                    n = 2 if g == 0 else 4
                    for tile in tiles:
                        no = p2_no(l, g, tile)
                        act.wait_ge(q_turned, no + 1)
                        src = ps[:, 6 + no % 2, 0:n * P].rearrange("p (h c) -> p h c", h=n)
                        dst = K[0][:, :, tile * P:(tile + 1) * P] if g == 0 else q_tile(tile, 4 * (g - 1), 4)[0]
                        nc.scalar.activation(dst, src, ACT.Copy).then_inc(qk_hi, 1)

                for g in range(3):
                    for c in range(4):
                        split(m + 1)
                        m += 1
                        if g > 0:
                            tl = p2_tiles(l, g - 1)
                            if c < 3:
                                squares(g - 1, tl[2 * c:2 * c + 2])
                            if c > 0:
                                turned(g - 1, tl[2 * c - 2:2 * c])
                        if c == 3:
                            copies(g, c)
                tl = p2_tiles(l, 2)
                for k in range(len(tl) + 2):
                    squares(2, tl[k:k + 1])
                    if l == 0:
                        split(m + 1)
                        m += 1
                    if k >= 2:
                        turned(2, tl[k - 2:k - 1])

                for s in LAYER_STREAMS[l]:
                    _, t0, nt, nk = STREAMS[s]
                    T, lat = nt * P, s > 0
                    split(m + 1)
                    m += 1

                    def probs_hi(h, i):
                        a = step_no(s, h, i)
                        act.wait_ge(p_turned, a + 1)
                        if h > 0 and i == 0:
                            act.wait_ge(pv_done, head_no(s, h))
                        src = p_bank(s, a)
                        nc.scalar.activation(PT[s][0][:, :, i * P:(i + 1) * P], src, ACT.Copy).then_inc(pt_hi, 1)

                    def gate_tanh(h):
                        act.wait_ge(chunk_done, done(XZ_N[8 * s + h] - 1))
                        if h > 0 or s > 0:
                            act.wait_ge(sza_ready, head_no(s, h))
                        nc.scalar.activation(THZ[:, 0:T], ps[:, 4, 0:T], ACT.Tanh, scale=0.5).then_inc(za_tanh, 1)

                    def pool_out(h):
                        g = h // 2
                        act.wait_ge(chunk_done, done(XZ_N[8 * s + h]))
                        no = 4 * s + g
                        if h % 2 == 0:
                            if no:
                                act.wait_ge(m_lo, no)
                            nc.scalar.activation(XP[:, PAD:PAD + T], ps[:, 5, 0:T], ACT.Copy).then_inc(xb_copied, 1)
                        else:
                            if no:
                                act.wait_ge(szb_ready, no)
                            nc.scalar.activation(THB[:, 0:T], ps[:, 5, 0:T], ACT.Tanh, scale=0.5).then_inc(zb_tanh, 1)

                    def pooled_hi(g):
                        no = 4 * s + g
                        act.wait_ge(pooled, no + 1)
                        nc.scalar.activation(M[s][0][:, g, :], PM[:, 0:T], ACT.Copy).then_inc(m_hi, 1)

                    def pool_gated_hi(g):
                        no = 4 * s + g
                        act.wait_ge(pg_ready, no + 1)
                        nc.scalar.activation(M[s][0][:, g, :], PM[:, 0:T], ACT.Copy).then_inc(pg_hi, 1)

                    def attn_out(h):
                        act.wait_ge(og_ready, head_no(s, h) + 1)
                        nc.scalar.activation(Q[min(s, 1)][0][:, h, :], OG[:, 0:T], ACT.Copy).then_inc(o_hi, 1)

                    act.wait_ge(rms_ready, p2_no(l, 2, 5) + 1)
                    prev = None
                    for h in range(HEADS):
                        for i in range(nt):
                            a = step_no(s, h, i)
                            if i == 0 or i == nt // 2:
                                split(m + 1)
                                m += 1
                            act.wait_ge(nb_ready, a + 1)
                            if a >= 2:
                                act.wait_ge(p_turned, a - 1)
                            nc.scalar.activation(PR[a % 2][:, 0:nk * P],
                                                 s_bank(s, a), ACT.Exp,
                                                 bias=NB[:, a % 2:a % 2 + 1], scale=RQ[:, t0 + i, h:h + 1],
                                                 accum_out=RSUM[:, a % 2:a % 2 + 1]).then_inc(exp_done, 1)
                            if prev is not None:
                                probs_hi(*prev)
                            prev = (h, i)
                            if i == nt // 2:
                                gate_tanh(h)
                            if i == 0 and h > 0:
                                pool_out(h - 1)
                            if lat and i == 2 and h % 2 == 1:
                                pooled_hi(h // 2)
                            if lat and i == 2 and h % 2 == 0 and h > 0:
                                pool_gated_hi(h // 2 - 1)
                            if not lat and i == 0 and h > 1:
                                (pool_gated_hi if h % 2 else pooled_hi)(h // 2 - 1)
                            if lat and i == 2 and h > 0:
                                attn_out(h - 1)
                            if not lat and i == 0 and h > 1:
                                attn_out(h - 2)
                    probs_hi(*prev)
                    if not lat:
                        pooled_hi(3)
                    pool_out(7)
                    pool_gated_hi(3)
                    if not lat:
                        attn_out(6)
                    attn_out(7)

                    for j in range(KD):
                        for g in range(4):
                            split(m + 1)
                            m += 1
                            n = GA_N[8 * s + j] + g
                            if g < 2:
                                act.wait_ge(chunk_done, done(n))
                                if j or s:
                                    act.wait_ge(merged, 8 * s + j)
                                if j == 0 and g == 0:
                                    act.wait_ge(pg_lo, 4 * s + 4)
                                    act.wait_ge(o_lo, 8 * s + 8)
                                nc.scalar.activation((THA_, THB_)[g][:, 0:T], ps[:, 4 * (j % 2) + g, 0:T],
                                                     ACT.Tanh, scale=0.5).then_inc(ga_tanh, 1)
                            if g == 2 and j > 0:
                                act.wait_ge(merged, 8 * s + j)
                                nc.scalar.activation(Y[s][0][:, j - 1, :], YA_[:, 0:T], ACT.Copy).then_inc(y_hi, 1)
                    act.wait_ge(merged, 8 * s + 8)
                    nc.scalar.activation(Y[s][0][:, 7, :], YA_[:, 0:T], ACT.Copy).then_inc(y_hi, 1)

                    for k in range(KD):
                        split(m + 1)
                        m += 1
                    def next_splits(count):
                        nonlocal m
                        for _ in range(count if s == 0 else 0):
                            split(m + 1)
                            m += 1

                    next_splits(5)
                    for tile in range(nt if s < 2 else 0):
                        no = out_no(s, tile)
                        if s == 1:
                            if tile:
                                turn_u(6 + no - 1, t0 + tile - 1, 2 * (tile - 1))
                            act.wait_ge(rstd_ready, no + 1)
                            act.wait_ge(centred, no + 1)
                            nc.scalar.activation(R[s][tile], R[s][tile], ACT.Identity, bias=NMR[:, no % 2:no % 2 + 1],
                                                 scale=RSTD[:, no % 2:no % 2 + 1]).then_inc(xhat_ready, 1)
                        else:
                            turn_u(6 + no, t0 + tile, 2 * tile)
                            next_splits(2 - tile)
                    if s == 1:
                        turn_u(6 + no, t0 + nt - 1, 2 * (nt - 1))

        @block.vector
        def _(dve):
            own = [0]

            def link(ins):
                own[0] += 1
                ins.then_inc(dve_own, 1)
                dve.wait_ge(dve_own, own[0])

            def split(m):
                if m >= len(splits):
                    return
                n = splits[m][0]
                if n in POOL_LO:
                    return
                hi, lo = split_place(m)
                dve.wait_ge(w_hi, m + 1)
                nc.vector.tensor_tensor(lo, raw_of(n), hi.bitcast(F32), ALU.subtract).then_inc(w_lo, 1)

            dve.wait_ge(silu_c, 1)
            link(nc.vector.scalar_tensor_tensor(out=CTH, in0=CTH, scalar=1.0, in1=CRAW, op0=ALU.add, op1=ALU.mult))
            nc.vector.tensor_scalar(SC, CTH, 0.5, None, ALU.mult).then_inc(silu_c, 1)
            dve.wait_ge(silu_c, 3)
            nc.vector.tensor_tensor(SC_LO, SC, SC_HI.bitcast(F32), ALU.subtract).then_inc(silu_c, 1)
            dve.wait_ge(consts, 16 * 2)
            link(nc.vector.tensor_scalar(PS, PS, 0.5, None, ALU.mult))

            def modulation(no):
                dve.wait_ge(chunk_done, done(MOD_N[no]))
                group, acc = MOD_GROUPS[no][1], ps[0:2, MOD_BANKS[no], :]
                if no < 4:
                    row = FIRST_ROWS[:, group * 512:(group + 1) * 512]
                    dve.wait_ge(rows_init, 16)
                    nc.vector.scalar_tensor_tensor(out=row, in0=acc, scalar=float(group >= 2), in1=row, op0=ALU.add,
                                                   op1=ALU.add).then_inc(mod_evac, 1)
                    return
                if no > 4:
                    dve.wait_ge(mod_stored, 16 * (no - 4))
                nc.vector.tensor_scalar(MODROW, acc, float(group in (2, 3)), None, ALU.add).then_inc(mod_evac, 1)

            def turn_u(no, tile, bank):
                dve.wait_ge(u_hi, no + 1)
                hi, lo = u_tile(tile)
                nc.vector.tensor_tensor(lo, ps[:, bank:bank + 2, :].rearrange("p a (b c) -> p (a b) c", c=P),
                                        hi.bitcast(F32), ALU.subtract).then_inc(u_lo, 1)

            def first_u(tile):
                s = 0 if tile < 2 else 1
                x_t = wk(4096 + 1024 * (tile % 3), 1024)
                dve.wait_ge(bc_copied, 4 if s else 3)
                dve.wait_ge(x_in[tile % 3], 16 * (tile // 3 + 1))
                link(nc.vector.tensor_tensor(x_t, x_t, BC[2 * s], ALU.mult))
                nc.vector.tensor_tensor(x_t, x_t, BC[2 * s + 1], ALU.add).then_inc(u_made, 1)

            def first_lo(tile):
                turn_u(tile, tile, 2 * (tile % 3))

            def splits_of(group):
                for i in range(4 * group, 4 * group + 4):
                    split(i)

            splits_of(0)
            for no in range(3):
                splits_of(no + 1)
                modulation(no)
            split(16)
            split(17)
            modulation(3)
            split(18)
            split(19)
            first_u(0)
            split(20)
            split(21)
            first_u(1)
            split(22)
            split(23)
            modulation(4)
            first_lo(0)
            first_u(2)
            split(24)
            split(25)
            first_lo(1)
            split(26)
            split(27)
            modulation(5)
            first_u(3)
            splits_of(7)
            first_lo(2)
            first_u(4)
            modulation(6)
            first_u(5)
            first_lo(3)
            first_lo(4)
            m = 32
            split(m)
            modulation(7)
            first_lo(5)
            for l in range(DEPTH):
                def v_lo(tile):
                    dve.wait_ge(q_copied, p2_no(l, 0, tile) + 1)
                    nc.vector.tensor_tensor(V[1][:, tile, :], ps[:, tile, 256:512], V[0][:, tile, :].bitcast(F32),
                                            ALU.subtract).then_inc(v_split, 1)

                def rope(g, tiles):
                    n = 2 if g == 0 else 4
                    for tile in tiles:
                        no = p2_no(l, g, tile)
                        dve.wait_ge(q_copied, no + 1)
                        dve.wait_ge(tab_ready, 4 * (l + 1))
                        x = QRAW[:, tile, 0:n * P]
                        ki = 2 if g == 0 else 0
                        heads_ = x.rearrange("p (h f) -> p h f", h=n)
                        dve.wait_ge(ssq_done, ssq_count(l, g, tile))
                        if tile < 2:
                            out = heads_
                            last = nc.vector.tensor_tensor(out, heads_, GN[:, ki:ki + 1, :].to_broadcast([P, n, P]),
                                                           ALU.mult)
                        else:
                            a, b = T1[:, 0:n * P], T2[:, 0:n * P]
                            dve.wait_ge(roped, no)
                            ca = TAB[:, tile - 2, ki:ki + 1, :].to_broadcast([P, n, P])
                            sn = TAB[:, tile - 2, ki + 1, :].rearrange("p (a z f) -> p a z f", z=2, f=32)
                            nc.vector.tensor_tensor(a.rearrange("p (h f) -> p h f", h=n), heads_, ca,
                                                    ALU.mult).then_inc(dve_own, 1)
                            for z in range(2):
                                nc.vector.tensor_tensor(
                                    b.rearrange("p (h a z f) -> p h a z f", a=2, z=2, f=32)[:, :, :, z, :],
                                    x.rearrange("p (h a z f) -> p h a z f", a=2, z=2, f=32)[:, :, :, 1 - z, :],
                                    sn[:, :, z, :].unsqueeze(1).to_broadcast([P, n, 2, 32]), ALU.mult).then_inc(dve_own, 1)
                            own[0] += 3
                            dve.wait_ge(dve_own, own[0])
                            last = nc.vector.tensor_tensor(x, a, b, ALU.add)
                        if g == 0:
                            link(last)
                            dve.wait_ge(rms_ready, no + 1)
                            last = nc.vector.tensor_tensor(
                                heads_, heads_, RK[:, tile, :].unsqueeze(2).to_broadcast([P, 2, P]), ALU.mult)
                        last.then_inc(roped, 1)

                def turned(g, tiles):
                    n = 2 if g == 0 else 4
                    for tile in tiles:
                        no = p2_no(l, g, tile)
                        dve.wait_ge(qk_hi, no + 1)
                        src = ps[:, 6 + no % 2, 0:n * P].rearrange("p (h c) -> p h c", h=n)
                        hi, lo = ((x[:, :, tile * P:(tile + 1) * P] for x in K) if g == 0
                                  else q_tile(tile, 4 * (g - 1), 4))
                        nc.vector.tensor_tensor(lo, src, hi.bitcast(F32), ALU.subtract).then_inc(qk_lo, 1)

                for g in range(3):
                    for c in range(4):
                        split(m + 1)
                        m += 1
                        if g == 0 and c == 2:
                            dve.wait_ge(tab_in, 16 * 7 * (l + 1))
                            for k in range(4):
                                nc.vector.tensor_tensor(TAB[:, :, k, :], CS[:, :, k % 2, :],
                                                        GN[:, k:k + 1, :].to_broadcast([P, 4, P]),
                                                        ALU.mult).then_inc(tab_ready, 1)
                        if g > 0:
                            tl = p2_tiles(l, g - 1)
                            if c < 3:
                                rope(g - 1, tl[2 * c:2 * c + 2])
                            if c > 0:
                                turned(g - 1, tl[2 * c - 2:2 * c])
                        if c == 3 and g == 0:
                            for tile in range(6):
                                v_lo(tile)
                tl = p2_tiles(l, 2)
                for k in range(len(tl) + 2):
                    rope(2, tl[k:k + 1])
                    if l == 0:
                        split(m + 1)
                        m += 1
                    if k >= 2:
                        turned(2, tl[k - 2:k - 1])
                    if l == 0 and k == 4:
                        modulation(8)

                for s in LAYER_STREAMS[l]:
                    _, t0, nt, nk = STREAMS[s]
                    T, lat = nt * P, s > 0
                    split(m + 1)
                    m += 1
                    dve.wait_ge(rms_ready, p2_no(l, 2, 5) + 1)
                    def softmax_max(h, i):
                        a = step_no(s, h, i)
                        dve.wait_ge(s_done, a + 1)
                        link(nc.vector.reduce_max(MX[:, a % 2:a % 2 + 1],
                                                  s_bank(s, a), AX_X))
                        nc.vector.tensor_scalar(NB[:, a % 2:a % 2 + 1], MX[:, a % 2:a % 2 + 1],
                                                RQ[:, t0 + i, h:h + 1], -1.0, ALU.mult, ALU.mult).then_inc(nb_ready, 1)

                    def softmax_norm(h, i):
                        a = step_no(s, h, i)
                        dve.wait_ge(exp_done, a + 1)
                        link(nc.vector.reciprocal(RINV[:, a % 2:a % 2 + 1], RSUM[:, a % 2:a % 2 + 1]))
                        nc.vector.tensor_scalar(PR[a % 2][:, 0:nk * P], PR[a % 2][:, 0:nk * P],
                                                RINV[:, a % 2:a % 2 + 1], 0.5, ALU.mult, ALU.mult).then_inc(p_ready, 1)

                    def probs_lo(h, i):
                        a = step_no(s, h, i)
                        dve.wait_ge(pt_hi, a + 1)
                        src = p_bank(s, a)
                        hi, lo = (x[:, :, i * P:(i + 1) * P] for x in PT[s])
                        nc.vector.tensor_tensor(lo, src, hi.bitcast(F32), ALU.subtract).then_inc(pt_lo, 1)

                    def gate_silu(h):
                        b = head_no(s, h)
                        dve.wait_ge(za_tanh, b + 1)
                        if b >= 2:
                            dve.wait_ge(og_ready, b - 1)
                        nc.vector.scalar_tensor_tensor(out=SZA[b % 2][:, 0:T], in0=THZ[:, 0:T], scalar=1.0,
                                                       in1=ps[:, 4, 0:T], op0=ALU.add, op1=ALU.mult).then_inc(sza_ready, 1)

                    def attn_out(h):
                        b = head_no(s, h)
                        dve.wait_ge(pv_done, b + 1)
                        dve.wait_ge(sza_ready, b + 1)
                        if b:
                            dve.wait_ge(o_lo, b)
                        nc.vector.tensor_tensor(OG[:, 0:T], ps[:, 6, 0:T], SZA[b % 2][:, 0:T],
                                                ALU.mult).then_inc(og_ready, 1)

                    def attn_out_lo(h):
                        b = head_no(s, h)
                        hi, lo = (x[:, h, :] for x in Q[min(s, 1)])
                        dve.wait_ge(o_hi, b + 1)
                        dve.wait_ge(og_ready, b + 1)
                        nc.vector.tensor_tensor(lo, OG[:, 0:T], hi.bitcast(F32), ALU.subtract).then_inc(o_lo, 1)

                    def pooled_lo(g):
                        no = 4 * s + g
                        dve.wait_ge(m_hi, no + 1)
                        dve.wait_ge(pooled, no + 1)
                        nc.vector.tensor_tensor(M[s][1][:, g, :], PM[:, 0:T], M[s][0][:, g, :].bitcast(F32),
                                                ALU.subtract).then_inc(m_lo, 1)

                    def pool_silu(g):
                        no = 4 * s + g
                        dve.wait_ge(zb_tanh, no + 1)
                        if no:
                            dve.wait_ge(pg_ready, no)
                        nc.vector.scalar_tensor_tensor(out=SZB[:, 0:T], in0=THB[:, 0:T], scalar=1.0,
                                                       in1=ps[:, 5, 0:T], op0=ALU.add, op1=ALU.mult).then_inc(szb_ready, 1)

                    def pool_gated(g):
                        no = 4 * s + g
                        dve.wait_ge(pool_mm, no + 1)
                        dve.wait_ge(szb_ready, no + 1)
                        nc.vector.scalar_tensor_tensor(out=PM[:, 0:T], in0=ps[:, 7, 0:T], scalar=PS[:, l, g:g + 1],
                                                       in1=SZB[:, 0:T], op0=ALU.mult, op1=ALU.mult).then_inc(pg_ready, 1)

                    def pool_gated_lo(g):
                        no = 4 * s + g
                        dve.wait_ge(pg_hi, no + 1)
                        dve.wait_ge(pg_ready, no + 1)
                        nc.vector.tensor_tensor(M[s][1][:, g, :], PM[:, 0:T], M[s][0][:, g, :].bitcast(F32),
                                                ALU.subtract).then_inc(pg_lo, 1)

                    prev = None
                    for h in range(HEADS):
                        for i in range(nt):
                            softmax_max(h, i)
                            if i == 0 or i == nt // 2:
                                split(m + 1)
                                m += 1
                            softmax_norm(h, i)
                            if s == 0 and (h, i) == (0, 0):
                                modulation(9)
                            if prev is not None:
                                probs_lo(*prev)
                            prev = (h, i)
                            if i == nt // 2:
                                gate_silu(h)
                            if i == 0 and h > 0:
                                if h % 2 == 0:
                                    pool_silu(h // 2 - 1)
                                    if not lat:
                                        pooled_lo(h // 2 - 1)
                                elif h > 1:
                                    if lat:
                                        pool_gated_lo(h // 2 - 1)
                                    else:
                                        pool_gated(h // 2 - 1)
                            if i == 1 and h > 1:
                                if lat and h % 2 == 0:
                                    pool_gated(h // 2 - 1)
                                if not lat and h % 2 == 1:
                                    pool_gated_lo(h // 2 - 1)
                            if lat and i == nt - 1 and h % 2 == 1:
                                pooled_lo(h // 2)
                            if lat and i == 2 and h > 0:
                                attn_out(h - 1)
                            if not lat and i == 0 and h > 1:
                                attn_out(h - 2)
                            if lat and i == 3 and h > 0:
                                attn_out_lo(h - 1)
                            if not lat and i == 1 and h > 1:
                                attn_out_lo(h - 2)
                    probs_lo(*prev)
                    if not lat:
                        pooled_lo(3)
                    pool_silu(3)
                    pool_gated(3)
                    pool_gated_lo(3)
                    for h in (6, 7) if not lat else (7,):
                        attn_out(h)
                        attn_out_lo(h)

                    for j in range(KD):
                        for g in range(4):
                            split(m + 1)
                            m += 1
                            n = GA_N[8 * s + j] + g
                            no = 8 * s + j
                            if g == 2 and j > 0:
                                dve.wait_ge(y_hi, no)
                                nc.vector.tensor_tensor(Y[s][1][:, j - 1, :], YA_[:, 0:T],
                                                        Y[s][0][:, j - 1, :].bitcast(F32), ALU.subtract).then_inc(y_lo, 1)
                        dve.wait_ge(chunk_done, done(n))
                        dve.wait_ge(ga_tanh, 2 * no + 2)
                        if no:
                            dve.wait_ge(y_lo, no)
                        b0 = 4 * (j % 2)
                        link(nc.vector.scalar_tensor_tensor(out=YA_[:, 0:T], in0=THA_[:, 0:T], scalar=1.0,
                                                            in1=ps[:, b0 + 2, 0:T], op0=ALU.add, op1=ALU.mult))
                        link(nc.vector.scalar_tensor_tensor(out=YB_[:, 0:T], in0=THB_[:, 0:T], scalar=1.0,
                                                            in1=ps[:, b0 + 3, 0:T], op0=ALU.add, op1=ALU.mult))
                        nc.vector.tensor_tensor(YA_[:, 0:T], YA_[:, 0:T], YB_[:, 0:T], ALU.add).then_inc(merged, 1)
                    dve.wait_ge(y_hi, 8 * s + 8)
                    nc.vector.tensor_tensor(Y[s][1][:, 7, :], YA_[:, 0:T], Y[s][0][:, 7, :].bitcast(F32),
                                            ALU.subtract).then_inc(y_lo, 1)

                    for k in range(KD):
                        split(m + 1)
                        m += 1
                    last_layer = s == 2
                    dve.wait_ge(bc_in, bc_count(s) if s < 2 else bc_count(2) - 32)
                    if not last_layer:
                        link(nc.vector.tensor_tensor(BC[1], BC[1], N[0], ALU.mult))
                        link(nc.vector.tensor_tensor(BC[2], BC[2], N[0], ALU.mult))
                        link(nc.vector.tensor_tensor(BC[2], BC[2], N[1], ALU.add))

                    def residual(tile):
                        no = out_no(s, tile)
                        x = R[s][tile]
                        if s > 0:
                            dve.wait_ge(out_acc, 4 * (s - 1) + tile + 1)
                        else:
                            dve.wait_ge(chunk_done, done(OUT_N[8 * s + 7]))
                        if last_layer:
                            dve.wait_ge(r_affine, tile + 1)
                        else:
                            dve.wait_ge(x_res[no % 2], 16 * (no // 2 + 1))
                        for hf in range(2):
                            cols = slice(hf * 512, (hf + 1) * 512)
                            if s > 0 and tile == nt - 1 and hf == 1:
                                dve.wait_ge(chunk_done, done(OUT_N[8 * s + 7]))
                            link(nc.vector.scalar_tensor_tensor(out=half[:], in0=ps[:, 2 * tile + hf, :], scalar=0.5,
                                                                in1=BC[0][:, cols], op0=ALU.mult, op1=ALU.mult))
                            link(nc.vector.scalar_tensor_tensor(out=x[:, cols], in0=x[:, cols], scalar=ALPHA,
                                                                in1=half[:], op0=ALU.mult, op1=ALU.add))
                            link(nc.vector.bn_stats(BN[:, hf, :], x[:, cols]))
                        if no >= 2:
                            dve.wait_ge(rstd_ready, no - 1)
                        nc.vector.bn_aggr(MV[:, no % 2, :], BN.rearrange("p a b -> p (a b)")).then_inc(var_ready, 1)

                    def centre(out, tile, cols, g):
                        no = out_no(s, tile)
                        dve.wait_ge(var_ready, no + 1)
                        nc.vector.scalar_tensor_tensor(out=out, in0=R[s][tile][:, cols], scalar=MV[:, no % 2, 0:1], in1=g[:, cols],
                                                       op0=ALU.subtract, op1=ALU.mult).then_inc(centred, 1)

                    def scale_and_shift(out, tile, cols, b, centred_count):
                        no = out_no(s, tile)
                        dve.wait_ge(rstd_ready, no + 1)
                        dve.wait_ge(centred, centred_count)
                        return nc.vector.scalar_tensor_tensor(out=out, in0=out, scalar=RSTD[:, no % 2:no % 2 + 1],
                                                              in1=b[:, cols], op0=ALU.mult, op1=ALU.add)

                    def next_u(tile):
                        no = out_no(s, tile)
                        if tile >= 2:
                            dve.wait_ge(u_turned, 6 + no - 1)
                        centre(N[tile % 2], tile, slice(0, D), BC[1])
                        scale_and_shift(N[tile % 2], tile, slice(0, D), BC[2], no + 1).then_inc(u_made, 1)

                    def next_lo(tile):
                        turn_u(6 + out_no(s, tile), t0 + tile, 2 * tile)

                    def output(tile):
                        for hf in range(2):
                            cols = slice(hf * 512, (hf + 1) * 512)
                            x = R[s][tile][:, cols]
                            centre(x, tile, cols, BC[3])
                            scale_and_shift(x, tile, cols, BC[4], 6 + 2 * tile + hf + 1).then_inc(out_ready, 1)

                    if s == 0:
                        residual(0)
                        split(m + 2)
                        next_u(0)
                        residual(1)
                        split(m + 4)
                        modulation(10)
                        next_lo(0)
                        next_u(1)
                        split(m + 6)
                        next_lo(1)
                        modulation(11)
                        split(m + 8)
                        m += 8
                    elif s == 1:
                        dve.wait_ge(mod_stored, 16 * 8)
                        for tile in range(nt):
                            residual(tile)
                            if tile:
                                next_lo(tile - 1)
                            next_u(tile)
                        next_lo(nt - 1)
                    else:
                        for tile in range(nt):
                            residual(tile)
                            if tile == 0:
                                dve.wait_ge(bc_in, bc_count(2))
                            output(tile)

        @block.gpsimd
        def _(pool):
            own = [0]

            def link(ins):
                own[0] += 1
                ins.then_inc(pool_own, 1)
                pool.wait_ge(pool_own, own[0])

            pool.dma_start(PS.rearrange("p l g -> p (l g)"), t["pool_scale"]).then_inc(consts, 16)
            pool.dma_start(EDGE.rearrange("p g e -> p (g e)"), t["edge"].partition_broadcast(P)).then_inc(consts, 16)
            link(nc.gpsimd.memset(ident[:], 0.0))
            nc.gpsimd.affine_select(out=ident[:], in_=ident[:], compare_op=ALU.not_equal, fill=1.0, base=0,
                                    pattern=[[-1, P]], channel_multiplier=1).then_inc(ident_ready, 1)
            link(nc.gpsimd.memset(MHALF, -0.5))
            for v in range(2):
                pool.dma_start(mod_rows[:, v, :], t["b_mod"]).then_inc(dram_init, 16)

            def row(l, s, part):
                return mod_rows[l, min(s, 1), part * D:(part + 1) * D].partition_broadcast(P)

            def x_rows(tile):
                return t["ctx"][tile * P:(tile + 1) * P, :] if tile < 2 else t["x"][(tile - 2) * P:(tile - 1) * P, :]

            def load_x(tile):
                if tile >= 3:
                    pool.wait_ge(u_turned, tile - 2)
                pool.dma_start(wk(4096 + 1024 * (tile % 3), 1024), x_rows(tile)).then_inc(x_in[tile % 3], 16)

            def store_rows(no):
                l, g = MOD_GROUPS[no]
                pool.wait_ge(mod_evac, no + 1)
                pool.dma_start(mod_rows[l, :, g * 512:(g + 1) * 512], MODROW, accum_op=ALU.add).then_inc(mod_stored, 16)

            gate_chunk = 0

            def split_gates(count):
                nonlocal gate_chunk
                for _ in range(count):
                    n = POOL_LO[gate_chunk]
                    hi, lo = split_place(split_no[n])
                    pool.wait_ge(w_hi, split_no[n] + 1)
                    nc.gpsimd.tensor_tensor(lo, raw_of(n), hi.bitcast(F32), ALU.subtract).then_inc(w_lo_pool, 1)
                    gate_chunk += 1

            load_x(0)
            pool.wait_ge(dram_init, 32)
            pool.wait_ge(rows_spread, 4)
            load_x(1)
            load_x(2)
            for tile in range(3, 6):
                load_x(tile)
                store_rows(tile + 1)
            store_rows(7)

            for l in range(DEPTH):
                pool.wait_ge(u_lo, (6, 12)[l])
                pool.dma_start(CS.rearrange("p t k f -> p t (k f)"), t["rope"].rearrange("(t p) f -> p t f", p=P)).then_inc(tab_in, 16)
                for k, g in enumerate((t["q_norm"], t["k_norm"])):
                    pool.dma_start(GN[:, 2 * k, :], g[l].partition_broadcast(P)).then_inc(tab_in, 16)
                    gh = g[l].rearrange("(a z f) -> a z f", z=2, f=32)
                    dst = GN[:, 2 * k + 1, :].rearrange("p (a z f) -> p a z f", z=2, f=32)
                    for z in range(2):
                        pool.dma_start(dst[:, :, z, :], gh[:, 1 - z, :].partition_broadcast(P)).then_inc(tab_in, 16)

                for g in range(3):
                    n = 2 if g == 0 else 4
                    for tile in p2_tiles(l, g):
                        no = p2_no(l, g, tile)
                        pool.wait_ge(ssq_done, ssq_count(l, g, tile))
                        v = RTMP[:, tile, 0:n]
                        link(nc.gpsimd.tensor_scalar(v, SSQ[:, tile, 0:n], 1.0 / P, EPS, ALU.mult, ALU.add))
                        if g == 0:
                            nc.gpsimd.tensor_tensor(RK[:, tile, :], v, MHALF[:, 0:n], ALU.pow).then_inc(rms_ready, 1)
                        else:
                            link(nc.gpsimd.tensor_tensor(v, v, MHALF[:, 0:n], ALU.pow))
                            nc.gpsimd.tensor_scalar(RQ[:, tile, 4 * (g - 1):4 * g], v, float(P) ** -0.5, 0.0,
                                                    ALU.mult, ALU.add).then_inc(rms_ready, 1)
                        if l == 0 and g == 2 and tile % 2 == 0:
                            split_gates(1)

                if l == 0:
                    split_gates(1)
                    store_rows(8)
                    store_rows(9)
                for s in LAYER_STREAMS[l]:
                    _, t0, nt, _ = STREAMS[s]
                    T, last_layer = nt * P, s == 2
                    pool.wait_ge(*((u_lo, 8) if s == 1 else (q_turned, p2_no(l, 2, 5) + 1)))
                    for buf in (XP[:, 0:PAD], XP[:, PAD + T:T + 2 * PAD], XA, XB_):
                        link(nc.gpsimd.memset(buf, 0.0))
                    for g in range(POOL_GROUPS):
                        no = 4 * s + g
                        pool.wait_ge(xb_copied, no + 1)
                        sums, w = XP, 1
                        while w < WINDOWS[g]:
                            a, b = (1, 0) if w == 1 else (w // 2, w // 2)
                            wide = (XA, XB_)[sums is XA]
                            link(nc.gpsimd.tensor_tensor(wide[:, a:T + 2 * PAD - b], sums[:, 0:T + 2 * PAD - a - b],
                                                         sums[:, a + b:T + 2 * PAD], ALU.add))
                            sums, w = wide, 2 * w
                        for e, t1 in enumerate((PAD, T)):
                            link(nc.gpsimd.tensor_tensor(sums[:, t1:t1 + 8], sums[:, t1:t1 + 8], EDGE[:, g, 8 * e:8 * e + 8],
                                                         ALU.mult))
                        link(nc.gpsimd.tensor_scalar(sums[:, PAD:PAD + T], sums[:, PAD:PAD + T], 1.0 / w, 0.0, ALU.mult,
                                                     ALU.add))
                        if no:
                            pool.wait_ge(pg_lo, no)
                        nc.gpsimd.tensor_tensor(PM[:, 0:T], sums[:, PAD:PAD + T], XP[:, PAD:PAD + T],
                                                ALU.subtract).then_inc(pooled, 1)
                    pool.wait_ge(o_lo, 8 * s + 8)
                    pool.wait_ge(pg_lo, 4 * s + 4)
                    pool.wait_ge(mod_stored, 16 * (8 if l else 6))
                    if s == 0:
                        wait_lo(pool, last_borrowed)
                    if last_layer:
                        rows = (row(l, s, 2), t["ln_g"][0].partition_broadcast(P), t["ln_b"][0].partition_broadcast(P))
                        for dst, src in zip((BC[0], BC[3], BC[4]), rows):
                            pool.dma_start(dst, src).then_inc(bc_in, 16)
                        for tile in range(nt):
                            no = out_no(s, tile)
                            if tile == 2:
                                pool.wait_ge(y_lo, 8 * s + 8)
                            pool.dma_start(R[s][tile], xhat_mid[tile * P:(tile + 1) * P, :]).then_inc(x_res[no % 2], 16)
                            pool.wait_ge(x_res[no % 2], 16 * (no // 2 + 1))
                            if tile == 0:
                                pool.wait_ge(bc_in, bc_count(s) - 32)
                            link(nc.gpsimd.tensor_tensor(R[s][tile], R[s][tile], BC[3], ALU.mult))
                            nc.gpsimd.tensor_tensor(R[s][tile], R[s][tile], BC[4], ALU.add).then_inc(r_affine, 1)
                            pool.wait_ge(r_affine, tile + 1)
                        for dst, src in zip((BC[3], BC[4]), (t["ln_g"][1], t["ln_b"][1])):
                            pool.dma_start(dst, src.partition_broadcast(P)).then_inc(bc_in, 16)
                    else:
                        rows = (row(l, s, 2), t["ln_g"][l].partition_broadcast(P), t["ln_b"][l].partition_broadcast(P),
                                row(l + 1, s, 1), row(l + 1, s, 0))
                        for dst, src in zip(BC, rows):
                            pool.dma_start(dst, src).then_inc(bc_in, 16)
                        pool.wait_ge(y_lo, 8 * s + 8)

                    def load_r(tile):
                        src = x_rows(t0 + tile)
                        pool.dma_start(R[s][tile], src).then_inc(x_res[tile % 2], 16)

                    if not last_layer:
                        load_r(0)
                        load_r(1)
                    if s == 0:
                        split_gates(1)
                    for tile in range(nt):
                        no = out_no(s, tile)
                        c = slice(no % 2, no % 2 + 1)
                        pool.wait_ge(var_ready, no + 1)
                        if last_layer and tile >= 2:
                            pool.wait_ge(out_ready, 2 * tile - 2)
                        elif no >= 2:
                            pool.wait_ge(u_made, 6 + no - 1)
                            if no >= 4:
                                pool.wait_ge(xhat_ready, no - 3)
                        link(nc.gpsimd.tensor_scalar(VEPS[:, c], MV[:, no % 2, 1:2], 1.0, EPS, ALU.mult, ALU.add))
                        link(nc.gpsimd.tensor_tensor(RSTD[:, c], VEPS[:, c], MHALF[:, 0:1], ALU.pow))
                        nc.gpsimd.tensor_scalar(NMR[:, c], MV[:, no % 2, 0:1], RSTD[:, c], -1.0, ALU.mult,
                                                ALU.mult).then_inc(rstd_ready, 1)
                        if s == 0:
                            split_gates((2, 1)[tile])
                            if tile == 1:
                                store_rows(10)
                                store_rows(11)
                        if s == 1:
                            pool.wait_ge(xhat_ready, no - 1)
                            pool.dma_start(xhat_mid[tile * P:(tile + 1) * P, :], R[s][tile]).then_inc(stored, 16)
                            if tile + 2 < nt:
                                pool.wait_ge(stored, 16 * (tile + 1))
                                load_r(tile + 2)
            pool.wait_ge(stored, 16 * 4)

        @block.tensor
        def _(pe):
            def product(out, st, mv, start, stop):
                nc.tensor.matmul(out, st[1], mv[0], start=start, stop=False)
                nc.tensor.matmul(out, st[0], mv[1], start=False, stop=False)
                return nc.tensor.matmul(out, st[0], mv[0], start=False, stop=stop)

            n = 0

            def modulation(no, qs=range(4)):
                nonlocal n
                if no >= 2 and qs[0] == 0:
                    pe.wait_ge(mod_evac, no - 1)
                for q in qs:
                    wait_lo(pe, n)
                    wh, wl = ring(n)
                    for kk in range(2):
                        k = 2 * q + kk
                        ins = product(ps[0:2, MOD_BANKS[no], :], (SC_HI[:, :, k], SC_LO[:, :, k]), (wh[:, kk, :], wl[:, kk, :]),
                                      k == 0, k == KD - 1)
                    ins.then_inc(chunk_done, 1)
                    n += 1

            def turn_u(no, src, bank):
                pe.wait_ge(u_made, no + 1)
                for k in range(KD):
                    ins = nc.tensor.transpose(ps[:, bank + k // 4, (k % 4) * P:(k % 4 + 1) * P],
                                              src[:, k * P:(k + 1) * P], ident[:])
                ins.then_inc(u_turned, 1)

            def first_turn(tile):
                if tile >= 3:
                    pe.wait_ge(u_lo, tile - 2)
                turn_u(tile, wk(4096 + 1024 * (tile % 3), 1024), 2 * (tile % 3))

            def spread(no):
                part, v = 1 - no // 2, no % 2
                pe.wait_ge(mod_evac, 2 + 2 * (no // 2))
                if no == 3:
                    pe.wait_ge(bc_copied, 1)
                for hf in range(2):
                    cols = slice(part * D + hf * 512, part * D + (hf + 1) * 512)
                    ins = nc.tensor.matmul(ps[:, 2 * (no % 3) + hf, :], ident[0:2, v:v + 1].to_broadcast([2, P]),
                                           FIRST_ROWS[:, cols], start=True, stop=True)
                ins.then_inc(rows_spread, 1)

            pe.wait_ge(silu_c, 4)
            for no in range(3):
                modulation(no)
            pe.wait_ge(ident_ready, 1)
            spread(0)
            spread(1)
            modulation(3)
            modulation(4, (0, 1))
            spread(2)
            spread(3)
            modulation(4, (2, 3))
            pe.wait_ge(bc_copied, 4)
            first_turn(0)
            first_turn(1)
            modulation(5)
            first_turn(2)
            modulation(6)
            first_turn(3)
            first_turn(4)
            modulation(7)
            first_turn(5)

            for l in range(DEPTH):
                if l == 0:
                    pe.wait_ge(u_lo, 6)
                    pe.wait_ge(mod_evac, 8)

                def turn_q(g, tiles):
                    nh = 2 if g == 0 else 4
                    for tile in tiles:
                        no = p2_no(l, g, tile)
                        pe.wait_ge(roped, no + 1)
                        if no >= 2:
                            pe.wait_ge(qk_lo, no - 1)
                        for h in range(nh):
                            ins = nc.tensor.transpose(ps[:, 6 + no % 2, h * P:(h + 1) * P],
                                                      QRAW[:, tile, h * P:(h + 1) * P], ident[:])
                        ins.then_inc(q_turned, 1)

                for g in range(3):
                    tl = p2_tiles(l, g)
                    for c in range(4):
                        if g > 0 and c > 0:
                            turn_q(g - 1, p2_tiles(l, g - 1)[2 * c - 2:2 * c])
                        wait_lo(pe, n)
                        wh, wl = ring(n)
                        for tile in tl:
                            if c == 0 and g == 0 and l == 1:
                                if tile == 5:
                                    turn_u(11, N[1], 6)
                                pe.wait_ge(u_lo, 9 + max(tile // 2, tile - 2))
                            if c == 0 and g > 0:
                                pe.wait_ge(q_copied, p2_no(l, g - 1, tile) + 1)
                                if g == 1:
                                    pe.wait_ge(v_split, 6 * l + tile + 1)
                            for kk in range(2):
                                k = 2 * c + kk
                                uh, ul = u_tile(tile)
                                ins = product(ps[:, tile, :], (uh[:, k, :], ul[:, k, :]), (wh[:, kk, :], wl[:, kk, :]),
                                              k == 0, k == KD - 1)
                            if tile == tl[-1]:
                                ins.then_inc(chunk_done, 1)
                            elif c == 3:
                                ins.then_inc(acc_done, 1)
                        n += 1
                tl = p2_tiles(l, 2)
                if l == 0:
                    pe.wait_ge(q_copied, p2_no(l, 2, 5) + 1)
                    modulation(8, (0,))
                    for tile in tl:
                        modulation(8 + (tile + 1) // 4, ((tile + 1) % 4,))
                        turn_q(2, [tile])
                    modulation(9, (3,))
                else:
                    turn_q(2, tl)

                for s in LAYER_STREAMS[l]:
                    _, t0, nt, nk = STREAMS[s]
                    T, lat = nt * P, s > 0
                    si = min(s, 1)
                    pe.wait_ge(qk_lo, p2_no(l, 2, 5) + 1)
                    wait_lo(pe, n)
                    if s == 1:
                        pe.wait_ge(u_lo, 8)
                    n += 1

                    def scores(h, i):
                        a = step_no(s, h, i)
                        if a > 1:
                            pe.wait_ge(exp_done, a - (s == 0))
                        qh, ql = (x[:, 0, :] for x in q_tile(t0 + i, h, 1))
                        kh, kl = (x[:, h // GROUP, :] for x in K)
                        for c0 in range(0, nk * P, 512):
                            c1 = min(c0 + 512, nk * P)
                            ins = product(s_bank(s, a)[:, c0:c1], (qh, ql), (kh[:, c0:c1], kl[:, c0:c1]), True, True)
                        ins.then_inc(s_done, 1)

                    def turn_p(h, i):
                        a = step_no(s, h, i)
                        pe.wait_ge(p_ready, a + 1)
                        if a > 1:
                            pe.wait_ge(pt_lo, a - (s == 0))
                        for k in range(nk):
                            ins = nc.tensor.transpose(p_bank(s, a)[:, k, :],
                                                      PR[a % 2][:, k * P:(k + 1) * P], ident[:])
                        ins.then_inc(p_turned, 1)

                    def values(h):
                        b = head_no(s, h)
                        if b:
                            pe.wait_ge(og_ready, b)
                        pe.wait_ge(pt_lo, step_no(s, h, nt - 1) + 1)
                        c0 = (h // GROUP) * P
                        for k in range(nk):
                            ins = product(ps[:, 6, 0:T], (V[0][:, k, c0:c0 + P], V[1][:, k, c0:c0 + P]),
                                          (PT[s][0][:, k, :], PT[s][1][:, k, :]), k == 0, k == nk - 1)
                        ins.then_inc(pv_done, 1)

                    def project(bank, n, ks, start, stop):
                        wh, wl = ring(n)
                        for k in ks:
                            ins = product(ps[:, bank, 0:T], (wh[:, k, :], wl[:, k, :]),
                                          (U[si][0][:, k, :], U[si][1][:, k, :]), start and k == ks[0], stop and k == ks[-1])
                        return ins

                    def pool_product(g):
                        no = 4 * s + g
                        pe.wait_ge(m_lo, no + 1)
                        if no:
                            pe.wait_ge(pg_ready, no)
                        product(ps[:, 7, 0:T], (WP[0][:, g, :], WP[1][:, g, :]), (M[s][0][:, g, :], M[s][1][:, g, :]),
                                True, True).then_inc(pool_mm, 1)

                    prev = None
                    half = nt // 2
                    ks_of = [list(range(KD))] if half == 1 else [[0, 1, 2, 3], [4, 5, 6, 7]]
                    for h in range(HEADS):
                        for i in range(nt):
                            scores(h, i)
                            if prev is not None:
                                turn_p(*prev)
                            prev = (h, i)
                            if i == 1 and h > 0:
                                values(h - 1)
                            part = i % half
                            bank = 4 + i // half
                            if part == 0:
                                wait_lo(pe, n)
                                b = head_no(s, h)
                                if b == 0:
                                    pe.wait_ge(mod_evac, bank + 5)
                                if bank == 4 and b:
                                    pe.wait_ge(sza_ready, b)
                                if bank == 5 and b:
                                    if h % 2:
                                        pe.wait_ge(xb_copied, 4 * s + h // 2 + 1)
                                    else:
                                        pe.wait_ge(szb_ready, 4 * s + h // 2)
                            ins = project(bank, n, ks_of[part], part == 0, part == half - 1)
                            if part == half - 1:
                                ins.then_inc(chunk_done, 1)
                                n += 1
                            if i == (0 if lat else 1) and h % 2 == 0 and h > 0:
                                pool_product(h // 2 - 1)
                    turn_p(*prev)
                    pool_product(3)
                    values(7)

                    for j in range(KD):
                        no = 8 * s + j
                        for g in range(4):
                            bank = 4 * (j % 2) + g
                            wait_lo(pe, n)
                            if g == 0:
                                if j >= 2:
                                    pe.wait_ge(merged, no - 1)
                                elif j == 0:
                                    pe.wait_ge(pt_lo, step_no(s, 7, nt - 1) + 1)
                                    pe.wait_ge(exp_done, step_no(s, 7, nt - 1) + 1)
                                elif j == 1:
                                    pe.wait_ge(pg_ready, 4 * s + 4)
                                    pe.wait_ge(og_ready, 8 * s + 8)
                            if g == 2 and j == 0:
                                pe.wait_ge(o_lo, 8 * s + 8)
                            if g == 3 and j == 0:
                                pe.wait_ge(pg_lo, 4 * s + 4)
                            if g < 2:
                                ins = project(bank, n, list(range(KD)), True, True)
                            else:
                                op = Q[si] if g == 2 else M[s]
                                nkk = KD if g == 2 else POOL_GROUPS
                                wh, wl = ring(n)
                                for k in range(nkk):
                                    ins = product(ps[:, bank, 0:T], (wh[:, k, :], wl[:, k, :]),
                                                  (op[0][:, k, :], op[1][:, k, :]), k == 0, k == nkk - 1)
                            ins.then_inc(chunk_done, 1)
                            n += 1

                    def out_product(n, k, tile, hfs=(0, 1)):
                        wh, wl = ring(n)
                        for hf in hfs:
                            st = tuple(x[:, k, tile * P:(tile + 1) * P] for x in Y[s])
                            mv = tuple(x[:, 0, hf * 512:(hf + 1) * 512] for x in (wh, wl))
                            ins = product(ps[:, 2 * tile + hf, :], st, mv, k == 0, k == KD - 1)
                        return ins

                    streamed = KD if s == 0 else 2
                    for k in range(streamed):
                        wait_lo(pe, n)
                        pe.wait_ge(y_lo, 8 * s + k + 1)
                        if k == 0:
                            pe.wait_ge(merged, 8 * s + 8)
                        for tile in range(nt):
                            ins = out_product(n, k, tile)
                        ins.then_inc(chunk_done, 1)
                        n += 1
                    if s == 0:
                        modulation(10)
                        turn_u(6, N[0], 0)
                        modulation(11)
                        turn_u(7, N[1], 2)
                        pe.wait_ge(mod_evac, 12)
                    else:
                        for tile in range(nt):
                            last = tile == nt - 1
                            for hfs in ((0,), (1,)) if last else ((0, 1),):
                                for k in range(streamed, KD):
                                    if tile == 0:
                                        wait_lo(pe, n + k - streamed)
                                        pe.wait_ge(y_lo, 8 * s + k + 1)
                                    ins = out_product(n + k - streamed, k, tile, hfs)
                                    if hfs == (1,):
                                        ins.then_inc(chunk_done, 1)
                                if hfs != (1,):
                                    ins.then_inc(out_acc, 1)
                            if s == 1 and tile:
                                turn_u(6 + out_no(s, tile - 1), N[(tile - 1) % 2], 2 * (tile - 1))
                        n += KD - streamed


def chunked(w, rows, cols):
    n, r, c = w.shape
    w = w.reshape(n, r // rows, rows // P, P, c // cols, cols).transpose(0, 4, 1, 3, 2, 5)
    return np.ascontiguousarray(w.reshape(n, c // cols, r // rows, P, rows // P * cols))


def rope_rows():
    tok = np.arange(LAT)
    pos = np.stack([tok // GRID_W, tok % GRID_W], 1).astype(np.float32)
    freq = (np.float32(1.0) / (np.float32(10000.0) ** (np.arange(32, dtype=np.float32) / np.float32(32)))).astype(np.float32)
    ang = pos[:, :, None] * freq
    cos, sin = np.cos(ang, dtype=np.float32), np.sin(ang, dtype=np.float32)
    c = np.stack([cos, cos], 2).reshape(LAT, P)
    s = np.stack([-sin, sin], 2).reshape(LAT, P)
    return np.ascontiguousarray(np.stack([c, s], 1).reshape(LAT, 2 * P).astype(np.float32))


def edge_rows():
    rows = []
    for w in WINDOWS:
        a = w // 2
        left = [w / (t + a - max(t - a, 0)) for t in range(8)]
        right = [w / (min(t + a, 8) - (t - a)) for t in range(8)]
        rows.append(left + right)
    return np.asarray(rows, np.float32).reshape(-1)


def kernel(**inputs):
    import concourse.bacc as bacc
    from concourse.bass_utils import run_bass_kernel_spmd as run

    nc = bacc.Bacc("TRN2", target_bir_lowering=False, num_devices=1)
    x = {k: np.asarray(v) for k, v in inputs.items()}
    w_in = x["w_in"]
    arrays = {
        "x": x["x"].reshape(LAT, D),
        "ctx": x["ctx"].reshape(CTX, D),
        "c_cols": np.stack([x["c_ctx"], x["c"][0]]).reshape(2, KD, P).transpose(2, 0, 1).reshape(P, 2 * KD),
        "pool_scale": x["pool_scale"].reshape(DEPTH, POOL_GROUPS, P).transpose(2, 0, 1).reshape(P, DEPTH * POOL_GROUPS),
        "w_mod": chunked(x["w_mod"], 2 * P, 512),
        "w_qkv": chunked(w_in[:, :, :COL_ZA], 2 * P, 512),
        "w_gates": chunked(w_in[:, :, COL_ZA:], D, P)[:, :, 0],
        "w_pool": x["w_pool"].transpose(0, 2, 1, 3).reshape(DEPTH, P, POOL_GROUPS * P),
        "w_br_a": chunked(x["w_br_a"], D, P)[:, :, 0],
        "w_br_b": chunked(x["w_br_b"], D // 2, P)[:, :, 0],
        "w_out": x["w_out"],
        "rope": rope_rows(),
        "edge": edge_rows(),
    }
    for name in ("b_mod", "q_norm", "k_norm", "ln_g", "ln_b"):
        arrays[name] = x[name]
    arrays = {k: np.ascontiguousarray(v) for k, v in arrays.items()}
    t = {k: nc.dram_tensor(k + "_dram", v.shape, F32, kind="ExternalInput").ap() for k, v in arrays.items()}
    t["out"] = nc.dram_tensor("out_dram", (LAT, D), F32, kind="ExternalOutput").ap()
    build(nc, t)
    r = run(nc, [{k + "_dram": v for k, v in arrays.items()}], core_ids=[0])
    return r.results[0]["out_dram"].reshape(1, LAT, D)
```

```python
import numpy as np
from contextlib import ExitStack

import concourse.bass as bass
from concourse import mybir

F32 = mybir.dt.float32
F32R = mybir.dt.float32r
ALU = mybir.AluOpType
ACT = mybir.ActivationFunctionType
AX_X = mybir.AxisListType.X

P = 128
D = 1024
KD = D // P
DEPTH = 2
LAT, CTX = 512, 256
TOK = LAT + CTX
HEADS, KV_HEADS, GROUP = 8, 2, 4
POOL_GROUPS = 4
WINDOWS = (2, 4, 8, 16)
GRID_W = 64
EPS = 1e-6
ALPHA = float((2 * DEPTH) ** 0.25)
COL_ZA = 1536
PAD = 8

STREAMS = ((0, 0, 2, 2), (0, 2, 4, 6), (1, 2, 4, 6))
LAYER_STREAMS = ((0, 1), (2,))


def weight_chunks(w):
    out = []

    def modulation(l, cgs):
        for cg in cgs:
            for q in range(4):
                out.append(("mod", w["w_mod"][l, cg, q], 2, 512))

    modulation(0, (2, 3, 0, 1))
    modulation(1, range(4))
    for l in range(DEPTH):
        for cg in (2, 0, 1):
            for q in range(4):
                out.append(("qkv", w["w_qkv"][l, cg, q], 2, 512))
        if l == 0:
            modulation(0, (4, 5))
        for s in LAYER_STREAMS[l]:
            out.append(("pool", w["w_pool"][l], 4, P))
            for h in range(HEADS):
                out.append(("za", w["w_gates"][l, h], KD, P))
                out.append(("xz", w["w_gates"][l, (8, 12)[h % 2] + h // 2], KD, P))
            for kinds, j in [("gg", 0), ("gg", 1), ("yy", 0), ("yy", 1)] + [("ggyy", j) for j in range(2, KD)]:
                if "g" in kinds:
                    out.append(("ga", w["w_gates"][l, 16 + j], KD, P))
                    out.append(("gb", w["w_gates"][l, 24 + j], KD, P))
                if "y" in kinds:
                    out.append(("ya", w["w_br_a"][l, j], KD, P))
                    out.append(("yb", w["w_br_b"][l, j], 4, P))
            for k in range(KD):
                out.append(("out", w["w_out"][l, k * P:(k + 1) * P, :], 1, D))
            if s == 0:
                modulation(1, (4, 5))
    return out


EARLY_MOD = 32
FIRST_ROWS_CHUNKS = 16
Q_PLACES = 6
RAW, BORROWED = (0, 1, 2), (3, 4, 5, 6)


def build(nc, t):
    chunks = weight_chunks(t)
    raw_slot, raw_before, raw_turn, split_no, ring_before = [], [], [], [], []
    last_in_raw, last_in_ring, splits, ring_no = {}, {}, [], 0
    uses, outs, streams_begun, last_yb, last_borrowed = {}, 0, 0, None, None
    phase, phase_begin, merge_chunks = None, 0, 0
    for n, (kind, _, a, b) in enumerate(chunks):
        if kind == "pool":
            streams_begun += 1
        s_now = streams_begun - 1
        if n < FIRST_ROWS_CHUNKS:
            now, slots = "first modulation", RAW + BORROWED
        elif s_now == 0 and 4 <= merge_chunks < 4 * (KD - 2):
            now, slots = "context merge", RAW + BORROWED
        else:
            now, slots = "else", RAW
        merge_chunks += kind in ("ga", "gb", "ya", "yb")
        if now != phase:
            phase, phase_begin = now, n
        slot = min(slots, key=lambda i: (last_in_raw.get(i, -1) if i in RAW else
                                         max(last_in_raw.get(i, -1), phase_begin - 0.5)))
        raw_slot.append(slot)
        raw_before.append(last_in_raw.get(slot))
        last_in_raw[slot] = n
        uses[slot] = uses.get(slot, 0) + 1
        raw_turn.append(uses[slot])
        if slot in BORROWED:
            last_borrowed = n
        split_no.append(len(splits))
        outs = outs + 1 if kind == "out" else outs
        if kind != "out" and kind != "mod":
            outs = 0
        if kind == "mod" and n < EARLY_MOD:
            place = ("q", n % Q_PLACES)
        elif kind == "out" and s_now >= 1 and outs > 2:
            place = ("q", outs - 3)
        elif kind in ("pool", "yb"):
            place = "pool"
        else:
            place = ring_no % 2
            ring_no += 1
        ring_before.append(last_yb if kind == "out" and isinstance(place, tuple) else last_in_ring.get(place))
        last_in_ring[place] = n
        if kind == "yb":
            last_yb = n
        splits.append((n, place))
    of_kind = {}
    for n, (kind, *_r) in enumerate(chunks):
        of_kind.setdefault(kind, []).append(n)
    XZ_N, GA_N, OUT_N, QKV_N = of_kind["xz"], of_kind["ga"], of_kind["out"], of_kind["qkv"]
    for s in range(3):
        ring_before[of_kind["yb"][8 * s]] = GA_N[8 * s] + 1

    done_count, ring_chunks = [], 0
    for kind, *_r in chunks:
        ring_chunks += kind != "pool"
        done_count.append(ring_chunks)

    MOD_N = [of_kind["mod"][4 * i + 3] for i in range(12)]
    MOD_GROUPS = [(0, g) for g in (2, 3, 0, 1)] + [(1, g) for g in range(4)] + [(0, 4), (0, 5), (1, 4), (1, 5)]
    MOD_BANKS = (6, 7, 6, 7, 6, 7, 6, 7, 2, 3, 6, 7)

    POOL_LO = of_kind["mod"][21::2]
    lo_no = {}
    for n in range(len(chunks)):
        lo_no[n] = POOL_LO.index(n) if n in POOL_LO else n - sum(p < n for p in POOL_LO)

    def done(n):
        return done_count[n]

    def p2_no(l, g, tile):
        if l == 0:
            return 6 * g + tile
        return 18 + (tile if g == 0 else 6 + 4 * (g - 1) + tile - 2)

    def p2_tiles(l, g):
        return list(range(6)) if l == 0 or g == 0 else list(range(2, 6))

    STEP0 = (0, 16, 48)

    def step_no(s, h, i):
        return STEP0[s] + h * STREAMS[s][2] + i

    def head_no(s, h):
        return 8 * s + h

    TILE0 = (0, 2, 6)

    def out_no(s, tile):
        return TILE0[s] + tile

    def acc_count(l, g, tile):
        n = 0
        for ll in range(DEPTH):
            for gg in range(3):
                for tt in p2_tiles(ll, gg)[:-1]:
                    n += 1
                    if (ll, gg, tt) == (l, g, tile):
                        return n
        raise ValueError

    def bc_count(s):
        return 16 * 5 * (s + 1)

    def ssq_count(l, g, tile):
        n = 0
        for ll in range(DEPTH):
            for gg in range(3):
                for tt in p2_tiles(ll, gg):
                    n += 2 if gg == 0 else 4
                    if (ll, gg, tt) == (l, g, tile):
                        return n
        raise ValueError

    with ExitStack() as ctx:
        def sb(name, n, dt=F32):
            return ctx.enter_context(nc.sbuf_tensor(name, [P, n], dt))

        def sem(name):
            return ctx.enter_context(nc.semaphore(name))

        arena = sb("arena", 41984, F32R)
        work = sb("work", 7168)
        raw = sb("raw", 3072)
        ident = sb("ident", P)
        stat = sb("stat", 272)
        sc_pair = sb("sc_pair", 32, F32R)
        half = sb("half", 512)

        def view(off, a, b):
            return arena[:, off:off + a * b].rearrange("p (a b) -> p a b", a=a)

        def pair(off, a, b):
            return view(off, a, b), view(off + a * b, a, b)

        U = (pair(0, KD, CTX), pair(4096, KD, LAT))
        Q = (pair(12288, HEADS, CTX), pair(16384, HEADS, LAT))
        K = pair(24576, KV_HEADS, TOK)
        V = pair(27648, 6, KV_HEADS * P)
        SCR = 30720
        PT = (pair(SCR, 2, CTX), pair(SCR, 6, LAT), pair(SCR, 6, LAT))
        Y = (pair(SCR, KD, CTX), pair(24576, KD, LAT), pair(24576, KD, LAT))
        M = (pair(SCR + 4096, POOL_GROUPS, CTX), pair(12288, POOL_GROUPS, LAT), pair(12288, POOL_GROUPS, LAT))
        W = (36864, 38912)
        POOL_PLACE = 40960
        Q_PLACE = 12288
        WP = pair(POOL_PLACE, POOL_GROUPS, P)

        def u_tile(tile):
            if tile < 2:
                return tuple(x[:, :, tile * P:(tile + 1) * P] for x in U[0])
            return tuple(x[:, :, (tile - 2) * P:(tile - 1) * P] for x in U[1])

        def q_tile(tile, h0, n):
            if tile < 2:
                return tuple(x[:, h0:h0 + n, tile * P:(tile + 1) * P] for x in Q[0])
            return tuple(x[:, h0:h0 + n, (tile - 2) * P:(tile - 1) * P] for x in Q[1])

        def split_place(m):
            n, place = splits[m]
            size = chunks[n][2] * chunks[n][3]
            if place == "pool":
                off = POOL_PLACE
            elif isinstance(place, tuple):
                off = Q_PLACE + 2048 * place[1]
            else:
                off = W[place]
            step = 512 if place == "pool" else 1024
            return arena[:, off:off + size], arena[:, off + step:off + step + size]

        def ring(n):
            hi, lo = split_place(split_no[n])
            a = chunks[n][2]
            return hi.rearrange("p (a b) -> p a b", a=a), lo.rearrange("p (a b) -> p a b", a=a)

        def raw_of(n):
            size, slot = chunks[n][2] * chunks[n][3], raw_slot[n]
            if slot in BORROWED:
                off = 1024 * (slot - BORROWED[0])
                return work[:, off:off + size]
            return raw[:, slot * 1024:slot * 1024 + size]

        def wk(off, n):
            return work[:, off:off + n]

        RQ = stat[:, 0:48].rearrange("p (t h) -> p t h", t=6)
        RK = stat[:, 48:60].rearrange("p (t h) -> p t h", t=6)
        SSQ = stat[:, 64:88].rearrange("p (t h) -> p t h", t=6)
        RTMP = stat[:, 88:112].rearrange("p (t h) -> p t h", t=6)
        MHALF = stat[:, 112:116]
        NB = stat[:, 116:118]
        MX = stat[:, 118:120]
        RSUM = stat[:, 120:122]
        RINV = stat[:, 122:124]
        BN = stat[:, 124:136].rearrange("p (a b) -> p a b", a=2)
        MV = stat[:, 264:268].rearrange("p (a b) -> p a b", a=2)
        RSTD = stat[:, 268:270]
        NMR = stat[:, 270:272]
        SC = stat[:, 140:156].rearrange("p (v k) -> p v k", v=2)
        SC_HI, SC_LO = (sc_pair[:, 16 * i:16 * i + 16].rearrange("p (v k) -> p v k", v=2) for i in range(2))
        CRAW = stat[:, 156:172].rearrange("p (v k) -> p v k", v=2)
        CTH = stat[:, 172:188].rearrange("p (v k) -> p v k", v=2)
        PS = stat[:, 188:196].rearrange("p (l g) -> p l g", l=2)
        EDGE = stat[:, 196:260].rearrange("p (g e) -> p g e", g=4)
        VEPS = stat[:, 260:262]

        ps = ctx.enter_context(nc.psum_tensor("ps", [P, 8, 512], F32))

        MODROW = half[0:2, :]
        FIRST_ROWS = work[0:2, 5120:7168]
        BC = [wk(1024 * i, 1024) for i in range(5)]
        R = ((wk(5120, 1024), wk(6144, 1024)), (wk(5120, 1024), wk(6144, 1024)) * 2,
             (wk(1024, 1024), wk(2048, 1024), wk(5120, 1024), wk(6144, 1024)))
        N = [wk(3072, 1024), wk(4096, 1024)]
        TAB = wk(0, 2048).rearrange("p (t k f) -> p t k f", t=4, k=4)
        GN = wk(2048, 512).rearrange("p (k f) -> p k f", k=4)
        QRAW = wk(2560, 3072).rearrange("p (t f) -> p t f", t=6)
        CS = wk(2560, 1024).rearrange("p (t k f) -> p t k f", t=4, k=2)
        SQ = wk(6656, 512)
        T1, T2 = wk(5632, 512), wk(6144, 512)
        PR = [wk(768 * i, 768) for i in range(2)]
        THZ = wk(1536, 512)
        SZA = ([wk(2048 + 256 * i, 256) for i in range(4)],) + ([wk(2048, 512), wk(2560, 512)],) * 2
        XP, XA, XB = wk(3072, 528), wk(3600, 528), wk(4128, 528)
        PM = wk(4656, 512)
        THB = wk(5168, 512)
        SZB = wk(5680, 512)
        OG = wk(6192, 512)
        THA, THG, YA, YB = wk(5120, 512), wk(5632, 512), wk(6144, 512), wk(6656, 512)

        mod_rows = nc.dram_tensor("mod_rows", (DEPTH, 2, 3 * D), F32, kind="Internal").ap()
        xhat_mid = nc.dram_tensor("xhat_mid", (LAT, D), F32, kind="Internal").ap()

        landed = [sem(f"raw_landed{i}") for i in range(len(RAW + BORROWED))]
        w_hi, w_lo, w_lo_pool = sem("w_hi"), sem("w_lo"), sem("w_lo_pool")
        chunk_done = sem("chunk_done")
        c_in, consts = sem("c_in"), sem("consts")
        ident_ready = sem("ident_ready")
        silu_c = sem("silu_c")
        dve_own, pool_own = sem("dve_own"), sem("pool_own")
        rows_init, dram_init = sem("rows_init"), sem("dram_init")
        rows_spread, bc_copied = sem("rows_spread"), sem("bc_copied")
        mod_evac, mod_stored = sem("mod_evac"), sem("mod_stored")
        bc_in = sem("bc_in")
        x_in = [sem(f"x_in{i}") for i in range(3)]
        x_res = [sem(f"x_res{i}") for i in range(2)]
        u_made, u_turned, u_hi, u_lo = sem("u_made"), sem("u_turned"), sem("u_hi"), sem("u_lo")
        tab_in, tab_ready = sem("tab_in"), sem("tab_ready")
        acc_done = sem("acc_done")
        q_copied, ssq_done, rms_ready = sem("q_copied"), sem("ssq_done"), sem("rms_ready")
        v_split = sem("v_split")
        roped, q_turned, qk_hi, qk_lo = sem("roped"), sem("q_turned"), sem("qk_hi"), sem("qk_lo")
        s_done, nb_ready, exp_done, p_ready = sem("s_done"), sem("nb_ready"), sem("exp_done"), sem("p_ready")
        p_turned, pt_hi, pt_lo = sem("p_turned"), sem("pt_hi"), sem("pt_lo")
        pv_done, og_ready, o_hi, o_lo = sem("pv_done"), sem("og_ready"), sem("o_hi"), sem("o_lo")
        za_tanh, sza_ready = sem("za_tanh"), sem("sza_ready")
        xb_copied, pooled = sem("xb_copied"), sem("pooled")
        m_hi, m_lo, pool_mm = sem("m_hi"), sem("m_lo"), sem("pool_mm")
        zb_tanh, szb_ready = sem("zb_tanh"), sem("szb_ready")
        pg_ready, pg_hi, pg_lo = sem("pg_ready"), sem("pg_hi"), sem("pg_lo")
        ga_tanh, merged, y_hi, y_lo = sem("ga_tanh"), sem("merged"), sem("y_hi"), sem("y_lo")
        out_acc, xhat_ready, stored = sem("out_acc"), sem("xhat_ready"), sem("stored")
        r_affine, out_ready, out_stored = sem("r_affine"), sem("out_ready"), sem("out_stored")
        centred = sem("centred")
        var_ready, rstd_ready = sem("var_ready"), sem("rstd_ready")
        block = ctx.enter_context(nc.Block())

        def s_bank(s, a):
            cols = STREAMS[s][3] * P
            return ps[:, a % 2, 0:cols] if s == 0 else ps[:, 0:2, :].rearrange("p a b -> p (a b)")[:, 0:cols]

        def p_bank(s, a):
            nk = STREAMS[s][3]
            bank = 2 + a % 2
            v = ps[:, bank:bank + 1, :] if s == 0 else ps[:, 2:4, :]
            return v.rearrange("p a (b c) -> p (a b) c", c=P)[:, 0:nk]

        def wait_lo(eng, n):
            eng.wait_ge(w_lo_pool if n in POOL_LO else w_lo, lo_no[n] + 1)

        @block.sync
        def _(sp):
            sp.dma_start(CRAW.rearrange("p v k -> p (v k)"), t["c_cols"]).then_inc(c_in, 16)
            for n, (kind, src, a, b) in enumerate(chunks):
                if n == len(RAW):
                    sp.dma_start(FIRST_ROWS, t["b_mod"][0, 0:2 * D].partition_broadcast(2)).then_inc(rows_init, 16)
                if n >= FIRST_ROWS_CHUNKS and raw_slot[n] in BORROWED:
                    sp.wait_ge(o_lo, 8)
                    sp.wait_ge(pg_lo, 4)
                if raw_before[n] is not None:
                    wait_lo(sp, raw_before[n])
                sp.dma_start(raw_of(n), src).then_inc(landed[raw_slot[n]], 16)
            for tile in range(4):
                for hf in range(2):
                    cols = slice(hf * 512, (hf + 1) * 512)
                    sp.wait_ge(out_ready, 2 * tile + hf + 1)
                    sp.dma_start(t["out"][tile * P:(tile + 1) * P, cols], R[2][tile][:, cols]).then_inc(out_stored, 16)
            sp.wait_ge(out_stored, 16 * 8)

        def wait_landed(eng, n):
            eng.wait_ge(landed[raw_slot[n]], 16 * raw_turn[n])

        @block.scalar
        def _(act):
            own = [0]
            m = 0

            def split(m):
                if m >= len(splits):
                    return
                n = splits[m][0]
                wait_landed(act, n)
                if ring_before[n] is not None:
                    act.wait_ge(chunk_done, done(ring_before[n]))
                nc.scalar.activation(split_place(m)[0], raw_of(n), ACT.Copy).then_inc(w_hi, 1)

            act.wait_ge(c_in, 16)
            nc.scalar.activation(CTH, CRAW, ACT.Tanh, scale=0.5).then_inc(silu_c, 1)
            act.wait_ge(silu_c, 2)
            nc.scalar.activation(SC_HI, SC, ACT.Copy).then_inc(silu_c, 1)

            def turn_u(no, tile, bank):
                act.wait_ge(u_turned, no + 1)
                nc.scalar.activation(u_tile(tile)[0], ps[:, bank:bank + 2, :].rearrange("p a (b c) -> p (a b) c", c=P),
                                     ACT.Copy).then_inc(u_hi, 1)

            def spread_copy(no):
                act.wait_ge(rows_spread, no + 1)
                if no == 0:
                    act.wait_ge(w_lo, FIRST_ROWS_CHUNKS)
                bank = 2 * (no % 3)
                nc.scalar.activation(BC[2 * (no % 2) + no // 2], ps[:, bank:bank + 2, :].rearrange("p a b -> p (a b)"),
                                     ACT.Copy).then_inc(bc_copied, 1)

            for m in range(18):
                split(m)
            spread_copy(0)
            spread_copy(1)
            split(18)
            split(19)
            spread_copy(2)
            spread_copy(3)
            for m in range(20, 24):
                split(m)
            for tile in range(2):
                turn_u(tile, tile, 2 * (tile % 3))
                for m in range(24 + 4 * tile, 28 + 4 * tile):
                    split(m)
            for tile in range(2, 5):
                turn_u(tile, tile, 2 * (tile % 3))
            m = EARLY_MOD
            split(m)
            turn_u(5, 5, 4)
            for l in range(DEPTH):
                def copies(g):
                    for tile in p2_tiles(l, g):
                        no = p2_no(l, g, tile)
                        if tile == p2_tiles(l, g)[-1]:
                            act.wait_ge(chunk_done, done(QKV_N[12 * l + 4 * g + 3]))
                        else:
                            act.wait_ge(acc_done, acc_count(l, g, tile))
                        if g > 0:
                            act.wait_ge(q_turned, p2_no(l, g - 1, tile) + 1)
                        elif tile == 0:
                            act.wait_ge(tab_ready, 4 * (l + 1))
                        if g == 0:
                            nc.scalar.activation(QRAW[:, tile, 0:256], ps[:, tile, 0:256], ACT.Copy)
                            nc.scalar.activation(V[0][:, tile, :], ps[:, tile, 256:512], ACT.Copy).then_inc(q_copied, 1)
                        else:
                            nc.scalar.activation(QRAW[:, tile, :], ps[:, tile, :], ACT.Copy).then_inc(q_copied, 1)

                def squares(g, tiles):
                    n = 2 if g == 0 else 4
                    for tile in tiles:
                        no = p2_no(l, g, tile)
                        act.wait_ge(q_copied, no + 1)
                        if g or l:
                            act.wait_ge(rms_ready, (p2_no(l, g - 1, tile) if g else p2_no(l - 1, 2, tile)) + 1)
                        if own[0]:
                            act.wait_ge(ssq_done, own[0])
                        for h in range(n):
                            ins = nc.scalar.activation(SQ[:, h * P:(h + 1) * P], QRAW[:, tile, h * P:(h + 1) * P],
                                                       ACT.Square, accum_out=SSQ[:, tile, h:h + 1])
                            own[0] += 1
                            ins.then_inc(ssq_done, 1)

                def turned(g, tiles):
                    n = 2 if g == 0 else 4
                    for tile in tiles:
                        no = p2_no(l, g, tile)
                        act.wait_ge(q_turned, no + 1)
                        src = ps[:, 6 + no % 2, 0:n * P].rearrange("p (h c) -> p h c", h=n)
                        dst = K[0][:, :, tile * P:(tile + 1) * P] if g == 0 else q_tile(tile, 4 * (g - 1), 4)[0]
                        nc.scalar.activation(dst, src, ACT.Copy).then_inc(qk_hi, 1)

                for g in range(3):
                    for c in range(4):
                        split(m + 1)
                        m += 1
                        if (l, g, c) == (1, 2, 3):
                            split(m + 1)
                            m += 1
                        if g > 0:
                            tl = p2_tiles(l, g - 1)
                            if c < 3:
                                squares(g - 1, tl[2 * c:2 * c + 2])
                            if c > 0:
                                turned(g - 1, tl[2 * c - 2:2 * c])
                        if c == 3:
                            copies(g)
                tl = p2_tiles(l, 2)
                for k in range(len(tl) + 2):
                    squares(2, tl[k:k + 1])
                    if l == 0 or k == 0:
                        split(m + 1)
                        m += 1
                    if k >= 2:
                        turned(2, tl[k - 2:k - 1])

                for s in LAYER_STREAMS[l]:
                    _, t0, nt, nk = STREAMS[s]
                    T, lat = nt * P, s > 0
                    for _ in range(1 if l else 3):
                        split(m + 1)
                        m += 1

                    def probs_hi(h, i):
                        a = step_no(s, h, i)
                        act.wait_ge(p_turned, a + 1)
                        if h > 0 and i == 0:
                            act.wait_ge(pv_done, head_no(s, h))
                        src = p_bank(s, a)
                        nc.scalar.activation(PT[s][0][:, :, i * P:(i + 1) * P], src, ACT.Copy).then_inc(pt_hi, 1)

                    def gate_tanh(h):
                        act.wait_ge(chunk_done, done(XZ_N[8 * s + h] - 1))
                        if h > 0 or s > 0:
                            act.wait_ge(sza_ready, head_no(s, h))
                        nc.scalar.activation(THZ[:, 0:T], ps[:, 4, 0:T], ACT.Tanh, scale=0.5).then_inc(za_tanh, 1)

                    def pool_out(h):
                        g = h // 2
                        act.wait_ge(chunk_done, done(XZ_N[8 * s + h]))
                        no = 4 * s + g
                        if h % 2 == 0:
                            if no:
                                act.wait_ge(m_lo, no)
                            nc.scalar.activation(XP[:, PAD:PAD + T], ps[:, 5, 0:T], ACT.Copy).then_inc(xb_copied, 1)
                        else:
                            if no:
                                act.wait_ge(szb_ready, no)
                            nc.scalar.activation(THB[:, 0:T], ps[:, 5, 0:T], ACT.Tanh, scale=0.5).then_inc(zb_tanh, 1)

                    def pooled_hi(g):
                        no = 4 * s + g
                        act.wait_ge(pooled, no + 1)
                        nc.scalar.activation(M[s][0][:, g, :], PM[:, 0:T], ACT.Copy).then_inc(m_hi, 1)

                    def pool_gated_hi(g):
                        no = 4 * s + g
                        act.wait_ge(pg_ready, no + 1)
                        nc.scalar.activation(M[s][0][:, g, :], PM[:, 0:T], ACT.Copy).then_inc(pg_hi, 1)

                    def attn_out(h):
                        act.wait_ge(og_ready, head_no(s, h) + 1)
                        nc.scalar.activation(Q[min(s, 1)][0][:, h, :], OG[:, 0:T], ACT.Copy).then_inc(o_hi, 1)

                    act.wait_ge(rms_ready, p2_no(l, 2, 5) + 1)
                    gate_tanh(0)
                    prev = None
                    for h in range(HEADS):
                        c = h + 1
                        for i in range(nt):
                            a = step_no(s, h, i)
                            if i == 0 or i == nt // 2:
                                split(m + 1)
                                m += 1
                            act.wait_ge(nb_ready, a + 1)
                            if a >= 2:
                                act.wait_ge(p_turned, a - 1)
                            nc.scalar.activation(PR[a % 2][:, 0:nk * P],
                                                 s_bank(s, a), ACT.Exp,
                                                 bias=NB[:, a % 2:a % 2 + 1], scale=RQ[:, t0 + i, h:h + 1],
                                                 accum_out=RSUM[:, a % 2:a % 2 + 1]).then_inc(exp_done, 1)
                            if prev is not None:
                                probs_hi(*prev)
                            prev = (h, i)
                            if i == nt // 2 and c < HEADS:
                                gate_tanh(c)
                            if i == 0:
                                pool_out(h)
                            if lat and i == 2:
                                if c % 2:
                                    pooled_hi(c // 2)
                                else:
                                    pool_gated_hi(c // 2 - 1)
                            if not lat and i == 0 and c > 1:
                                (pool_gated_hi if c % 2 else pooled_hi)(c // 2 - 1)
                            if lat and i == 2 and h > 0:
                                attn_out(h - 1)
                            if not lat and i == 0 and h > 1:
                                attn_out(h - 2)
                    probs_hi(*prev)
                    split(m + 1)
                    if not lat:
                        pool_gated_hi(3)
                        attn_out(6)
                    attn_out(7)

                    split(m + 2)
                    m += 2
                    for j in range(KD):
                        if j == 1:
                            split(m + 1)
                            split(m + 2)
                            m += 2
                        for g in range(4):
                            if j > 1 or j == 0 and g >= 2:
                                split(m + 1)
                                m += 1
                            n = of_kind[("ga", "gb", "ya", "yb")[g]][8 * s + j]
                            if g < 2:
                                act.wait_ge(chunk_done, done(n))
                                if j or s:
                                    act.wait_ge(merged, 8 * s + j)
                                if j == 0 and g == 0:
                                    act.wait_ge(pg_lo, 4 * s + 4)
                                    act.wait_ge(o_lo, 8 * s + 8)
                                nc.scalar.activation((THA, THG)[g][:, 0:T], ps[:, 4 * ((j + 1) % 2) + g, 0:T],
                                                     ACT.Tanh, scale=0.5).then_inc(ga_tanh, 1)
                            if g == 2 and j > 0:
                                act.wait_ge(merged, 8 * s + j)
                                nc.scalar.activation(Y[s][0][:, j - 1, :], YA[:, 0:T], ACT.Copy).then_inc(y_hi, 1)
                    act.wait_ge(merged, 8 * s + 8)
                    nc.scalar.activation(Y[s][0][:, 7, :], YA[:, 0:T], ACT.Copy).then_inc(y_hi, 1)

                    for k in range(KD):
                        split(m + 1)
                        m += 1
                    def next_splits(count):
                        nonlocal m
                        for _ in range(count if s == 0 else 0):
                            split(m + 1)
                            m += 1

                    next_splits(5)
                    for tile in range(nt if s < 2 else 0):
                        no = out_no(s, tile)
                        if s == 1:
                            if tile:
                                turn_u(6 + no - 1, t0 + tile - 1, 2 * (tile - 1))
                            act.wait_ge(rstd_ready, no + 1)
                            act.wait_ge(centred, no + 1)
                            nc.scalar.activation(R[s][tile], R[s][tile], ACT.Identity, bias=NMR[:, no % 2:no % 2 + 1],
                                                 scale=RSTD[:, no % 2:no % 2 + 1]).then_inc(xhat_ready, 1)
                        else:
                            turn_u(6 + no, t0 + tile, 2 * tile)
                            next_splits(2 - tile)
                    if s == 1:
                        turn_u(6 + no, t0 + nt - 1, 2 * (nt - 1))

        @block.vector
        def _(dve):
            own = [0]

            def link(ins):
                own[0] += 1
                ins.then_inc(dve_own, 1)
                dve.wait_ge(dve_own, own[0])

            def split(m):
                if m >= len(splits):
                    return
                n = splits[m][0]
                if n in POOL_LO:
                    return
                hi, lo = split_place(m)
                dve.wait_ge(w_hi, m + 1)
                nc.vector.tensor_tensor(lo, raw_of(n), hi.bitcast(F32), ALU.subtract).then_inc(w_lo, 1)

            dve.wait_ge(silu_c, 1)
            link(nc.vector.scalar_tensor_tensor(out=CTH, in0=CTH, scalar=1.0, in1=CRAW, op0=ALU.add, op1=ALU.mult))
            nc.vector.tensor_scalar(SC, CTH, 0.5, None, ALU.mult).then_inc(silu_c, 1)
            dve.wait_ge(silu_c, 3)
            nc.vector.tensor_tensor(SC_LO, SC, SC_HI.bitcast(F32), ALU.subtract).then_inc(silu_c, 1)
            dve.wait_ge(consts, 16 * 2)
            link(nc.vector.tensor_scalar(PS, PS, 0.5, None, ALU.mult))

            def modulation(no):
                dve.wait_ge(chunk_done, done(MOD_N[no]))
                group, acc = MOD_GROUPS[no][1], ps[0:2, MOD_BANKS[no], :]
                if no < 4:
                    row = FIRST_ROWS[:, group * 512:(group + 1) * 512]
                    dve.wait_ge(rows_init, 16)
                    nc.vector.scalar_tensor_tensor(out=row, in0=acc, scalar=float(group >= 2), in1=row, op0=ALU.add,
                                                   op1=ALU.add).then_inc(mod_evac, 1)
                    return
                if no > 4:
                    dve.wait_ge(mod_stored, 16 * (no - 4))
                nc.vector.tensor_scalar(MODROW, acc, float(group in (2, 3)), None, ALU.add).then_inc(mod_evac, 1)

            def turn_u(no, tile, bank):
                dve.wait_ge(u_hi, no + 1)
                hi, lo = u_tile(tile)
                nc.vector.tensor_tensor(lo, ps[:, bank:bank + 2, :].rearrange("p a (b c) -> p (a b) c", c=P),
                                        hi.bitcast(F32), ALU.subtract).then_inc(u_lo, 1)

            def first_u(tile):
                s = 0 if tile < 2 else 1
                x_t = wk(4096 + 1024 * (tile % 3), 1024)
                dve.wait_ge(bc_copied, 4 if s else 3)
                dve.wait_ge(x_in[tile % 3], 16 * (tile // 3 + 1))
                link(nc.vector.tensor_tensor(x_t, x_t, BC[2 * s], ALU.mult))
                nc.vector.tensor_tensor(x_t, x_t, BC[2 * s + 1], ALU.add).then_inc(u_made, 1)

            def first_lo(tile):
                turn_u(tile, tile, 2 * (tile % 3))

            def splits_of(group):
                for i in range(4 * group, 4 * group + 4):
                    split(i)

            splits_of(0)
            for no in range(3):
                splits_of(no + 1)
                modulation(no)
            split(16)
            split(17)
            modulation(3)
            split(18)
            split(19)
            first_u(0)
            split(20)
            first_u(1)
            split(22)
            modulation(4)
            first_lo(0)
            first_u(2)
            split(24)
            first_lo(1)
            first_u(3)
            split(26)
            first_u(4)
            modulation(5)
            splits_of(7)
            first_lo(2)
            first_u(5)
            modulation(6)
            first_lo(3)
            first_lo(4)
            m = EARLY_MOD
            split(m)
            modulation(7)
            first_lo(5)
            for l in range(DEPTH):
                def v_lo(tile):
                    dve.wait_ge(q_copied, p2_no(l, 0, tile) + 1)
                    nc.vector.tensor_tensor(V[1][:, tile, :], ps[:, tile, 256:512], V[0][:, tile, :].bitcast(F32),
                                            ALU.subtract).then_inc(v_split, 1)

                def rope(g, tiles):
                    n = 2 if g == 0 else 4
                    for tile in tiles:
                        no = p2_no(l, g, tile)
                        dve.wait_ge(q_copied, no + 1)
                        dve.wait_ge(tab_ready, 4 * (l + 1))
                        x = QRAW[:, tile, 0:n * P]
                        ki = 2 if g == 0 else 0
                        heads_ = x.rearrange("p (h f) -> p h f", h=n)
                        dve.wait_ge(ssq_done, ssq_count(l, g, tile))
                        if tile < 2:
                            out = heads_
                            last = nc.vector.tensor_tensor(out, heads_, GN[:, ki:ki + 1, :].to_broadcast([P, n, P]),
                                                           ALU.mult)
                        else:
                            a, b = T1[:, 0:n * P], T2[:, 0:n * P]
                            dve.wait_ge(roped, no)
                            ca = TAB[:, tile - 2, ki:ki + 1, :].to_broadcast([P, n, P])
                            sn = TAB[:, tile - 2, ki + 1, :].rearrange("p (a z f) -> p a z f", z=2, f=32)
                            nc.vector.tensor_tensor(a.rearrange("p (h f) -> p h f", h=n), heads_, ca,
                                                    ALU.mult).then_inc(dve_own, 1)
                            for z in range(2):
                                nc.vector.tensor_tensor(
                                    b.rearrange("p (h a z f) -> p h a z f", a=2, z=2, f=32)[:, :, :, z, :],
                                    x.rearrange("p (h a z f) -> p h a z f", a=2, z=2, f=32)[:, :, :, 1 - z, :],
                                    sn[:, :, z, :].unsqueeze(1).to_broadcast([P, n, 2, 32]), ALU.mult).then_inc(dve_own, 1)
                            own[0] += 3
                            dve.wait_ge(dve_own, own[0])
                            last = nc.vector.tensor_tensor(x, a, b, ALU.add)
                        if g == 0:
                            link(last)
                            dve.wait_ge(rms_ready, no + 1)
                            last = nc.vector.tensor_tensor(
                                heads_, heads_, RK[:, tile, :].unsqueeze(2).to_broadcast([P, 2, P]), ALU.mult)
                        last.then_inc(roped, 1)

                def turned(g, tiles):
                    n = 2 if g == 0 else 4
                    for tile in tiles:
                        no = p2_no(l, g, tile)
                        dve.wait_ge(qk_hi, no + 1)
                        src = ps[:, 6 + no % 2, 0:n * P].rearrange("p (h c) -> p h c", h=n)
                        hi, lo = ((x[:, :, tile * P:(tile + 1) * P] for x in K) if g == 0
                                  else q_tile(tile, 4 * (g - 1), 4))
                        nc.vector.tensor_tensor(lo, src, hi.bitcast(F32), ALU.subtract).then_inc(qk_lo, 1)

                for g in range(3):
                    for c in range(4):
                        split(m + 1)
                        m += 1
                        if (l, g, c) == (1, 2, 3):
                            split(m + 1)
                            m += 1
                        if g == 0 and c == 2:
                            dve.wait_ge(tab_in, 16 * 7 * (l + 1))
                            for k in range(4):
                                nc.vector.tensor_tensor(TAB[:, :, k, :], CS[:, :, k % 2, :],
                                                        GN[:, k:k + 1, :].to_broadcast([P, 4, P]),
                                                        ALU.mult).then_inc(tab_ready, 1)
                        if g > 0:
                            tl = p2_tiles(l, g - 1)
                            if c < 3:
                                rope(g - 1, tl[2 * c:2 * c + 2])
                            if c > 0:
                                turned(g - 1, tl[2 * c - 2:2 * c])
                        if c == 3 and g == 0:
                            for tile in range(6):
                                v_lo(tile)
                tl = p2_tiles(l, 2)
                for k in range(len(tl) + 2):
                    rope(2, tl[k:k + 1])
                    if l == 0 or k == 0:
                        split(m + 1)
                        m += 1
                    if k >= 2:
                        turned(2, tl[k - 2:k - 1])
                    if l == 0 and k == 4:
                        modulation(8)

                for s in LAYER_STREAMS[l]:
                    _, t0, nt, nk = STREAMS[s]
                    T, lat = nt * P, s > 0
                    for _ in range(1 if l else 3):
                        split(m + 1)
                        m += 1
                    dve.wait_ge(rms_ready, p2_no(l, 2, 5) + 1)
                    def softmax_max(h, i):
                        a = step_no(s, h, i)
                        dve.wait_ge(s_done, a + 1)
                        link(nc.vector.reduce_max(MX[:, a % 2:a % 2 + 1],
                                                  s_bank(s, a), AX_X))
                        nc.vector.tensor_scalar(NB[:, a % 2:a % 2 + 1], MX[:, a % 2:a % 2 + 1],
                                                RQ[:, t0 + i, h:h + 1], -1.0, ALU.mult, ALU.mult).then_inc(nb_ready, 1)

                    def softmax_norm(h, i):
                        a = step_no(s, h, i)
                        dve.wait_ge(exp_done, a + 1)
                        link(nc.vector.reciprocal(RINV[:, a % 2:a % 2 + 1], RSUM[:, a % 2:a % 2 + 1]))
                        nc.vector.tensor_scalar(PR[a % 2][:, 0:nk * P], PR[a % 2][:, 0:nk * P],
                                                RINV[:, a % 2:a % 2 + 1], 0.5, ALU.mult, ALU.mult).then_inc(p_ready, 1)

                    def probs_lo(h, i):
                        a = step_no(s, h, i)
                        dve.wait_ge(pt_hi, a + 1)
                        src = p_bank(s, a)
                        hi, lo = (x[:, :, i * P:(i + 1) * P] for x in PT[s])
                        nc.vector.tensor_tensor(lo, src, hi.bitcast(F32), ALU.subtract).then_inc(pt_lo, 1)

                    def gate_silu(h):
                        b = head_no(s, h)
                        dve.wait_ge(za_tanh, b + 1)
                        if b >= len(SZA[s]):
                            dve.wait_ge(og_ready, b - len(SZA[s]) + 1)
                        nc.vector.scalar_tensor_tensor(out=SZA[s][b % len(SZA[s])][:, 0:T], in0=THZ[:, 0:T], scalar=1.0,
                                                       in1=ps[:, 4, 0:T], op0=ALU.add, op1=ALU.mult).then_inc(sza_ready, 1)

                    def attn_out(h):
                        b = head_no(s, h)
                        dve.wait_ge(pv_done, b + 1)
                        dve.wait_ge(sza_ready, b + 1)
                        if b:
                            dve.wait_ge(o_lo, b)
                        nc.vector.tensor_tensor(OG[:, 0:T], ps[:, 6, 0:T], SZA[s][b % len(SZA[s])][:, 0:T],
                                                ALU.mult).then_inc(og_ready, 1)

                    def attn_out_lo(h):
                        b = head_no(s, h)
                        hi, lo = (x[:, h, :] for x in Q[min(s, 1)])
                        dve.wait_ge(o_hi, b + 1)
                        dve.wait_ge(og_ready, b + 1)
                        nc.vector.tensor_tensor(lo, OG[:, 0:T], hi.bitcast(F32), ALU.subtract).then_inc(o_lo, 1)

                    def pooled_lo(g):
                        no = 4 * s + g
                        dve.wait_ge(m_hi, no + 1)
                        dve.wait_ge(pooled, no + 1)
                        nc.vector.tensor_tensor(M[s][1][:, g, :], PM[:, 0:T], M[s][0][:, g, :].bitcast(F32),
                                                ALU.subtract).then_inc(m_lo, 1)

                    def pool_silu(g):
                        no = 4 * s + g
                        dve.wait_ge(zb_tanh, no + 1)
                        if no:
                            dve.wait_ge(pg_ready, no)
                        nc.vector.scalar_tensor_tensor(out=SZB[:, 0:T], in0=THB[:, 0:T], scalar=1.0,
                                                       in1=ps[:, 5, 0:T], op0=ALU.add, op1=ALU.mult).then_inc(szb_ready, 1)

                    def pool_gated(g):
                        no = 4 * s + g
                        dve.wait_ge(pool_mm, no + 1)
                        dve.wait_ge(szb_ready, no + 1)
                        nc.vector.scalar_tensor_tensor(out=PM[:, 0:T], in0=ps[:, 7, 0:T], scalar=PS[:, l, g:g + 1],
                                                       in1=SZB[:, 0:T], op0=ALU.mult, op1=ALU.mult).then_inc(pg_ready, 1)

                    def pool_gated_lo(g):
                        no = 4 * s + g
                        dve.wait_ge(pg_hi, no + 1)
                        dve.wait_ge(pg_ready, no + 1)
                        nc.vector.tensor_tensor(M[s][1][:, g, :], PM[:, 0:T], M[s][0][:, g, :].bitcast(F32),
                                                ALU.subtract).then_inc(pg_lo, 1)

                    gate_silu(0)
                    prev = None
                    for h in range(HEADS):
                        c = h + 1
                        for i in range(nt):
                            softmax_max(h, i)
                            if i == 0 or i == nt // 2:
                                split(m + 1)
                                m += 1
                            if lat and i == 1 and c % 2 == 0:
                                pool_gated(c // 2 - 1)
                            if lat and i == 3:
                                if c < HEADS:
                                    gate_silu(c)
                                if h > 0:
                                    attn_out_lo(h - 1)
                            softmax_norm(h, i)
                            if s < 2 and (h, i) == (0, 0):
                                modulation((9, 11)[s])
                            if prev is not None:
                                probs_lo(*prev)
                            prev = (h, i)
                            if i == 0:
                                if c % 2 == 0:
                                    pool_silu(c // 2 - 1)
                                    if not lat:
                                        pooled_lo(c // 2 - 1)
                                elif c > 1:
                                    if lat:
                                        pool_gated_lo(c // 2 - 1)
                                    else:
                                        pool_gated(c // 2 - 1)
                            if not lat and i == 1 and c > 1 and c % 2:
                                pool_gated_lo(c // 2 - 1)
                            if lat and i == nt - 1 and c % 2 == 1:
                                pooled_lo(c // 2)
                            if lat and i == 2 and h > 0:
                                attn_out(h - 1)
                            if not lat and i == 0 and h > 1:
                                attn_out(h - 2)
                            if not lat and i == 1 and c < HEADS:
                                gate_silu(c)
                            if not lat and i == 1 and h > 1:
                                attn_out_lo(h - 2)
                    probs_lo(*prev)
                    split(m + 1)
                    if not lat:
                        pool_gated(3)
                    pool_gated_lo(3)
                    for h in (6, 7) if not lat else (7,):
                        attn_out(h)
                        attn_out_lo(h)

                    split(m + 2)
                    m += 2
                    for j in range(KD):
                        if j == 1:
                            split(m + 1)
                            split(m + 2)
                            m += 2
                        for g in range(4):
                            if j > 1 or j == 0 and g >= 2:
                                split(m + 1)
                                m += 1
                            n = of_kind[("ga", "gb", "ya", "yb")[g]][8 * s + j]
                            no = 8 * s + j
                            if g == 2 and j > 0:
                                dve.wait_ge(y_hi, no)
                                nc.vector.tensor_tensor(Y[s][1][:, j - 1, :], YA[:, 0:T],
                                                        Y[s][0][:, j - 1, :].bitcast(F32), ALU.subtract).then_inc(y_lo, 1)
                        dve.wait_ge(chunk_done, done(n))
                        dve.wait_ge(ga_tanh, 2 * no + 2)
                        if no:
                            dve.wait_ge(y_lo, no)
                        b0 = 4 * ((j + 1) % 2)
                        link(nc.vector.scalar_tensor_tensor(out=YA[:, 0:T], in0=THA[:, 0:T], scalar=1.0,
                                                            in1=ps[:, b0 + 2, 0:T], op0=ALU.add, op1=ALU.mult))
                        link(nc.vector.scalar_tensor_tensor(out=YB[:, 0:T], in0=THG[:, 0:T], scalar=1.0,
                                                            in1=ps[:, b0 + 3, 0:T], op0=ALU.add, op1=ALU.mult))
                        nc.vector.tensor_tensor(YA[:, 0:T], YA[:, 0:T], YB[:, 0:T], ALU.add).then_inc(merged, 1)
                    dve.wait_ge(y_hi, 8 * s + 8)
                    nc.vector.tensor_tensor(Y[s][1][:, 7, :], YA[:, 0:T], Y[s][0][:, 7, :].bitcast(F32),
                                            ALU.subtract).then_inc(y_lo, 1)

                    for k in range(KD):
                        split(m + 1)
                        m += 1
                    last_layer = s == 2
                    dve.wait_ge(bc_in, bc_count(s) if s < 2 else bc_count(2) - 32)
                    if not last_layer:
                        link(nc.vector.tensor_tensor(BC[1], BC[1], N[0], ALU.mult))
                        link(nc.vector.tensor_tensor(BC[2], BC[2], N[0], ALU.mult))
                        link(nc.vector.tensor_tensor(BC[2], BC[2], N[1], ALU.add))

                    def residual(tile):
                        no = out_no(s, tile)
                        x = R[s][tile]
                        if s > 0:
                            dve.wait_ge(out_acc, 4 * (s - 1) + tile + 1)
                        else:
                            dve.wait_ge(chunk_done, done(OUT_N[8 * s + 7]))
                        if last_layer:
                            dve.wait_ge(r_affine, tile + 1)
                        else:
                            dve.wait_ge(x_res[no % 2], 16 * (no // 2 + 1))
                        for hf in range(2):
                            cols = slice(hf * 512, (hf + 1) * 512)
                            if s > 0 and tile == nt - 1 and hf == 1:
                                dve.wait_ge(chunk_done, done(OUT_N[8 * s + 7]))
                            link(nc.vector.scalar_tensor_tensor(out=half[:], in0=ps[:, 2 * tile + hf, :], scalar=0.5,
                                                                in1=BC[0][:, cols], op0=ALU.mult, op1=ALU.mult))
                            link(nc.vector.scalar_tensor_tensor(out=x[:, cols], in0=x[:, cols], scalar=ALPHA,
                                                                in1=half[:], op0=ALU.mult, op1=ALU.add))
                            link(nc.vector.bn_stats(BN[:, hf, :], x[:, cols]))
                        if no >= 2:
                            dve.wait_ge(rstd_ready, no - 1)
                        nc.vector.bn_aggr(MV[:, no % 2, :], BN.rearrange("p a b -> p (a b)")).then_inc(var_ready, 1)

                    def centre(out, tile, cols, g):
                        no = out_no(s, tile)
                        dve.wait_ge(var_ready, no + 1)
                        nc.vector.scalar_tensor_tensor(out=out, in0=R[s][tile][:, cols], scalar=MV[:, no % 2, 0:1],
                                                       in1=g[:, cols], op0=ALU.subtract, op1=ALU.mult).then_inc(centred, 1)

                    def scale_and_shift(out, tile, cols, b, centred_count):
                        no = out_no(s, tile)
                        dve.wait_ge(rstd_ready, no + 1)
                        dve.wait_ge(centred, centred_count)
                        return nc.vector.scalar_tensor_tensor(out=out, in0=out, scalar=RSTD[:, no % 2:no % 2 + 1],
                                                              in1=b[:, cols], op0=ALU.mult, op1=ALU.add)

                    def next_u(tile):
                        no = out_no(s, tile)
                        if tile >= 2:
                            dve.wait_ge(u_turned, 6 + no - 1)
                        centre(N[tile % 2], tile, slice(0, D), BC[1])
                        scale_and_shift(N[tile % 2], tile, slice(0, D), BC[2], no + 1).then_inc(u_made, 1)

                    def next_lo(tile):
                        turn_u(6 + out_no(s, tile), t0 + tile, 2 * tile)

                    def output(tile):
                        for hf in range(2):
                            cols = slice(hf * 512, (hf + 1) * 512)
                            x = R[s][tile][:, cols]
                            centre(x, tile, cols, BC[3])
                            scale_and_shift(x, tile, cols, BC[4], 6 + 2 * tile + hf + 1).then_inc(out_ready, 1)

                    if s == 0:
                        residual(0)
                        split(m + 2)
                        next_u(0)
                        residual(1)
                        split(m + 4)
                        modulation(10)
                        next_lo(0)
                        next_u(1)
                        split(m + 6)
                        next_lo(1)
                        split(m + 8)
                        m += 8
                    elif s == 1:
                        dve.wait_ge(mod_stored, 16 * 8)
                        for tile in range(nt):
                            residual(tile)
                            if tile:
                                next_lo(tile - 1)
                            next_u(tile)
                        next_lo(nt - 1)
                    else:
                        for tile in range(nt):
                            residual(tile)
                            if tile == 0:
                                dve.wait_ge(bc_in, bc_count(2))
                            output(tile)

        @block.gpsimd
        def _(pool):
            own = [0]

            def link(ins):
                own[0] += 1
                ins.then_inc(pool_own, 1)
                pool.wait_ge(pool_own, own[0])

            pool.dma_start(PS.rearrange("p l g -> p (l g)"), t["pool_scale"]).then_inc(consts, 16)
            pool.dma_start(EDGE.rearrange("p g e -> p (g e)"), t["edge"].partition_broadcast(P)).then_inc(consts, 16)
            link(nc.gpsimd.memset(ident[:], 0.0))
            nc.gpsimd.affine_select(out=ident[:], in_=ident[:], compare_op=ALU.not_equal, fill=1.0, base=0,
                                    pattern=[[-1, P]], channel_multiplier=1).then_inc(ident_ready, 1)
            link(nc.gpsimd.memset(MHALF, -0.5))
            for v in range(2):
                pool.dma_start(mod_rows[:, v, :], t["b_mod"]).then_inc(dram_init, 16)

            def row(l, s, part):
                return mod_rows[l, min(s, 1), part * D:(part + 1) * D].partition_broadcast(P)

            def x_rows(tile):
                return t["ctx"][tile * P:(tile + 1) * P, :] if tile < 2 else t["x"][(tile - 2) * P:(tile - 1) * P, :]

            def load_x(tile):
                if tile >= 3:
                    pool.wait_ge(u_turned, tile - 2)
                pool.dma_start(wk(4096 + 1024 * (tile % 3), 1024), x_rows(tile)).then_inc(x_in[tile % 3], 16)

            def store_rows(no):
                l, g = MOD_GROUPS[no]
                pool.wait_ge(mod_evac, no + 1)
                pool.dma_start(mod_rows[l, :, g * 512:(g + 1) * 512], MODROW, accum_op=ALU.add).then_inc(mod_stored, 16)

            pool_chunk = 0

            def split_mod(count):
                nonlocal pool_chunk
                for _ in range(count):
                    n = POOL_LO[pool_chunk]
                    hi, lo = split_place(split_no[n])
                    pool.wait_ge(w_hi, split_no[n] + 1)
                    nc.gpsimd.tensor_tensor(lo, raw_of(n), hi.bitcast(F32), ALU.subtract).then_inc(w_lo_pool, 1)
                    pool_chunk += 1

            load_x(0)
            pool.wait_ge(dram_init, 32)
            pool.wait_ge(rows_spread, 4)
            load_x(1)
            load_x(2)
            split_mod(2)
            load_x(3)
            load_x(4)
            store_rows(4)
            split_mod(2)
            load_x(5)
            store_rows(5)
            split_mod(2)
            store_rows(6)
            store_rows(7)

            for l in range(DEPTH):
                pool.wait_ge(u_lo, (6, 12)[l])
                pool.dma_start(CS.rearrange("p t k f -> p t (k f)"),
                               t["rope"].rearrange("(t p) f -> p t f", p=P)).then_inc(tab_in, 16)
                for k, g in enumerate((t["q_norm"], t["k_norm"])):
                    pool.dma_start(GN[:, 2 * k, :], g[l].partition_broadcast(P)).then_inc(tab_in, 16)
                    gh = g[l].rearrange("(a z f) -> a z f", z=2, f=32)
                    dst = GN[:, 2 * k + 1, :].rearrange("p (a z f) -> p a z f", z=2, f=32)
                    for z in range(2):
                        pool.dma_start(dst[:, :, z, :], gh[:, 1 - z, :].partition_broadcast(P)).then_inc(tab_in, 16)

                for g in range(3):
                    n = 2 if g == 0 else 4
                    for tile in p2_tiles(l, g):
                        no = p2_no(l, g, tile)
                        pool.wait_ge(ssq_done, ssq_count(l, g, tile))
                        v = RTMP[:, tile, 0:n]
                        link(nc.gpsimd.tensor_scalar(v, SSQ[:, tile, 0:n], 1.0 / P, EPS, ALU.mult, ALU.add))
                        if g == 0:
                            nc.gpsimd.tensor_tensor(RK[:, tile, :], v, MHALF[:, 0:n], ALU.pow).then_inc(rms_ready, 1)
                        else:
                            link(nc.gpsimd.tensor_tensor(v, v, MHALF[:, 0:n], ALU.pow))
                            nc.gpsimd.tensor_scalar(RQ[:, tile, 4 * (g - 1):4 * g], v, float(P) ** -0.5, 0.0,
                                                    ALU.mult, ALU.add).then_inc(rms_ready, 1)
                        if l == 0 and g == 2 and tile % 2 == 0:
                            split_mod(1)

                if l == 0:
                    split_mod(1)
                    store_rows(8)
                    store_rows(9)
                for s in LAYER_STREAMS[l]:
                    _, t0, nt, _ = STREAMS[s]
                    T, last_layer = nt * P, s == 2
                    pool.wait_ge(*((u_lo, 8) if s == 1 else (q_turned, p2_no(l, 2, 5) + 1)))
                    for buf in (XP[:, 0:PAD], XP[:, PAD + T:T + 2 * PAD], XA, XB):
                        link(nc.gpsimd.memset(buf, 0.0))
                    for g in range(POOL_GROUPS):
                        no = 4 * s + g
                        pool.wait_ge(xb_copied, no + 1)
                        sums, w = XP, 1
                        while w < WINDOWS[g]:
                            a, b = (1, 0) if w == 1 else (w // 2, w // 2)
                            wide = (XA, XB)[sums is XA]
                            link(nc.gpsimd.tensor_tensor(wide[:, a:T + 2 * PAD - b], sums[:, 0:T + 2 * PAD - a - b],
                                                         sums[:, a + b:T + 2 * PAD], ALU.add))
                            sums, w = wide, 2 * w
                        for e, t1 in enumerate((PAD, T)):
                            link(nc.gpsimd.tensor_tensor(sums[:, t1:t1 + 8], sums[:, t1:t1 + 8],
                                                         EDGE[:, g, 8 * e:8 * e + 8], ALU.mult))
                        link(nc.gpsimd.tensor_scalar(sums[:, PAD:PAD + T], sums[:, PAD:PAD + T], 1.0 / w, 0.0, ALU.mult,
                                                     ALU.add))
                        if no:
                            pool.wait_ge(pg_lo, no)
                        nc.gpsimd.tensor_tensor(PM[:, 0:T], sums[:, PAD:PAD + T], XP[:, PAD:PAD + T],
                                                ALU.subtract).then_inc(pooled, 1)
                    pool.wait_ge(o_lo, 8 * s + 8)
                    pool.wait_ge(pg_lo, 4 * s + 4)
                    pool.wait_ge(mod_stored, 16 * (8 if l else 6))
                    if s == 0:
                        wait_lo(pool, last_borrowed)
                    if last_layer:
                        rows = (row(l, s, 2), t["ln_g"][0].partition_broadcast(P), t["ln_b"][0].partition_broadcast(P))
                        for dst, src in zip((BC[0], BC[3], BC[4]), rows):
                            pool.dma_start(dst, src).then_inc(bc_in, 16)
                        for tile in range(nt):
                            no = out_no(s, tile)
                            if tile == 2:
                                pool.wait_ge(y_lo, 8 * s + 8)
                            pool.dma_start(R[s][tile], xhat_mid[tile * P:(tile + 1) * P, :]).then_inc(x_res[no % 2], 16)
                            pool.wait_ge(x_res[no % 2], 16 * (no // 2 + 1))
                            if tile == 0:
                                pool.wait_ge(bc_in, bc_count(s) - 32)
                            link(nc.gpsimd.tensor_tensor(R[s][tile], R[s][tile], BC[3], ALU.mult))
                            nc.gpsimd.tensor_tensor(R[s][tile], R[s][tile], BC[4], ALU.add).then_inc(r_affine, 1)
                            pool.wait_ge(r_affine, tile + 1)
                        for dst, src in zip((BC[3], BC[4]), (t["ln_g"][1], t["ln_b"][1])):
                            pool.dma_start(dst, src.partition_broadcast(P)).then_inc(bc_in, 16)
                    else:
                        rows = (row(l, s, 2), t["ln_g"][l].partition_broadcast(P), t["ln_b"][l].partition_broadcast(P),
                                row(l + 1, s, 1), row(l + 1, s, 0))
                        for dst, src in zip(BC, rows):
                            pool.dma_start(dst, src).then_inc(bc_in, 16)
                        pool.wait_ge(y_lo, 8 * s + 8)

                    def load_r(tile):
                        src = x_rows(t0 + tile)
                        pool.dma_start(R[s][tile], src).then_inc(x_res[tile % 2], 16)

                    if not last_layer:
                        load_r(0)
                        load_r(1)
                    if s == 0:
                        split_mod(1)
                    for tile in range(nt):
                        no = out_no(s, tile)
                        c = slice(no % 2, no % 2 + 1)
                        pool.wait_ge(var_ready, no + 1)
                        if last_layer and tile >= 2:
                            pool.wait_ge(out_ready, 2 * tile - 2)
                        elif no >= 2:
                            pool.wait_ge(u_made, 6 + no - 1)
                            if no >= 4:
                                pool.wait_ge(xhat_ready, no - 3)
                        link(nc.gpsimd.tensor_scalar(VEPS[:, c], MV[:, no % 2, 1:2], 1.0, EPS, ALU.mult, ALU.add))
                        link(nc.gpsimd.tensor_tensor(RSTD[:, c], VEPS[:, c], MHALF[:, 0:1], ALU.pow))
                        nc.gpsimd.tensor_scalar(NMR[:, c], MV[:, no % 2, 0:1], RSTD[:, c], -1.0, ALU.mult,
                                                ALU.mult).then_inc(rstd_ready, 1)
                        if s == 0:
                            split_mod((2, 1)[tile])
                            if tile == 1:
                                store_rows(10)
                                store_rows(11)
                        if s == 1:
                            pool.wait_ge(xhat_ready, no - 1)
                            pool.dma_start(xhat_mid[tile * P:(tile + 1) * P, :], R[s][tile]).then_inc(stored, 16)
                            if tile + 2 < nt:
                                pool.wait_ge(stored, 16 * (tile + 1))
                                load_r(tile + 2)
            pool.wait_ge(stored, 16 * 4)

        @block.tensor
        def _(pe):
            def product(out, st, mv, start, stop):
                nc.tensor.matmul(out, st[1], mv[0], start=start, stop=False)
                nc.tensor.matmul(out, st[0], mv[1], start=False, stop=False)
                return nc.tensor.matmul(out, st[0], mv[0], start=False, stop=stop)

            n = 0

            def modulation(no, qs=range(4)):
                nonlocal n
                if no >= 2 and qs[0] == 0:
                    pe.wait_ge(mod_evac, no - 1)
                for q in qs:
                    wait_lo(pe, n)
                    wh, wl = ring(n)
                    for kk in range(2):
                        k = 2 * q + kk
                        ins = product(ps[0:2, MOD_BANKS[no], :], (SC_HI[:, :, k], SC_LO[:, :, k]),
                                      (wh[:, kk, :], wl[:, kk, :]), k == 0, k == KD - 1)
                    ins.then_inc(chunk_done, 1)
                    n += 1

            def turn_u(no, src, bank):
                pe.wait_ge(u_made, no + 1)
                for k in range(KD):
                    ins = nc.tensor.transpose(ps[:, bank + k // 4, (k % 4) * P:(k % 4 + 1) * P],
                                              src[:, k * P:(k + 1) * P], ident[:])
                ins.then_inc(u_turned, 1)

            def first_turn(tile):
                if tile >= 3:
                    pe.wait_ge(u_lo, tile - 2)
                turn_u(tile, wk(4096 + 1024 * (tile % 3), 1024), 2 * (tile % 3))

            def spread(no):
                part, v = 1 - no // 2, no % 2
                pe.wait_ge(mod_evac, 2 + 2 * (no // 2))
                if no == 3:
                    pe.wait_ge(bc_copied, 1)
                for hf in range(2):
                    cols = slice(part * D + hf * 512, part * D + (hf + 1) * 512)
                    ins = nc.tensor.matmul(ps[:, 2 * (no % 3) + hf, :], ident[0:2, v:v + 1].to_broadcast([2, P]),
                                           FIRST_ROWS[:, cols], start=True, stop=True)
                ins.then_inc(rows_spread, 1)

            pe.wait_ge(silu_c, 4)
            for no in range(3):
                modulation(no)
            pe.wait_ge(ident_ready, 1)
            spread(0)
            spread(1)
            modulation(3)
            modulation(4, (0, 1))
            spread(2)
            spread(3)
            modulation(4, (2, 3))
            pe.wait_ge(bc_copied, 4)
            first_turn(0)
            first_turn(1)
            modulation(5)
            first_turn(2)
            modulation(6)
            first_turn(3)
            first_turn(4)
            modulation(7)
            first_turn(5)

            for l in range(DEPTH):
                if l == 0:
                    pe.wait_ge(u_lo, 6)
                    pe.wait_ge(mod_evac, 8)

                def turn_q(g, tiles):
                    nh = 2 if g == 0 else 4
                    for tile in tiles:
                        no = p2_no(l, g, tile)
                        pe.wait_ge(roped, no + 1)
                        if no >= 2:
                            pe.wait_ge(qk_lo, no - 1)
                        for h in range(nh):
                            ins = nc.tensor.transpose(ps[:, 6 + no % 2, h * P:(h + 1) * P],
                                                      QRAW[:, tile, h * P:(h + 1) * P], ident[:])
                        ins.then_inc(q_turned, 1)

                for g in range(3):
                    tl = p2_tiles(l, g)
                    for c in range(4):
                        if g > 0 and c > 0:
                            turn_q(g - 1, p2_tiles(l, g - 1)[2 * c - 2:2 * c])
                        wait_lo(pe, n)
                        wh, wl = ring(n)
                        for tile in tl:
                            if c == 0 and g == 0 and l == 1:
                                if tile == 5:
                                    turn_u(11, N[1], 6)
                                pe.wait_ge(u_lo, 9 + max(tile // 2, tile - 2))
                            if c == 0 and g > 0:
                                pe.wait_ge(q_copied, p2_no(l, g - 1, tile) + 1)
                                if g == 1:
                                    pe.wait_ge(v_split, 6 * l + tile + 1)
                            for kk in range(2):
                                k = 2 * c + kk
                                uh, ul = u_tile(tile)
                                ins = product(ps[:, tile, :], (uh[:, k, :], ul[:, k, :]), (wh[:, kk, :], wl[:, kk, :]),
                                              k == 0, k == KD - 1)
                            if tile == tl[-1]:
                                ins.then_inc(chunk_done, 1)
                            elif c == 3:
                                ins.then_inc(acc_done, 1)
                        n += 1
                tl = p2_tiles(l, 2)
                if l == 0:
                    pe.wait_ge(q_copied, p2_no(l, 2, 3) + 1)
                    for tile in tl:
                        modulation(8 + tile // 4, (tile % 4,))
                        turn_q(2, [tile])
                    modulation(9, (2, 3))
                for s in LAYER_STREAMS[l]:
                    _, t0, nt, nk = STREAMS[s]
                    T, lat = nt * P, s > 0
                    si = min(s, 1)

                    def scores(h, i):
                        a = step_no(s, h, i)
                        if a > 1:
                            pe.wait_ge(exp_done, a - (s == 0))
                        qh, ql = (x[:, 0, :] for x in q_tile(t0 + i, h, 1))
                        kh, kl = (x[:, h // GROUP, :] for x in K)
                        for c0 in range(0, nk * P, 512):
                            c1 = min(c0 + 512, nk * P)
                            ins = product(s_bank(s, a)[:, c0:c1], (qh, ql), (kh[:, c0:c1], kl[:, c0:c1]), True, True)
                        ins.then_inc(s_done, 1)

                    def turn_p(h, i):
                        a = step_no(s, h, i)
                        pe.wait_ge(p_ready, a + 1)
                        if a < 2:
                            pe.wait_ge(mod_evac, 9 + a)
                        if a > 1:
                            pe.wait_ge(pt_lo, a - (s == 0))
                        for k in range(nk):
                            ins = nc.tensor.transpose(p_bank(s, a)[:, k, :],
                                                      PR[a % 2][:, k * P:(k + 1) * P], ident[:])
                        ins.then_inc(p_turned, 1)

                    def values(h):
                        b = head_no(s, h)
                        if b:
                            pe.wait_ge(og_ready, b)
                        pe.wait_ge(pt_lo, step_no(s, h, nt - 1) + 1)
                        c0 = (h // GROUP) * P
                        for k in range(nk):
                            ins = product(ps[:, 6, 0:T], (V[0][:, k, c0:c0 + P], V[1][:, k, c0:c0 + P]),
                                          (PT[s][0][:, k, :], PT[s][1][:, k, :]), k == 0, k == nk - 1)
                        ins.then_inc(pv_done, 1)

                    def project(bank, n, ks, start, stop):
                        wh, wl = ring(n)
                        for k in ks:
                            ins = product(ps[:, bank, 0:T], (wh[:, k, :], wl[:, k, :]),
                                          (U[si][0][:, k, :], U[si][1][:, k, :]), start and k == ks[0], stop and k == ks[-1])
                        return ins

                    def pool_product(g):
                        no = 4 * s + g
                        pe.wait_ge(m_lo, no + 1)
                        if no:
                            pe.wait_ge(pg_ready, no)
                        product(ps[:, 7, 0:T], (WP[0][:, g, :], WP[1][:, g, :]), (M[s][0][:, g, :], M[s][1][:, g, :]),
                                True, True).then_inc(pool_mm, 1)

                    half = nt // 2
                    ks_of = [list(range(KD))] if half == 1 else [[0, 1, 2, 3], [4, 5, 6, 7]]

                    def project_gate(n, part):
                        if part % half == 0:
                            wait_lo(pe, n)
                        ins = project(4 + part // half, n, ks_of[part % half], part % half == 0, part % half == half - 1)
                        if part % half == half - 1:
                            ins.then_inc(chunk_done, 1)

                    if s == 1:
                        pe.wait_ge(u_lo, 7)
                        scores(0, 0)
                        turn_u(7, N[1], 2)
                        modulation(11, (2, 3))
                    n += 1
                    if l == 0:
                        for part in range(nt):
                            project_gate(n + part // half, part)
                    else:
                        pe.wait_ge(q_copied, p2_no(l, 2, 5) + 1)
                        for part, tile in enumerate(tl):
                            if part < 3:
                                project_gate(n + part // half, part)
                            turn_q(2, [tile])
                        project_gate(n + 1, 3)
                    n += 2
                    if s == 1:
                        pe.wait_ge(u_lo, 8)
                    wait_lo(pe, n - 3)
                    pe.wait_ge(qk_lo, p2_no(l, 2, 5) + 1)
                    prev = None
                    for h in range(HEADS):
                        c = h + 1
                        for i in range(nt):
                            if (s, h, i) != (1, 0, 0):
                                scores(h, i)
                            if prev is not None:
                                turn_p(*prev)
                            prev = (h, i)
                            if i == 1 and h > 0:
                                values(h - 1)
                            if not lat and i == 1 and c % 2 == 0:
                                pool_product(c // 2 - 1)
                            if i % half == 0:
                                b = head_no(s, c)
                                if i == 0:
                                    pe.wait_ge(sza_ready, b)
                                elif c % 2:
                                    pe.wait_ge(xb_copied, 4 * s + c // 2 + 1)
                                else:
                                    pe.wait_ge(szb_ready, 4 * s + c // 2)
                            project_gate(n, i)
                            if i % half == half - 1:
                                n += 1
                            if (s, h, i) == (1, 1, 0):
                                pe.wait_ge(mod_evac, 12)
                            if lat and i == 0 and c % 2 == 0:
                                pool_product(c // 2 - 1)
                    turn_p(*prev)
                    pe.wait_ge(exp_done, step_no(s, 7, nt - 1) + 1)
                    wait_lo(pe, n)
                    project(0, n, list(range(KD)), True, True).then_inc(chunk_done, 1)
                    values(7)
                    wait_lo(pe, n + 1)
                    project(1, n + 1, list(range(KD)), True, True).then_inc(chunk_done, 1)
                    n += 2

                    for j in range(KD):
                        no = 8 * s + j
                        for g in range(4):
                            if j < 2 and g < 2:
                                continue
                            bank = 4 * ((j + 1) % 2) + g
                            wait_lo(pe, n)
                            if g == 0:
                                pe.wait_ge(merged, no - 1)
                            if g == 2 and j == 1:
                                pe.wait_ge(pt_lo, step_no(s, 7, nt - 1) + 1)
                            if g == 2 and j == 0:
                                pe.wait_ge(og_ready, 8 * s + 8)
                                pe.wait_ge(o_lo, 8 * s + 8)
                            if g == 3 and j == 0:
                                pe.wait_ge(pg_ready, 4 * s + 4)
                                pe.wait_ge(pg_lo, 4 * s + 4)
                            if g < 2:
                                ins = project(bank, n, list(range(KD)), True, True)
                            else:
                                op = Q[si] if g == 2 else M[s]
                                nkk = KD if g == 2 else POOL_GROUPS
                                wh, wl = ring(n)
                                for k in range(nkk):
                                    ins = product(ps[:, bank, 0:T], (wh[:, k, :], wl[:, k, :]),
                                                  (op[0][:, k, :], op[1][:, k, :]), k == 0, k == nkk - 1)
                            ins.then_inc(chunk_done, 1)
                            n += 1

                    def out_product(n, k, tile, hfs=(0, 1)):
                        wh, wl = ring(n)
                        for hf in hfs:
                            st = tuple(x[:, k, tile * P:(tile + 1) * P] for x in Y[s])
                            mv = tuple(x[:, 0, hf * 512:(hf + 1) * 512] for x in (wh, wl))
                            ins = product(ps[:, 2 * tile + hf, :], st, mv, k == 0, k == KD - 1)
                        return ins

                    streamed = KD if s == 0 else 2
                    for k in range(streamed):
                        wait_lo(pe, n)
                        pe.wait_ge(y_lo, 8 * s + k + 1)
                        if k == 0:
                            pe.wait_ge(merged, 8 * s + 8)
                        for tile in range(nt):
                            ins = out_product(n, k, tile)
                        ins.then_inc(chunk_done, 1)
                        n += 1
                    if s == 0:
                        modulation(10)
                        turn_u(6, N[0], 0)
                        modulation(11, (0, 1))
                    else:
                        for tile in range(nt):
                            last = tile == nt - 1
                            for hfs in ((0,), (1,)) if last else ((0, 1),):
                                for k in range(streamed, KD):
                                    if tile == 0:
                                        wait_lo(pe, n + k - streamed)
                                        pe.wait_ge(y_lo, 8 * s + k + 1)
                                    ins = out_product(n + k - streamed, k, tile, hfs)
                                    if hfs == (1,):
                                        ins.then_inc(chunk_done, 1)
                                if hfs != (1,):
                                    ins.then_inc(out_acc, 1)
                            if s == 1 and tile:
                                turn_u(6 + out_no(s, tile - 1), N[(tile - 1) % 2], 2 * (tile - 1))
                        n += KD - streamed


def chunked(w, rows, cols):
    n, r, c = w.shape
    w = w.reshape(n, r // rows, rows // P, P, c // cols, cols).transpose(0, 4, 1, 3, 2, 5)
    return np.ascontiguousarray(w.reshape(n, c // cols, r // rows, P, rows // P * cols))


def rope_rows():
    tok = np.arange(LAT)
    pos = np.stack([tok // GRID_W, tok % GRID_W], 1).astype(np.float32)
    freq = (np.float32(1.0) / (np.float32(10000.0) ** (np.arange(32, dtype=np.float32) / np.float32(32)))).astype(np.float32)
    ang = pos[:, :, None] * freq
    cos, sin = np.cos(ang, dtype=np.float32), np.sin(ang, dtype=np.float32)
    c = np.stack([cos, cos], 2).reshape(LAT, P)
    s = np.stack([-sin, sin], 2).reshape(LAT, P)
    return np.ascontiguousarray(np.stack([c, s], 1).reshape(LAT, 2 * P).astype(np.float32))


def edge_rows():
    rows = []
    for w in WINDOWS:
        a = w // 2
        left = [w / (t + a - max(t - a, 0)) for t in range(8)]
        right = [w / (min(t + a, 8) - (t - a)) for t in range(8)]
        rows.append(left + right)
    return np.asarray(rows, np.float32).reshape(-1)


def kernel(**inputs):
    import concourse.bacc as bacc
    from concourse.bass_utils import run_bass_kernel_spmd as run

    nc = bacc.Bacc("TRN2", target_bir_lowering=False, num_devices=1)
    x = {k: np.asarray(v) for k, v in inputs.items()}
    w_in = x["w_in"]
    arrays = {
        "x": x["x"].reshape(LAT, D),
        "ctx": x["ctx"].reshape(CTX, D),
        "c_cols": np.stack([x["c_ctx"], x["c"][0]]).reshape(2, KD, P).transpose(2, 0, 1).reshape(P, 2 * KD),
        "pool_scale": x["pool_scale"].reshape(DEPTH, POOL_GROUPS, P).transpose(2, 0, 1).reshape(P, DEPTH * POOL_GROUPS),
        "w_mod": chunked(x["w_mod"], 2 * P, 512),
        "w_qkv": chunked(w_in[:, :, :COL_ZA], 2 * P, 512),
        "w_gates": chunked(w_in[:, :, COL_ZA:], D, P)[:, :, 0],
        "w_pool": x["w_pool"].transpose(0, 2, 1, 3).reshape(DEPTH, P, POOL_GROUPS * P),
        "w_br_a": chunked(x["w_br_a"], D, P)[:, :, 0],
        "w_br_b": chunked(x["w_br_b"], D // 2, P)[:, :, 0],
        "w_out": x["w_out"],
        "rope": rope_rows(),
        "edge": edge_rows(),
    }
    for name in ("b_mod", "q_norm", "k_norm", "ln_g", "ln_b"):
        arrays[name] = x[name]
    arrays = {k: np.ascontiguousarray(v) for k, v in arrays.items()}
    t = {k: nc.dram_tensor(k + "_dram", v.shape, F32, kind="ExternalInput").ap() for k, v in arrays.items()}
    t["out"] = nc.dram_tensor("out_dram", (LAT, D), F32, kind="ExternalOutput").ap()
    build(nc, t)
    r = run(nc, [{k + "_dram": v for k, v in arrays.items()}], core_ids=[0])
    return r.results[0]["out_dram"].reshape(1, LAT, D)
```
